# Optimizing a Trainium2 kernel written in Bass

```python
import math
import jax
import jax.numpy as jnp
from jax import lax
import numpy as np

D_MODEL = 1024
BATCH = 1
SEQ = 256
DEPTH = 2

HEAD_DIM = 64
ATTN_SCALE = HEAD_DIM ** -0.5
ROPE_THETA = 10000.0
Q_BLOCK = 128
NEG_INF = -1e30
NORM_EPS = 1e-6

A_HEADS = D_MODEL // (4 * HEAD_DIM)
A_KV_HEADS = max(1, A_HEADS // 2)
A_WINDOW = 128

B_HEADS = D_MODEL // (4 * HEAD_DIM)
B_KV_HEADS = 1
CMP_STRIDE = 16
CMP_LEN = 2 * CMP_STRIDE
CMP_HIDDEN = 4 * HEAD_DIM
SLC_LEN = 64
SLC_TOPK = 16
NSA_WINDOW = 512
SLC_FORCED_SCORE = 1e9

C_HEAD_DIM = 128
C_HEADS = D_MODEL // (2 * C_HEAD_DIM)
CONV_WIDTH = 4
GDN_CHUNK = 64

D_FF_RAW = -(-8 * D_MODEL // 3)
D_FF = -(-D_FF_RAW // 256) * 256

A_Q = A_HEADS * HEAD_DIM
A_KV = A_KV_HEADS * HEAD_DIM
B_Q = B_HEADS * HEAD_DIM
B_KV = B_KV_HEADS * HEAD_DIM
B_GATES = 3 * B_HEADS
C_QK = C_HEADS * C_HEAD_DIM
MIX_WIDTH = A_Q + B_Q + C_QK
IN_SPLITS = (A_Q, A_KV, A_KV, B_Q, B_KV, B_KV, B_KV, B_KV, B_KV, B_KV, B_GATES, 3 * C_QK, C_QK, C_HEADS, C_HEADS)
IN_WIDTH = sum(IN_SPLITS)


def rms_norm(x, gain):
    xf = x.astype(jnp.float32)
    y = xf * lax.rsqrt(jnp.mean(xf * xf, axis=-1, keepdims=True) + NORM_EPS)
    return (y * gain.astype(jnp.float32)).astype(x.dtype)

def l2norm(x):
    return x * lax.rsqrt(jnp.sum(x * x, axis=-1, keepdims=True) + NORM_EPS)

def rope_tables(seq, dim):
    inv = 1.0 / (ROPE_THETA ** (jnp.arange(0, dim, 2, dtype=jnp.float32) / dim))
    ang = jnp.arange(seq, dtype=jnp.float32)[:, None] * inv[None, :]
    return jnp.cos(ang), jnp.sin(ang)

def apply_rope(x, cos, sin):
    x1, x2 = jnp.split(x.astype(jnp.float32), 2, axis=-1)
    c = cos[None, :, None, :]
    s = sin[None, :, None, :]
    return jnp.concatenate([x1 * c - x2 * s, x2 * c + x1 * s], axis=-1).astype(x.dtype)

def banded_attention(q, k, v, window, sink=None):
    B, S, H, d = q.shape
    Hkv = k.shape[2]
    G = H // Hkv
    nb = S // Q_BLOCK
    n_prev = window // Q_BLOCK
    span = (n_prev + 1) * Q_BLOCK
    pad = ((0, 0), (window, 0), (0, 0), (0, 0))
    kb = jnp.pad(k, pad).reshape(B, nb + n_prev, Q_BLOCK, Hkv, d)
    vb = jnp.pad(v, pad).reshape(B, nb + n_prev, Q_BLOCK, Hkv, d)
    k_ctx = jnp.concatenate([kb[:, j:j + nb] for j in range(n_prev + 1)], axis=2)
    v_ctx = jnp.concatenate([vb[:, j:j + nb] for j in range(n_prev + 1)], axis=2)
    qb = q.reshape(B, nb, Q_BLOCK, Hkv, G, d)
    s = jnp.einsum('bnqhgd,bnkhd->bnhgqk', qb, k_ctx, preferred_element_type=jnp.float32) * ATTN_SCALE
    q_rel = jnp.arange(Q_BLOCK)[:, None]
    k_rel = jnp.arange(span)[None, :] - window
    band = (k_rel <= q_rel) & (k_rel > q_rel - window)
    in_seq = (jnp.arange(nb)[:, None] * Q_BLOCK + k_rel) >= 0
    mask = band[None, :, :] & in_seq[:, None, :]
    s = jnp.where(mask[None, :, None, None], s, NEG_INF)
    if sink is None:
        p = jax.nn.softmax(s, axis=-1)
    else:
        sink_col = jnp.broadcast_to(sink.astype(jnp.float32).reshape(1, 1, Hkv, G, 1, 1), s.shape[:-1] + (1,))
        p = jax.nn.softmax(jnp.concatenate([s, sink_col], axis=-1), axis=-1)[..., :-1]
    o = jnp.einsum('bnhgqk,bnkhd->bnqhgd', p.astype(v.dtype), v_ctx)
    return o.reshape(B, S, H, d)

def compress_tokens(x, w1, w2, pe):
    B, S, Hkv, d = x.shape
    strides = x.reshape(B, S // CMP_STRIDE, CMP_STRIDE, Hkv, d)
    win = jnp.concatenate([strides[:, :-1], strides[:, 1:]], axis=2) + pe[:, None, :]
    flat = win.transpose(0, 1, 3, 2, 4).reshape(B, S // CMP_STRIDE - 1, Hkv, CMP_LEN * d)
    return jax.nn.silu(flat @ w1) @ w2

def nsa_mixer(q, k_cmp_in, v_cmp_in, k_slc, v_slc, k_win, v_win, gate_logits, cos, sin,
              cmp_k_w1, cmp_k_w2, cmp_v_w1, cmp_v_w2, cmp_pe_k, cmp_pe_v):
    B, S, H, d = q.shape
    Hkv = k_slc.shape[2]
    G = H // Hkv
    n_cmp = S // CMP_STRIDE - 1
    n_slc = S // SLC_LEN
    nb = S // Q_BLOCK
    ratio = SLC_LEN // CMP_STRIDE
    top_k = min(SLC_TOPK, n_slc)

    k_cmp = compress_tokens(k_cmp_in, cmp_k_w1, cmp_k_w2, cmp_pe_k)
    v_cmp = compress_tokens(v_cmp_in, cmp_v_w1, cmp_v_w2, cmp_pe_v)
    q_rot = apply_rope(q, cos, sin)
    ks_blocks = apply_rope(k_slc, cos, sin).reshape(B, n_slc, SLC_LEN, Hkv, d).transpose(0, 3, 1, 2, 4)
    vs_blocks = v_slc.reshape(B, n_slc, SLC_LEN, Hkv, d).transpose(0, 3, 1, 2, 4)
    cmp_end = jnp.arange(n_cmp) * CMP_STRIDE + (CMP_LEN - 1)
    blk_ids = jnp.arange(n_slc)
    gather = jax.vmap(jax.vmap(lambda blocks, ids: blocks[ids]))

    def block_fn(args):
        i, qb, qrb = args
        t = i * Q_BLOCK + jnp.arange(Q_BLOCK)
        s = jnp.einsum('bqhgd,bnhd->bhgqn', qb, k_cmp, preferred_element_type=jnp.float32) * ATTN_SCALE
        valid = cmp_end[None, :] <= t[:, None]
        p_cmp = jnp.where(valid, jax.nn.softmax(jnp.where(valid, s, NEG_INF), axis=-1), 0.0)
        o_cmp = jnp.einsum('bhgqn,bnhd->bqhgd', p_cmp.astype(v_cmp.dtype), v_cmp)
        imp = jnp.pad(p_cmp.sum(axis=2), ((0, 0), (0, 0), (0, 0), (0, ratio * n_slc - n_cmp)))
        imp = imp.reshape(B, Hkv, Q_BLOCK, n_slc, ratio)
        imp = imp.sum(-1) + jnp.pad(imp[..., :-1, -1], ((0, 0), (0, 0), (0, 0), (1, 0)))
        cur = (t // SLC_LEN)[:, None]
        forced = (blk_ids == 0) | (blk_ids == cur) | (blk_ids == cur - 1)
        causal = blk_ids * SLC_LEN <= t[:, None]
        score = jnp.where(forced, SLC_FORCED_SCORE, jnp.where(causal, imp, NEG_INF))
        _, idx = lax.top_k(score, top_k)
        kg = gather(ks_blocks, idx).reshape(B, Hkv, Q_BLOCK, top_k * SLC_LEN, d)
        vg = gather(vs_blocks, idx).reshape(B, Hkv, Q_BLOCK, top_k * SLC_LEN, d)
        kpos = (idx[..., None] * SLC_LEN + jnp.arange(SLC_LEN)).reshape(B, Hkv, Q_BLOCK, top_k * SLC_LEN)
        sel_ok = kpos <= t[None, None, :, None]
        s = jnp.einsum('bqhgd,bhqkd->bhgqk', qrb, kg, preferred_element_type=jnp.float32) * ATTN_SCALE
        p = jax.nn.softmax(jnp.where(sel_ok[:, :, None], s, NEG_INF), axis=-1)
        o_slc = jnp.einsum('bhgqk,bhqkd->bqhgd', p.astype(vg.dtype), vg)
        return o_cmp, o_slc

    def to_blocks(a):
        return a.reshape(B, nb, Q_BLOCK, Hkv, G, d).transpose(1, 0, 2, 3, 4, 5)

    def from_blocks(a):
        return a.transpose(1, 0, 2, 3, 4, 5).reshape(B, S, H, d)

    o_cmp, o_slc = lax.map(block_fn, (jnp.arange(nb), to_blocks(q), to_blocks(q_rot)))
    o_win = banded_attention(q_rot, apply_rope(k_win, cos, sin), v_win, NSA_WINDOW)
    gates = jax.nn.sigmoid(gate_logits.astype(jnp.float32)).reshape(B, S, 3, H, 1).astype(q.dtype)
    o = gates[:, :, 0] * from_blocks(o_cmp) + gates[:, :, 1] * from_blocks(o_slc) + gates[:, :, 2] * o_win
    return o.reshape(B, S, H * d)

def short_causal_conv(x, w):
    y = lax.conv_general_dilated(x, w[:, None, :].astype(x.dtype), window_strides=(1,),
                                 padding=[(CONV_WIDTH - 1, 0)], dimension_numbers=('NWC', 'WIO', 'NWC'),
                                 feature_group_count=x.shape[-1])
    return jax.nn.silu(y)

def gated_delta_net(qkv, a, b, z, conv_w, A_log, dt_bias, norm_w):
    B, S, _ = qkv.shape
    H, dk = C_HEADS, C_HEAD_DIM
    C = GDN_CHUNK
    nc = S // C
    f32 = jnp.float32
    q, k, v = jnp.split(short_causal_conv(qkv, conv_w).astype(f32), 3, axis=-1)
    q = l2norm(q.reshape(B, S, H, dk)) * (dk ** -0.5)
    k = l2norm(k.reshape(B, S, H, dk))
    v = v.reshape(B, S, H, dk)
    beta = jax.nn.sigmoid(b.astype(f32))
    g = -jnp.exp(A_log.astype(f32)) * jax.nn.softplus(a.astype(f32) + dt_bias.astype(f32))

    def chunk(t):
        return t.reshape(B, nc, C, H, dk).transpose(0, 3, 1, 2, 4)

    q, k, v = chunk(q), chunk(k), chunk(v)
    beta = beta.reshape(B, nc, C, H).transpose(0, 3, 1, 2)
    gc = jnp.cumsum(g.reshape(B, nc, C, H).transpose(0, 3, 1, 2), axis=-1)
    lower = jnp.tril(jnp.ones((C, C), dtype=bool))
    strict = jnp.tril(jnp.ones((C, C), dtype=bool), -1)
    decay = jnp.where(lower, jnp.exp(jnp.where(lower, gc[..., :, None] - gc[..., None, :], 0.0)), 0.0)
    k_beta = k * beta[..., None]
    a_mat = jnp.where(strict, jnp.einsum('bhncd,bhnsd->bhncs', k_beta, k) * decay, 0.0)
    rhs = jnp.concatenate([v * beta[..., None], k_beta * jnp.exp(gc)[..., None]], axis=-1)
    sol = lax.linalg.triangular_solve(a_mat + jnp.eye(C, dtype=f32), rhs, left_side=True, lower=True,
                                      unit_diagonal=True)
    u, w = sol[..., :dk], sol[..., dk:]
    qk = jnp.where(lower, jnp.einsum('bhncd,bhnsd->bhncs', q, k) * decay, 0.0)
    q_dec = q * jnp.exp(gc)[..., None]
    k_dec = k * jnp.exp(gc[..., -1:] - gc)[..., None]
    g_last = jnp.exp(gc[..., -1])

    def step(state, inp):
        u_c, w_c, qk_c, qd_c, kd_c, gl_c = inp
        v_new = u_c - jnp.einsum('bhcd,bhde->bhce', w_c, state)
        o_c = jnp.einsum('bhcd,bhde->bhce', qd_c, state) + jnp.einsum('bhcs,bhse->bhce', qk_c, v_new)
        state = state * gl_c[..., None, None] + jnp.einsum('bhcd,bhce->bhde', kd_c, v_new)
        return state, o_c

    xs = tuple(jnp.moveaxis(t, 2, 0) for t in (u, w, qk, q_dec, k_dec, g_last))
    _, o = lax.scan(step, jnp.zeros((B, H, dk, dk), f32), xs)
    o = o.transpose(1, 0, 3, 2, 4).reshape(B, S, H, dk)
    o = rms_norm(o, norm_w) * jax.nn.silu(z.reshape(B, S, H, dk).astype(f32))
    return o.reshape(B, S, H * dk).astype(z.dtype)

def hybrid_layer(x, c, cos, sin, norm_mix, norm_ffn, ada_w, ada_b, w_in, attn_sinks,
                 cmp_k_w1, cmp_k_w2, cmp_v_w1, cmp_v_w2, cmp_pe_k, cmp_pe_v,
                 conv_w, A_log, dt_bias, gdn_norm, w_out, w_gate_up, w_down):
    B, S, _ = x.shape
    mod = jax.nn.silu(c) @ ada_w + ada_b
    sh_m, sc_m, gt_m, sh_f, sc_f, gt_f = jnp.split(mod[:, None, :], 6, axis=-1)

    h = rms_norm(x, norm_mix) * (1 + sc_m) + sh_m
    points = np.cumsum(IN_SPLITS)[:-1].tolist()
    (aq, ak, av, bq, bkc, bvc, bks, bvs, bkw, bvw, bg, cqkv, cz, ca, cb) = jnp.split(h @ w_in, points, axis=-1)

    def heads(t, n):
        return t.reshape(B, S, n, -1)

    o_a = banded_attention(apply_rope(heads(aq, A_HEADS), cos, sin), apply_rope(heads(ak, A_KV_HEADS), cos, sin),
                           heads(av, A_KV_HEADS), A_WINDOW, attn_sinks).reshape(B, S, A_Q)
    o_b = nsa_mixer(heads(bq, B_HEADS), heads(bkc, B_KV_HEADS), heads(bvc, B_KV_HEADS),
                    heads(bks, B_KV_HEADS), heads(bvs, B_KV_HEADS), heads(bkw, B_KV_HEADS), heads(bvw, B_KV_HEADS),
                    bg, cos, sin, cmp_k_w1, cmp_k_w2, cmp_v_w1, cmp_v_w2, cmp_pe_k, cmp_pe_v)
    o_c = gated_delta_net(cqkv, ca, cb, cz, conv_w, A_log, dt_bias, gdn_norm)
    x = x + gt_m * (jnp.concatenate([o_a, o_b, o_c], axis=-1) @ w_out)

    h = rms_norm(x, norm_ffn) * (1 + sc_f) + sh_f
    gate, up = jnp.split(h @ w_gate_up, 2, axis=-1)
    return x + gt_f * ((jax.nn.silu(gate) * up) @ w_down)

def first_inputs(seed: int = 0) -> dict:
    key = jax.random.key(seed)
    ks = jax.random.split(key, 24)
    f32 = jnp.float32
    L, D = DEPTH, D_MODEL
    cmp_in = CMP_LEN * HEAD_DIM

    def nrm(k, shape, scale):
        return jax.random.normal(k, shape, f32) * scale

    dt = jnp.exp(jax.random.uniform(ks[16], (L, C_HEADS), f32, math.log(1e-3), math.log(1e-1)))
    return {
        'x': nrm(ks[0], (BATCH, SEQ, D), 1.0),
        'c': nrm(ks[1], (BATCH, D), 1.0),
        'norm_mix': 1.0 + nrm(ks[2], (L, D), 0.1),
        'norm_ffn': 1.0 + nrm(ks[3], (L, D), 0.1),
        'ada_w': nrm(ks[4], (L, D, 6 * D), 0.5 * D ** -0.5),
        'ada_b': nrm(ks[5], (L, 6 * D), 0.01),
        'w_in': nrm(ks[6], (L, D, IN_WIDTH), D ** -0.5),
        'attn_sinks': nrm(ks[7], (L, A_HEADS), 1.0),
        'cmp_k_w1': nrm(ks[8], (L, cmp_in, CMP_HIDDEN), cmp_in ** -0.5),
        'cmp_k_w2': nrm(ks[9], (L, CMP_HIDDEN, HEAD_DIM), CMP_HIDDEN ** -0.5),
        'cmp_v_w1': nrm(ks[10], (L, cmp_in, CMP_HIDDEN), cmp_in ** -0.5),
        'cmp_v_w2': nrm(ks[11], (L, CMP_HIDDEN, HEAD_DIM), CMP_HIDDEN ** -0.5),
        'cmp_pe_k': nrm(ks[12], (L, CMP_LEN, HEAD_DIM), 0.1),
        'cmp_pe_v': nrm(ks[13], (L, CMP_LEN, HEAD_DIM), 0.1),
        'gdn_conv_w': nrm(ks[14], (L, CONV_WIDTH, 3 * C_QK), CONV_WIDTH ** -0.5),
        'gdn_A_log': jnp.log(jax.random.uniform(ks[15], (L, C_HEADS), f32, 1.0, 16.0)),
        'gdn_dt_bias': dt + jnp.log(-jnp.expm1(-dt)),
        'gdn_norm': 1.0 + nrm(ks[17], (L, C_HEAD_DIM), 0.1),
        'w_out': nrm(ks[18], (L, MIX_WIDTH, D), MIX_WIDTH ** -0.5),
        'w_gate_up': nrm(ks[19], (L, D, 2 * D_FF), D ** -0.5),
        'w_down': nrm(ks[20], (L, D_FF, D), D_FF ** -0.5),
        'final_norm': 1.0 + nrm(ks[21], (D,), 0.1),
    }

def first_block(x, c, norm_mix, norm_ffn, ada_w, ada_b, w_in, attn_sinks, cmp_k_w1, cmp_k_w2, cmp_v_w1,
              cmp_v_w2, cmp_pe_k, cmp_pe_v, gdn_conv_w, gdn_A_log, gdn_dt_bias, gdn_norm, w_out,
              w_gate_up, w_down, final_norm):
    cos, sin = rope_tables(x.shape[1], HEAD_DIM)
    for l in range(DEPTH):
        x = hybrid_layer(x, c, cos, sin, norm_mix[l], norm_ffn[l], ada_w[l], ada_b[l], w_in[l], attn_sinks[l],
                         cmp_k_w1[l], cmp_k_w2[l], cmp_v_w1[l], cmp_v_w2[l], cmp_pe_k[l], cmp_pe_v[l],
                         gdn_conv_w[l], gdn_A_log[l], gdn_dt_bias[l], gdn_norm[l], w_out[l],
                         w_gate_up[l], w_down[l])
    return rms_norm(x, final_norm)


N_HEADS = 16
A_HEADS_2 = 8
B_HEADS_2 = 8
MOBA_BLOCK = 256
MOBA_TOPK = 3
MOBA_Q_CHUNK = 64
IDX_HEADS = 16
IDX_DIM = 64
DSA_TOPK_MAX = 256
DSA_Q_CHUNK = 128
DILATED_PATTERNS = ((128, 1), (512, 4), (2048, 16))
REL_BUCKETS = 32
REL_MAX_DIST = 128
D_FF_2 = 2816
CONV_WIDTH_2 = 3
RMS_EPS = 1e-6


def rmsnorm(x, g):
    x32 = x.astype(jnp.float32)
    y = x32 * lax.rsqrt(jnp.mean(x32 * x32, axis=-1, keepdims=True) + RMS_EPS)
    return (y * g.astype(jnp.float32)).astype(x.dtype)

def t5_bucket(dist):
    n = jnp.maximum(dist, 0)
    max_exact = REL_BUCKETS // 2
    nf = jnp.maximum(n, max_exact).astype(jnp.float32)
    large = max_exact + (jnp.log(nf / max_exact) / math.log(REL_MAX_DIST / max_exact)
                         * (REL_BUCKETS - max_exact)).astype(jnp.int32)
    large = jnp.minimum(large, REL_BUCKETS - 1)
    return jnp.where(n < max_exact, n, large)

def split_cols(a, sizes):
    out, off = [], 0
    for s in sizes:
        out.append(a[..., off:off + s])
        off += s
    return out

def moba_attention(q, k, v, table_hk):
    B, H, S, Dh = q.shape
    nb = -(-S // MOBA_BLOCK)
    pad = nb * MOBA_BLOCK - S
    kb = jnp.pad(k, ((0, 0), (0, 0), (0, pad), (0, 0))).reshape(B, H, nb, MOBA_BLOCK, Dh)
    vb = jnp.pad(v, ((0, 0), (0, 0), (0, pad), (0, 0))).reshape(B, H, nb, MOBA_BLOCK, Dh)
    kmean = jnp.mean(kb.astype(jnp.float32), axis=3).astype(k.dtype)
    n_sel = min(MOBA_TOPK, nb - 1)
    scale = Dh ** -0.5
    nq = S // MOBA_Q_CHUNK
    qc = jnp.moveaxis(q.reshape(B, H, nq, MOBA_Q_CHUNK, Dh), 2, 0)
    bi = jnp.arange(B)[:, None, None, None]
    hi = jnp.arange(H)[None, :, None, None]
    offs = jnp.arange(MOBA_BLOCK)
    blk_ids = jnp.arange(nb)

    def chunk(args):
        qi, c = args
        q0 = c * MOBA_Q_CHUNK
        t = q0 + jnp.arange(MOBA_Q_CHUNK)
        own = q0 // MOBA_BLOCK
        k_own = lax.dynamic_index_in_dim(kb, own, axis=2, keepdims=False)
        v_own = lax.dynamic_index_in_dim(vb, own, axis=2, keepdims=False)
        d_own = t[:, None] - (own * MOBA_BLOCK + offs)[None, :]
        l_own = jnp.einsum('bhqd,bhkd->bhqk', qi, k_own).astype(jnp.float32) * scale
        l_own = jnp.where(d_own >= 0, l_own + table_hk[:, t5_bucket(d_own)], -jnp.inf)
        if n_sel == 0:
            p = jax.nn.softmax(l_own, axis=-1).astype(v.dtype)
            return jnp.einsum('bhqk,bhkd->bhqd', p, v_own)
        gate = jnp.einsum('bhqd,bhnd->bhqn', qi, kmean).astype(jnp.float32)
        gate = jnp.where(blk_ids < own, gate, -jnp.inf)
        _, sel = lax.top_k(gate, n_sel)
        k_sel = kb[bi, hi, sel]
        v_sel = vb[bi, hi, sel]
        d_sel = t[None, None, :, None, None] - (sel[..., None] * MOBA_BLOCK + offs)
        l_sel = jnp.einsum('bhqd,bhqnkd->bhqnk', qi, k_sel).astype(jnp.float32) * scale
        l_sel = l_sel + table_hk[hi[..., None], t5_bucket(d_sel)]
        l_sel = jnp.where((sel < own)[..., None], l_sel, -jnp.inf)
        n_k = n_sel * MOBA_BLOCK
        logits = jnp.concatenate([l_sel.reshape(B, H, MOBA_Q_CHUNK, n_k), l_own], axis=-1)
        p = jax.nn.softmax(logits, axis=-1).astype(v.dtype)
        p_sel = p[..., :n_k].reshape(B, H, MOBA_Q_CHUNK, n_sel, MOBA_BLOCK)
        p_own = p[..., n_k:]
        return (jnp.einsum('bhqnk,bhqnkd->bhqd', p_sel, v_sel)
                + jnp.einsum('bhqk,bhkd->bhqd', p_own, v_own))

    out = lax.map(chunk, (qc, jnp.arange(nq, dtype=jnp.int32)))
    return jnp.moveaxis(out, 0, 2).reshape(B, H, S, Dh)

def dsa_attention(q, k, v, q_idx, k_idx, w_idx, table_hk):
    B, S, H, Dh = q.shape
    n_keep = min(DSA_TOPK_MAX, S // 4)
    nq = S // DSA_Q_CHUNK
    scale = Dh ** -0.5
    key_pos = jnp.arange(S)
    bi = jnp.arange(B)[:, None, None]

    def chunkify(a):
        return jnp.moveaxis(a.reshape((B, nq, DSA_Q_CHUNK) + a.shape[2:]), 1, 0)

    def chunk(args):
        qi, qii, wi, c = args
        t = c * DSA_Q_CHUNK + jnp.arange(DSA_Q_CHUNK)
        rel = jax.nn.relu(jnp.einsum('bqhd,bsd->bqhs', qii, k_idx) * (IDX_DIM ** -0.5))
        score = jnp.einsum('bqhs,bqh->bqs', rel, wi).astype(jnp.float32)
        score = jnp.where(key_pos[None, :] <= t[:, None], score, -jnp.inf)
        _, sel = lax.top_k(score, n_keep)
        k_sel = k[bi, sel]
        v_sel = v[bi, sel]
        d = t[None, :, None] - sel
        logits = jnp.einsum('bqhd,bqkhd->bhqk', qi, k_sel).astype(jnp.float32) * scale
        logits = logits + jnp.moveaxis(table_hk[:, t5_bucket(d)], 0, 1)
        logits = jnp.where((d >= 0)[:, None], logits, -jnp.inf)
        p = jax.nn.softmax(logits, axis=-1).astype(v.dtype)
        return jnp.einsum('bhqk,bqkhd->bqhd', p, v_sel)

    out = lax.map(chunk, (chunkify(q), chunkify(q_idx), chunkify(w_idx),
                          jnp.arange(nq, dtype=jnp.int32)))
    return jnp.moveaxis(out, 0, 1).reshape(B, S, H, Dh)

def dilated_branch(q, k, v, table_hk, window, dilation):
    B, H, S, Dh = q.shape
    w_sub = window // dilation
    bb = w_sub
    n = S // dilation
    nbk = -(-n // bb)
    npad = nbk * bb
    scale = Dh ** -0.5

    def to_sub(a):
        a = jnp.swapaxes(a.reshape(B, H, n, dilation, Dh), 2, 3)
        return jnp.pad(a, ((0, 0), (0, 0), (0, 0), (0, npad - n), (0, 0)))

    def band(a):
        ap = jnp.pad(a, ((0, 0), (0, 0), (0, 0), (bb, 0), (0, 0)))
        prev = ap[:, :, :, :npad].reshape(B, H, dilation, nbk, bb, Dh)
        cur = a.reshape(B, H, dilation, nbk, bb, Dh)
        return jnp.concatenate([prev, cur], axis=4)

    qs = to_sub(q).reshape(B, H, dilation, nbk, bb, Dh)
    kband = band(to_sub(k))
    vband = band(to_sub(v))
    logits = jnp.einsum('bhrnqd,bhrnkd->bhrnqk', qs, kband).astype(jnp.float32) * scale
    a_i = jnp.arange(bb)
    m_i = jnp.arange(2 * bb)
    di = a_i[:, None] + bb - m_i[None, :]
    band_ok = (di >= 0) & (di <= w_sub)
    j_idx = jnp.arange(nbk)[:, None] * bb - bb + m_i[None, :]
    mask = band_ok[None] & (j_idx >= 0)[:, None, :]
    bias = table_hk[:, t5_bucket(di * dilation)][:, None, None]
    logits = jnp.where(mask, logits + bias, -jnp.inf)
    mx = jnp.max(logits, axis=-1, keepdims=True)
    e = jnp.exp(logits - mx)
    den = jnp.sum(e, axis=-1, keepdims=True)
    o = jnp.einsum('bhrnqk,bhrnkd->bhrnqd', (e / den).astype(v.dtype), vband)
    lse = (mx + jnp.log(den))[..., 0]
    o = jnp.swapaxes(o.reshape(B, H, dilation, npad, Dh)[:, :, :, :n], 2, 3).reshape(B, H, S, Dh)
    lse = jnp.swapaxes(lse.reshape(B, H, dilation, npad)[:, :, :, :n], 2, 3).reshape(B, H, S)
    return o, lse

def dilated_mixture(q, k, v, table_hk):
    outs, lses = [], []
    for window, dilation in DILATED_PATTERNS:
        o, l = dilated_branch(q, k, v, table_hk, window, dilation)
        outs.append(o)
        lses.append(l)
    alpha = jax.nn.softmax(jnp.stack(lses, axis=0), axis=0)
    return jnp.einsum('pbhs,pbhsd->bhsd', alpha.astype(v.dtype), jnp.stack(outs, axis=0))

def conv_ffn(h, w_up, conv_w, conv_b, w_down):
    S = h.shape[1]
    u = h @ w_up
    up = jnp.pad(u, ((0, 0), (CONV_WIDTH_2 - 1, 0), (0, 0)))
    c = conv_b
    for j in range(CONV_WIDTH_2):
        c = c + conv_w[j] * up[:, j:j + S]
    val, gate = jnp.split(c, 2, axis=-1)
    return (jax.nn.silu(gate) * val) @ w_down

def second_inputs(seed: int = 0) -> dict:
    key = jax.random.key(seed)
    ks = jax.random.split(key, 13)
    n_even = (DEPTH + 1) // 2
    n_odd = DEPTH // 2
    even_in = 3 * A_HEADS_2 * HEAD_DIM + 3 * B_HEADS_2 * HEAD_DIM + IDX_HEADS * IDX_DIM + IDX_DIM + IDX_HEADS
    odd_in = 3 * N_HEADS * HEAD_DIM
    mix = N_HEADS * HEAD_DIM

    def nrm(k, shape, s):
        return jax.random.normal(k, shape, jnp.float32) * s

    return {
        'x': nrm(ks[0], (BATCH, SEQ, D_MODEL), 1.0),
        'w_in_even': nrm(ks[1], (n_even, D_MODEL, even_in), D_MODEL ** -0.5),
        'idx_k_norm': 1.0 + nrm(ks[2], (n_even, IDX_DIM), 0.02),
        'w_in_odd': nrm(ks[3], (n_odd, D_MODEL, odd_in), D_MODEL ** -0.5),
        'w_o': nrm(ks[4], (DEPTH, mix, D_MODEL), mix ** -0.5),
        'rel_bias': nrm(ks[5], (REL_BUCKETS, N_HEADS), 0.2),
        'attn_norm': 1.0 + nrm(ks[6], (DEPTH, D_MODEL), 0.02),
        'ffn_norm': 1.0 + nrm(ks[7], (DEPTH, D_MODEL), 0.02),
        'w_up': nrm(ks[8], (DEPTH, D_MODEL, 2 * D_FF_2), D_MODEL ** -0.5),
        'conv_w': nrm(ks[9], (DEPTH, CONV_WIDTH_2, 2 * D_FF_2), CONV_WIDTH_2 ** -0.5),
        'conv_b': nrm(ks[10], (DEPTH, 2 * D_FF_2), 0.02),
        'w_down': nrm(ks[11], (DEPTH, D_FF_2, D_MODEL), D_FF_2 ** -0.5),
        'final_norm': 1.0 + nrm(ks[12], (D_MODEL,), 0.02),
    }

def second_block(x, w_in_even, idx_k_norm, w_in_odd, w_o, rel_bias, attn_norm, ffn_norm,
              w_up, conv_w, conv_b, w_down, final_norm):
    B, S, _ = x.shape
    mix = N_HEADS * HEAD_DIM
    sizes_even = [A_HEADS_2 * HEAD_DIM] * 3 + [B_HEADS_2 * HEAD_DIM] * 3 + [IDX_HEADS * IDX_DIM, IDX_DIM, IDX_HEADS]
    sizes_odd = [N_HEADS * HEAD_DIM] * 3
    table_a = rel_bias[:, :A_HEADS_2].T
    table_b = rel_bias[:, A_HEADS_2:A_HEADS_2 + B_HEADS_2].T
    table_c = rel_bias.T
    for layer in range(DEPTH):
        h = rmsnorm(x, attn_norm[layer])
        if layer % 2 == 0:
            j = layer // 2
            qa, ka, va, qb, kb, vb, qi, ki, wi = split_cols(h @ w_in_even[j], sizes_even)
            qa, ka, va = (jnp.swapaxes(a.reshape(B, S, A_HEADS_2, HEAD_DIM), 1, 2) for a in (qa, ka, va))
            o_a = jnp.swapaxes(moba_attention(qa, ka, va, table_a), 1, 2)
            qb, kb, vb = (a.reshape(B, S, B_HEADS_2, HEAD_DIM) for a in (qb, kb, vb))
            o_b = dsa_attention(qb, kb, vb,
                                qi.reshape(B, S, IDX_HEADS, IDX_DIM),
                                rmsnorm(ki, idx_k_norm[j]),
                                wi * (IDX_HEADS ** -0.5),
                                table_b)
            mixed = jnp.concatenate([o_a, o_b], axis=2).reshape(B, S, mix)
        else:
            j = layer // 2
            qc, kc, vc = (jnp.swapaxes(a.reshape(B, S, N_HEADS, HEAD_DIM), 1, 2)
                          for a in split_cols(h @ w_in_odd[j], sizes_odd))
            o_c = dilated_mixture(qc, kc, vc, table_c)
            mixed = jnp.swapaxes(o_c, 1, 2).reshape(B, S, mix)
        x = x + mixed @ w_o[layer]
        h = rmsnorm(x, ffn_norm[layer])
        x = x + conv_ffn(h, w_up[layer], conv_w[layer], conv_b[layer], w_down[layer])
    return rmsnorm(x, final_norm)


def setup_inputs(seed=0):
    out = dict(first_inputs(seed))
    for name, value in second_inputs(seed + 1).items():
        if name != "x":
            out[name + "_2"] = value
    return out


def reference(
    x, c, norm_mix, norm_ffn, ada_w, ada_b, w_in, attn_sinks, cmp_k_w1, cmp_k_w2, cmp_v_w1,
    cmp_v_w2, cmp_pe_k, cmp_pe_v, gdn_conv_w, gdn_A_log, gdn_dt_bias, gdn_norm, w_out,
    w_gate_up, w_down, final_norm, w_in_even_2, idx_k_norm_2, w_in_odd_2, w_o_2, rel_bias_2,
    attn_norm_2, ffn_norm_2, w_up_2, conv_w_2, conv_b_2, w_down_2, final_norm_2,
):
    x = first_block(
        x, c, norm_mix, norm_ffn, ada_w, ada_b, w_in, attn_sinks, cmp_k_w1, cmp_k_w2, cmp_v_w1,
        cmp_v_w2, cmp_pe_k, cmp_pe_v, gdn_conv_w, gdn_A_log, gdn_dt_bias, gdn_norm, w_out,
        w_gate_up, w_down, final_norm,
    )
    return second_block(
        x, w_in_even_2, idx_k_norm_2, w_in_odd_2, w_o_2, rel_bias_2, attn_norm_2, ffn_norm_2,
        w_up_2, conv_w_2, conv_b_2, w_down_2, final_norm_2,
    )


_drawn_inputs = setup_inputs


def setup_inputs(seed=0):
    import zlib

    import numpy as np

    out = dict(_drawn_inputs(seed))
    spreads = {}
    factors = {'attn_sinks': 5.828,
     'cmp_pe_k': 8.0,
     'cmp_pe_v': 3.861,
     'idx_k_norm_2': 3.211,
     'ffn_norm_2': 2.752,
     'conv_b_2': 2.769,
     'final_norm_2': 2.835}
    for name, (base, spread) in spreads.items():
        noise = np.random.default_rng([zlib.crc32(name.encode()), seed]).standard_normal(out[name].shape)
        drawn = base * np.exp(spread * noise) if base else spread * noise
        out[name] = jnp.asarray(drawn.astype(out[name].dtype))
    for name, factor in factors.items():
        out[name] = (out[name] * factor).astype(out[name].dtype)
    return out
```

```python
import concourse.bass as bass
from concourse import mybir
from contextlib import ExitStack

F32 = mybir.dt.float32
ALU = mybir.AluOpType
ACT = mybir.ActivationFunctionType
AX = mybir.AxisListType

P = 128
S = 256
QT = S // P
D = 1024
KT = D // P
HD = 64
NG = 4
L1 = 2
DFF = 2816
FT = DFF // P
CH = 512
ADA_L = 6 * D // CH
ADA = L1 * ADA_L
ADA_FIRST = 2 * D // CH
SLOTS = 3
EPS = 1e-6
SCALE = HD ** -0.5
NEG = -1e30
N_CMP = S // 16 - 1
CMP_PAIRS = 16
GH = 4
GD = 128
NCH = QT * GH
DEPTH = 3
LEVELS = 7
TOKW = 276
GATES, A_COL, B_COL = 256, 268, 272
KQ_BANKS = (4, 5, 6, 3)
MOD_COL = 256
BIAS_W = 384

V1 = dict(norm_mix=(0, 8), norm_ffn=(8, 8), ada_b=(16, 48), conv=(64, 48), gnorm=(112, 128), sink=(240, 4),
          a_log=(244, 4), dt=(248, 4), pe_k=(252, 16), pe_v=(268, 16), w2k=(284, 256), w2v=(540, 128))
V1W = 668
V2 = dict(norm_attn=(0, 8), norm_ffn=(8, 8), conv_w=(16, 132), conv_b=(148, 44))
V2W = 192
CN = dict(cos=(0, 256), sin=(256, 256), ident=(512, 128), rot=(640, 128), ones=(768, 128), halves=(896, 128),
          upper=(1024, 128), strict=(1152, 128), levels=(1280, 896), causal0=(2176, 128), band1=(2304, 256),
          causal1=(2560, 256), cmp_mask=(2816, 30), cmp_valid=(2846, 30), final1=(2876, 8), final2=(2884, 8),
          knorm=(2892, 1), eps=(2893, 1))
CNW = 2894


class Chain:

    def __init__(self, eng, sem):
        self.eng, self.sem, self.n = eng, sem, 0

    def mark(self, ins):
        self.n += 1
        ins.then_inc(self.sem, 1)

    def wait(self):
        self.eng.wait_ge(self.sem, self.n)

    def __call__(self, ins):
        self.mark(ins)
        self.wait()


def hybrid_then_mixture(nc, xT, c, vec1, vec2, consts, dist, table, ada, w_mix, w_tok, w_cmp, w_out, w_gu, w_dn,
                        even_in, even_tail, odd_in, w_o2, w_up2, w_dn2, y, bias_dram,
                        bias_wide):
    phases = {}
    count = dict(chunk=0, event=0, tile=0, ada=0)
    chunk_end = []
    ada_at = []

    def phase(name, chunks, events, tiles, ada_after=0):
        phases[name] = dict(n0=count["chunk"], e0=count["event"], t0=count["tile"], chunks=chunks, at=[])
        for j, ev in enumerate(events):
            phases[name]["at"].append(count["chunk"])
            count["event"] += ev
            chunk_end.append(("event", count["event"]))
            count["chunk"] += 1
            if j < ada_after:
                ada_chunks(1)
        count["tile"] += tiles

    def ada_chunks(n):
        for _ in range(n):
            ada_at.append(count["chunk"])
            count["ada"] += 1
            chunk_end.append(("sums", count["ada"]))
            count["chunk"] += 1

    ada_chunks(ADA_FIRST)
    for l in range(L1):
        phase(f"in{l}", 6, [4] * 5 + [2], 22, 6)
        phase(f"tok{l}", 1, [2], 2)
        phase(f"cmp{l}", 2, [1] * 2, 0)
        ada_chunks(2)
        phase(f"out{l}", 2, [4] * 2, 8)
        phase(f"gu{l}", 11, [4] * 11, 44)
        phase(f"dn{l}", 8, [1] * 8, 8, ADA_FIRST if l == 0 else 0)
    phase("even", 8, [4, 4, 2, 4, 4, 2, 4, 4], 28)
    phase("tail", 1, [3], 3)
    phase("o0", 2, [4] * 2, 8)
    phase("up0", 11, [4] * 11, 44)
    phase("down0", 8, [1] * 8, 8)
    phase("odd", 6, [4, 4, 4, 4, 2, 2], 20)
    phase("o1", 2, [4] * 2, 8)
    phase("up1", 11, [4] * 11, 44)
    phase("down1", 8, [1] * 8, 8)

    norm_input = [None, "out0", "dn0", "out1", "dn1", None, "o0", "down0", "o1", "down1"]
    in_place = 4
    norm_end = [KT * (n + 1 - (n >= in_place)) for n in range(len(norm_input))]

    ctx = ExitStack()
    with ctx:
        def sb(name, shape):
            return ctx.enter_context(nc.sbuf_tensor(name, shape, F32))

        def sem(name):
            return ctx.enter_context(nc.semaphore(name))

        ring = sb("ring", [P, SLOTS, KT * CH])
        x = sb("x", [P, KT, S])
        h = sb("h", [P, KT, S])
        mix = sb("mix", [P, KT, S])
        v1 = sb("v1", [P, L1, V1W])
        v2 = sb("v2", [P, 2, V2W])
        cn = sb("cn", [P, CNW])
        c_in = sb("c_in", [P, KT])
        c_silu = sb("c_silu", [P, KT])
        table_sb = sb("table_sb", [33, 16])
        mod = sb("mod", [P, L1, 48])
        gain = sb("gain", [P, L1, 2, KT])
        std = sb("std", [P, S])
        rstd = sb("rstd", [P, S])
        sg = sb("sg", [P, 2, S])
        small = sb("small", [P, 176])
        lg = sb("lg", [P, DEPTH, NG, S])
        pT = sb("pT", [P, 2, QT, NG * P])
        negm = sb("negm", [P, DEPTH, NG])
        sums = sb("sums", [P, DEPTH, NG])
        esink = sb("esink", [P, DEPTH, NG])
        rec = sb("rec", [P, DEPTH, NG])
        kcT = sb("kcT", [P, N_CMP])
        vc = sb("vc", [N_CMP, HD])
        hid = sb("hid", [P, 2, 2, N_CMP])
        arena = sb("arena", [P, 23104])

        def view(at, *shape):
            size = 1
            for n in shape:
                size *= n
            flat = arena[:, at:at + size]
            if len(shape) == 1:
                return flat
            if len(shape) == 2:
                return flat.rearrange("p (a b) -> p a b", a=shape[0])
            return flat.rearrange("p (a b c) -> p a b c", a=shape[0], b=shape[1])

        conv_in = view(0, 12, S + 3)
        conv = view(3108, 12, S)
        kn = view(0, NCH, GD)
        kb = view(1024, NCH, GD)
        vb = view(2048, NCH, GD)
        qn = view(3072, NCH, GD)
        kbg = view(4096, GH, GD)
        qd = view(4608, GH, GD)
        kd = view(5120, GH, GD)
        act_T = view(0, FT, S)
        cv = view(FT * S, 2, 2, S)
        tok = view(6656, 3, NCH, GD)
        kbqT = view(6656, NCH, 2, GD)
        knT = view(8704, NCH, GD)
        qdT = view(9728, GH, GD)
        Dm = view(10240, NCH, P)
        MT = view(11264, NCH, P)
        QKT = view(12288, NCH, P)
        MbT = view(13312, 2, NCH, P)
        X = view(15360, NCH, P)
        XT = view(16384, NCH, P)
        T1 = view(17408, NCH, P)
        U = view(10240, NCH, GD)
        wT = view(18432, GH, P)
        st = view(18944, GH, GD)
        z = view(19456, QT, GH * GD)
        tokp = view(20480, QT, TOKW)
        gB = view(13312, NCH, P)
        sq_tok = view(14336, NCH, GD)
        o_n = view(15360, NCH, GD)
        raw = view(21056, 8, S)
        dist_sb = view(21056, 2, BIAS_W)[0:33]
        tab_rows = view(21824, 2, BIAS_W)[0:16]
        rot = view(11264, 7, S)
        xpe = view(16384, 2, CMP_PAIRS * N_CMP).rearrange("p a (k n) -> p a k n", k=CMP_PAIRS)
        tmp = sg
        acc = view(17408, 2, CH)
        qk2 = view(0, 25, S)
        vv2 = view(6656, QT, 1024)
        bias2 = view(8704, 2, 16, S)
        rel = view(16896, 2, NG, S)
        score = view(18944, QT, S)
        work = view(19456, 2, S)
        selm = view(19968, QT, S)
        wi = view(20480, QT, 16)
        max8 = view(20512, 8)

        bank = ctx.enter_context(nc.psum_tensor("bank", [P, 8, 512], F32))

        def vec(l, name):
            at, n = V1[name]
            return v1[:, l, at:at + n]

        def vec_b(l, name):
            at, n = V2[name]
            return v2[:, l, at:at + n]

        def const(name):
            at, n = CN[name]
            return cn[:, at:at + n]

        ident = const("ident")
        upper = const("upper")

        def over(ap, n):
            return ap.rearrange("p (a m) -> p a m", a=1).to_broadcast([ap.shape[0], n, ap.shape[1]])

        def along(ap, n):
            return ap.rearrange("p (m a) -> p m a", a=1).to_broadcast([ap.shape[0], ap.shape[1], n])

        consts_in = sem("consts_in")
        c_loaded = sem("c_loaded")
        slot_in = [sem(f"slot_in{s}") for s in range(SLOTS)]
        gemm_ready = sem("gemm_ready")
        gemm_freed = sem("gemm_freed")
        c_ready = sem("c_ready")
        x_ready = sem("x_ready")
        acc_ready = sem("acc_ready")
        mod_ready = sem("mod_ready")
        mod_read = sem("mod_read")
        sq_ready = sem("sq_ready")
        ssq_ready = sem("ssq_ready")
        std_ready = sem("std_ready")
        hn_ready = sem("hn_ready")
        h_ready = sem("h_ready")
        rot_ready = sem("rot_ready")
        rope_done = sem("rope_done")
        conv_ready = sem("conv_ready")
        silu_ready = sem("silu_ready")
        xpe_ready = sem("xpe_ready")
        hid_ready = sem("hid_ready")
        kc_ps_ready = sem("kc_ps_ready")
        kc_ready = sem("kc_ready")
        gate_exp = sem("gate_exp")
        gate_arg = sem("gate_arg")
        scores_ready = sem("scores_ready")
        logits_done = sem("logits_done")
        exps_done = sem("exps_done")
        rec_ready = sem("rec_ready")
        probs_ready = sem("probs_ready")
        trans_ready = sem("trans_ready")
        pt_ready = sem("pt_ready")
        pv_done = sem("pv_done")
        o_evac = sem("o_evac")
        gt_ready = sem("gt_ready")
        gt_copied = sem("gt_copied")
        g_arg = sem("g_arg")
        g_fun = sem("g_fun")
        g_ready = sem("g_ready")
        gc_ready = sem("gc_ready")
        scaled = sem("scaled")
        kq_ready = sem("kq_ready")
        mt_ready = sem("mt_ready")
        mb_ready = sem("mb_ready")
        t1_ready = sem("t1_ready")
        t1_copied = sem("t1_copied")
        dx_ready = sem("dx_ready")
        x_upd = sem("x_upd")
        u_ready = sem("u_ready")
        u_copied = sem("u_copied")
        state_ready = sem("state_ready")
        state_copied = sem("state_copied")
        ws_ready = sem("ws_ready")
        vnew_ready = sem("vnew_ready")
        o_ready = sem("o_ready")
        osq_ready = sem("osq_ready")
        on_ready = sem("on_ready")
        cv_ready = sem("cv_ready")
        tap_done = sem("tap_done")
        sg_ready = sem("sg_ready")
        act_ready = sem("act_ready")
        tab_ready = sem("tab_ready")
        tab_copied = sem("tab_copied")
        tab_out = sem("tab_out")
        wide_out = sem("wide_out")
        bias_in = sem("bias_in")
        ki_sq = sem("ki_sq")
        ki_ssq = sem("ki_ssq")
        ki_std = sem("ki_std")
        ki_ready = sem("ki_ready")
        ix_ready = sem("ix_ready")
        ix_relu = sem("ix_relu")
        ix_acc = sem("ix_acc")
        y_out = sem("y_out")
        dve_chain = sem("dve_chain")
        act_chain = sem("act_chain")
        pool_chain = sem("pool_chain")

        units = []
        stages = {}

        def stage(name, us):
            stages[name] = (len(units), len(units) + len(us))
            units.extend(us)

        LO, HI = slice(0, HD), slice(HD, P)

        def hybrid_units(l):
            us = []
            for qt in range(QT):
                qs, w = slice(qt * P, qt * P + P), P * (qt + 1)
                rows = [(0, LO), (1, LO), (0, HI), (1, HI)]
                us.append(dict(
                    q=[rot[r, t, qs] for t, r in rows], k=[rot[r, 2, 0:w] for _, r in rows], w=w,
                    bias=over(const("causal0") if qt == 0 else const("band1"), NG), sink=vec(l, "sink"),
                    pv=[(0, 2, lambda kt: tokp[:, kt, 0:HD]), (2, 4, lambda kt: tokp[:, kt, HD:2 * HD])],
                    start=True, end=True, qs=qs, evac=[(0, LO, 0), (1, HI, 0), (2, LO, 1), (3, HI, 1)], gate=None))
            heads = [(0, LO), (1, LO), (0, HI), (1, HI)]
            evac = [(0, LO, 2), (1, LO, 3), (2, HI, 2), (3, HI, 3)]
            for qt in range(QT):
                qs, w = slice(qt * P, qt * P + P), P * (qt + 1)
                causal = over(const("causal0") if qt == 0 else const("causal1"), NG)
                cm = const("cmp_mask")[:, qt * N_CMP:(qt + 1) * N_CMP]
                cval = const("cmp_valid")[:, qt * N_CMP:(qt + 1) * N_CMP]
                gates = [small[:, 16 * qt + NG * b:16 * qt + NG * b + NG] for b in range(3)]
                us.append(dict(
                    q=[raw[r, 3 + t, qs] for t, r in heads], k=[kcT[r, :] for _, r in heads], w=N_CMP,
                    bias=over(cm, NG), valid=over(cval, NG), sink=None, gate=gates[0],
                    pv=[(0, 4, lambda kt: vc[:, :])], start=True, end=False, qs=qs, evac=evac))
                us.append(dict(
                    q=[rot[r, 3 + t, qs] for t, r in heads],
                    k=[rot[r, 5 if r is LO else 6, 0:w] for _, r in heads], w=w,
                    bias=causal, sink=None, gate=gates[1],
                    pv=[(0, 4, lambda kt: tokp[:, kt, 2 * HD:3 * HD])], start=False, end=False, qs=qs, evac=evac))
                us.append(dict(
                    q=[rot[r, 3 + t, qs] for t, r in heads],
                    k=[rot[r, 6 if r is LO else 5, 0:w] for _, r in heads], w=w,
                    bias=causal, sink=None, gate=gates[2],
                    pv=[(0, 4, lambda kt: tokp[:, kt, 3 * HD:4 * HD])], start=False, end=True, qs=qs, evac=evac))
            return us

        def biased_units(q0, k0, v0, groups, bset, g0, sel):
            us = []
            for g in range(groups):
                for qt in range(QT):
                    qs, w = slice(qt * P, qt * P + P), P * (qt + 1)
                    rows = [(0, LO), (1, LO), (0, HI), (1, HI)]
                    head = [0, 2, 1, 3]
                    us.append(dict(
                        q=[qk2[r, q0 + 2 * g + t, qs] for t, r in rows],
                        k=[qk2[r, k0 + 2 * g + t, 0:w] for t, r in rows], w=w,
                        bias=bias2[:, bset, NG * (g0 + g):NG * (g0 + g) + NG, S - w:S], sink=None, gate=None,
                        sel=over(selm[:, qt, 0:w], NG) if sel else None,
                        pv=[(s, s + 1, (lambda at: lambda kt: vv2[:, kt, at:at + HD])(v0 + HD * (NG * g + head[s])))
                            for s in range(NG)],
                        start=True, end=True, qs=qs,
                        evac=[(0, LO, 2 * (g0 + g)), (1, LO, 2 * (g0 + g) + 1),
                              (2, HI, 2 * (g0 + g)), (3, HI, 2 * (g0 + g) + 1)]))
            return us

        for l in range(L1):
            stage(f"hybrid{l}", hybrid_units(l))
        stage("even", biased_units(0, 4, 0, 2, 0, 0, False) + biased_units(8, 12, 512, 2, 0, 2, True))
        stage("odd", biased_units(0, 8, 0, 4, 1, 0, False))

        def evacs_before(u):
            return sum(units[i]["end"] for i in range(u))

        def key_tiles(u):
            w = units[u]["w"]
            return [(kt, min(P, w - kt * P)) for kt in range((w + P - 1) // P)]

        block = ctx.enter_context(nc.Block())

        @block.sync
        def _(sp):
            sp.dma_start(c_in[:, :], c).then_inc(c_loaded, 16)

            def load(n, src, size):
                if n >= SLOTS:
                    kind, value = chunk_end[n - SLOTS]
                    sp.wait_ge(gemm_ready if kind == "event" else acc_ready, value)
                sp.dma_start(ring[:, n % SLOTS, 0:size], src).then_inc(slot_in[n % SLOTS], 16)

            def load_phase(name, src, per_chunk, size):
                ph = phases[name]
                n0, e0, chunks = ph["n0"], ph["e0"], ph["chunks"]
                turns = (chunks - SLOTS) // SLOTS if per_chunk else 0
                for j in range(min(SLOTS, chunks)):
                    load(n0 + j, src[j], size)
                if turns > 1:
                    with sp.Fori(0, turns) as i:
                        for j in range(SLOTS):
                            sp.wait_ge(gemm_ready, i * (SLOTS * per_chunk) + e0 + per_chunk * (j + 1))
                            sp.dma_start(ring[:, (n0 + j) % SLOTS, 0:size].rearrange("p (a n) -> p a n", a=1),
                                         src[bass.ds(i * SLOTS + SLOTS + j, 1)].rearrange("a p n -> p a n"))\
                                .then_inc(slot_in[(n0 + j) % SLOTS], 16)
                    done = SLOTS * (turns + 1)
                else:
                    done = min(SLOTS, chunks)
                for j in range(done, chunks):
                    load(n0 + j, src[j], size)

            full = KT * CH

            def load_ada(m):
                load(ada_at[m], ada[m], full)

            for l in range(L1):
                if l == 0:
                    for m in range(SLOTS):
                        load_ada(m)
                    for dst, src in ((cn[:, :], consts), (x[:, :, :], xT), (v1[:, :, :], vec1),
                                     (v2[:, :, :], vec2), (dist_sb[:, :, :], dist), (table_sb[:, :], table)):
                        sp.dma_start(dst, src).then_inc(consts_in, 16)
                    for m in range(SLOTS, ADA_FIRST):
                        load_ada(m)
                m = ADA_L * l + ADA_FIRST
                for j, at in enumerate(phases[f"in{l}"]["at"]):
                    load(at, w_mix[l][j], full)
                    load_ada(m + j)
                load(phases[f"tok{l}"]["n0"], w_tok[l], KT * TOKW)
                load_phase(f"cmp{l}", w_cmp[l], 0, full)
                load_ada(m + 6)
                load_ada(m + 7)
                load_phase(f"out{l}", w_out[l], 0, full)
                if l == 0:
                    sp.wait_ge(tab_out, 16)
                    sp.dma_start(bias_wide, bass.AP(tensor=bias_dram.tensor, offset=0,
                                                    ap=[[BIAS_W, 32], [0, P], [1, BIAS_W]])).then_inc(wide_out, 16)
                load_phase(f"gu{l}", w_gu[l], 4, full)
                for j, at in enumerate(phases[f"dn{l}"]["at"]):
                    load(at, w_dn[l][j], FT * P)
                    if l == 0 and j < ADA_FIRST:
                        load_ada(ADA_L + j)
            sp.wait_ge(wide_out, 16)
            sp.wait_ge(gemm_freed, phases["gu1"]["t0"])
            for a in range(2):
                skewed = bass.AP(tensor=bias_wide.tensor, offset=a * 16 * P * BIAS_W + P - 1,
                                 ap=[[BIAS_W - 1, P], [P * BIAS_W, 16], [1, S]])
                sp.dma_start(bias2[:, a, :, :], skewed).then_inc(bias_in, 16)
            load_phase("even", even_in, 0, full)
            load(phases["tail"]["n0"], even_tail, KT * 144)
            load_phase("o0", w_o2[0], 0, full)
            load_phase("up0", w_up2[0], 4, full)
            load_phase("down0", w_dn2[0], 1, FT * P)
            load_phase("odd", odd_in, 0, full)
            load_phase("o1", w_o2[1], 0, full)
            load_phase("up1", w_up2[1], 4, full)
            load_phase("down1", w_dn2[1], 1, FT * P)
            sp.wait_ge(h_ready, norm_end[-1])
            sp.dma_start(y, h[:, :, :]).then_inc(y_out, 16)
            sp.wait_ge(y_out, 16)

        @block.tensor
        def _(pe):
            def chunk_in(n):
                pe.wait_ge(slot_in[n % SLOTS], 16 * (n // SLOTS + 1))

            def tile_free(name, j):
                t0 = phases[name]["t0"]
                if j >= 4:
                    pe.wait_ge(gemm_freed, t0 + j - 3)
                elif j == 0 and t0:
                    pe.wait_ge(gemm_freed, t0)

            def weights(n, cols):
                return ring[:, n % SLOTS, 0:KT * cols].rearrange("p (k n) -> p k n", k=KT)

            def channel_tile(out, w, col, src):
                for k in range(KT):
                    last = nc.tensor.matmul(out, w[:, k, col:col + P], src[:, k, :], start=(k == 0), stop=(k == KT - 1))
                last.then_inc(gemm_ready, 1)

            def token_tile(out, w, lo, hi, src, qt):
                for k in range(KT):
                    last = nc.tensor.matmul(out, src[:, k, qt * P:qt * P + P], w[:, k, lo:hi],
                                            start=(k == 0), stop=(k == KT - 1))
                last.then_inc(gemm_ready, 1)

            def norm_sums(n):
                for k in range(KT):
                    if k % 2 == 0:
                        pe.wait_ge(sq_ready, 4 * n + k // 2 + 1)
                    last = nc.tensor.matmul(bank[:, 7, 0:S], const("ones"), h[:, k, :],
                                            start=(k == 0), stop=(k == KT - 1))
                last.then_inc(ssq_ready, 1)

            def modulations(m0, m1):
                for m in range(m0, m1):
                    pe.wait_ge(acc_ready, m + 1)
                    for t in range(4):
                        at = MOD_COL + 4 * m + t
                        last = nc.tensor.matmul(bank[:, 7, at:at + 1], acc[:, m % 2, t * P:t * P + P],
                                                const("ones")[:, 0:1], start=True, stop=True)
                    last.then_inc(mod_ready, 1)

            def attention(name, m_next=None):
                u0, u1 = stages[name]

                def scores(u):
                    U = units[u]
                    if u >= 2:
                        pe.wait_ge(logits_done, u - 1)
                    for s in range(NG):
                        last = nc.tensor.matmul(bank[:, 2 * (u % 2) + s // 2, (s % 2) * S:(s % 2) * S + U["w"]],
                                                U["q"][s], U["k"][s], start=True, stop=True)
                    last.then_inc(scores_ready, 1)

                def transposes(u):
                    pe.wait_ge(probs_ready, u + 1)
                    if u >= 1:
                        pe.wait_ge(pt_ready, u)
                    for kt, n in key_tiles(u):
                        for s in range(NG):
                            last = nc.tensor.transpose(bank[0:n, 4 + kt, s * P:s * P + P],
                                                       lg[:, u % DEPTH, s, kt * P:kt * P + n], ident)
                    last.then_inc(trans_ready, 1)

                def values(u):
                    U = units[u]
                    pe.wait_ge(pt_ready, u + 1)
                    if U["start"] and evacs_before(u):
                        pe.wait_ge(o_evac, evacs_before(u))
                    tiles = key_tiles(u)
                    for lo, hi, v in U["pv"]:
                        for kt, n in tiles:
                            last = nc.tensor.matmul(
                                bank[0:HD, 6, lo * P:hi * P], v(kt), pT[0:n, u % 2, kt, lo * P:hi * P],
                                start=U["start"] and kt == 0, stop=U["end"] and kt == tiles[-1][0])
                    last.then_inc(pv_done, 1)

                for u in range(u0, u0 + DEPTH):
                    scores(u)
                for u in range(u0, u1):
                    if m_next and u in (u0 + 1, u0 + 2):
                        modulations(m_next + u - u0 - 1, m_next + u - u0)
                    transposes(u)
                    if u + DEPTH < u1:
                        scores(u + DEPTH)
                    values(u)

            def delta_net(l):
                g0 = 15 * l
                u_end = stages[f"hybrid{l}"][1]

                def group(j, srcs, done):
                    if j >= 4:
                        pe.wait_ge(gt_copied, done)
                    for i, src in enumerate(srcs):
                        last = nc.tensor.transpose(bank[:, j % 4, i * P:i * P + P], src, ident)
                    last.then_inc(gt_ready, 1)

                pe.wait_ge(silu_ready, 3 * (l + 1))
                pe.wait_ge(logits_done, u_end)
                for j in range(6):
                    group(j, [conv[:, 4 * (j // 2) + hd, (j % 2) * P:(j % 2) * P + P] for hd in range(GH)], g0 + j - 3)
                pe.wait_ge(g_ready, l + 1)
                pe.wait_ge(pt_ready, u_end)
                pe.wait_ge(o_evac, evacs_before(u_end))
                nc.tensor.matmul(bank[:, 6, 0:NCH], upper, small[:, 96:96 + NCH], start=True, stop=True)
                for ch in range(NCH):
                    last = nc.tensor.matmul(bank[:, 4 + ch // 4, (ch % 4) * P:(ch % 4) * P + P], gB[:, ch, :], upper,
                                            start=True, stop=True)
                last.then_inc(gc_ready, 1)
                pe.wait_ge(scaled, l + 1)
                lists = [[kb[:, 4 * cc + i, :] for i in range(4)] for cc in range(2)] \
                    + [[kn[:, 4 * cc + i, :] for i in range(4)] for cc in range(2)] \
                    + [[qn[:, 4 * cc + i, :] for i in range(4)] for cc in range(2)] + [[qd[:, i, :] for i in range(4)]]
                for j, srcs in enumerate(lists):
                    group(6 + j, srcs, g0 + 6 + j - 3)
                pe.wait_ge(gt_copied, g0 + 13)
                for ch in range(NCH):
                    last = nc.tensor.matmul(bank[:, KQ_BANKS[ch // 2], (ch % 2) * S:(ch % 2) * S + S], knT[:, ch, :],
                                            kbqT[:, ch, :, :].rearrange("p a n -> p (a n)"), start=True, stop=True)
                    if ch % 2:
                        last.then_inc(kq_ready, 1)
                for lv in range(LEVELS):
                    pe.wait_ge(mb_ready, l * LEVELS + lv + 1)
                    for half in range(2):
                        if lv:
                            pe.wait_ge(x_upd, l * 2 * LEVELS + 2 * (lv - 1) + half + 1)
                        for i in range(4):
                            ch = 4 * half + i
                            last = nc.tensor.matmul(bank[:, half, i * P:i * P + P], MbT[:, lv % 2, ch, :],
                                                    X[:, ch, :] if lv else ident, start=True, stop=True)
                        last.then_inc(t1_ready, 1)
                    for half in range(2 if lv else 0):
                        pe.wait_ge(t1_copied, l * 2 * (LEVELS - 1) + 2 * (lv - 1) + half + 1)
                        for i in range(4):
                            ch = 4 * half + i
                            if lv < LEVELS - 1:
                                nc.tensor.matmul(bank[:, 2 + half, i * P:i * P + P], XT[:, ch, :], T1[:, ch, :],
                                                 start=True, stop=True)
                            last = nc.tensor.matmul(bank[:, 4 + half, i * P:i * P + P], T1[:, ch, :], XT[:, ch, :],
                                                    start=True, stop=True)
                        last.then_inc(dx_ready, 1)
                pe.wait_ge(x_upd, (l + 1) * 2 * LEVELS)
                for ch in range(NCH):
                    nc.tensor.matmul(bank[:, ch // 4, (ch % 4) * P:(ch % 4) * P + P], XT[:, ch, :], vb[:, ch, :],
                                     start=True, stop=True)
                for i in range(GH):
                    last = nc.tensor.matmul(bank[:, 2, i * P:i * P + P], kbg[:, i, :], XT[:, GH + i, :],
                                            start=True, stop=True)
                last.then_inc(u_ready, 1)
                pe.wait_ge(u_copied, l + 1)
                for i in range(GH):
                    last = nc.tensor.matmul(bank[:, 3, i * P:i * P + P], kd[:, i, :], U[:, i, :], start=True, stop=True)
                last.then_inc(state_ready, 1)
                for i in range(GH):
                    last = nc.tensor.matmul(bank[:, 4, i * P:i * P + P], QKT[:, i, :], U[:, i, :], start=True, stop=True)
                last.then_inc(o_ready, 1)
                pe.wait_ge(state_copied, l + 1)
                for i in range(GH):
                    last = nc.tensor.matmul(bank[:, 5, i * P:i * P + P], wT[:, i, :], st[:, i, :], start=True, stop=True)
                last.then_inc(ws_ready, 1)
                pe.wait_ge(vnew_ready, l + 1)
                for i in range(GH):
                    nc.tensor.matmul(bank[:, 6, i * P:i * P + P], qdT[:, i, :], st[:, i, :], start=True, stop=False)
                    last = nc.tensor.matmul(bank[:, 6, i * P:i * P + P], QKT[:, GH + i, :], U[:, GH + i, :],
                                            start=False, stop=True)
                last.then_inc(o_ready, 1)
                pe.wait_ge(on_ready, l + 1)
                for cc in range(2):
                    group(13 + cc, [o_n[:, GH * cc + i, :] for i in range(GH)], g0 + 13)

            def projection(name, src, tiles_from):
                ph = phases[name]
                for j in range(KT):
                    if j % 4 == 0:
                        chunk_in(ph["n0"] + j // 4)
                    tile_free(name, j)
                    channel_tile(bank[:, j % 4, 0:S], weights(ph["n0"] + j // 4, CH), (j % 4) * P, src)

            def up(name):
                ph = phases[name]
                n0, t0 = ph["n0"], ph["t0"]

                def one(j, arrived, free):
                    w = weights(n0 + j, CH)
                    pe.wait_ge(slot_in[(n0 + j) % SLOTS], arrived)
                    for m in range(4):
                        pe.wait_ge(gemm_freed, free + m)
                        channel_tile(bank[:, m, 0:S], w, m * P, h)

                turns = 11 // SLOTS
                pe.wait_ge(gemm_freed, t0)
                with pe.Fori(0, turns) as i:
                    for j in range(SLOTS):
                        one(j, i * 16 + 16 * ((n0 + j) // SLOTS + 1), i * (4 * SLOTS) + t0 + 4 * j - 3)
                for j in range(SLOTS * turns, 11):
                    one(j, 16 * ((n0 + j) // SLOTS + 1), t0 + 4 * j - 3)

            def down(name):
                ph = phases[name]
                for j in range(KT):
                    if name == "dn0" and 1 <= j <= ADA_FIRST:
                        modulations(ADA_L + j - 1, ADA_L + j)
                    n = ph["at"][j]
                    chunk_in(n)
                    tile_free(name, j)
                    w = ring[:, n % SLOTS, 0:FT * P].rearrange("p (k n) -> p k n", k=FT)
                    for k in range(FT):
                        last = nc.tensor.matmul(bank[:, j % 4, 0:S], w[:, k, :], act_T[:, k, :],
                                                start=(k == 0), stop=(k == FT - 1))
                    last.then_inc(gemm_ready, 1)

            pe.wait_ge(consts_in, 16 * 6)
            modulations(0, ADA_FIRST)
            for a in range(2):
                last = nc.tensor.matmul(bank[0:16, a, 0:BIAS_W], table_sb[:, :], dist_sb[:, a, :], start=True, stop=True)
            last.then_inc(tab_ready, 1)
            n = 0
            for l in range(L1):
                pe.wait_ge(mod_read, l + 1)
                norm_sums(n)
                pe.wait_ge(tab_copied, 2)
                ph = phases[f"in{l}"]
                m = ADA_L * l + ADA_FIRST
                for j in range(22):
                    if j >= 8 and j % 4 == 0:
                        modulations(m + j // 4 - 2, m + j // 4 - 1)
                    if j < 20:
                        if j % 4 == 0:
                            chunk_in(ph["at"][j // 4])
                        if j == 0:
                            pe.wait_ge(h_ready, norm_end[n])
                        tile_free(f"in{l}", j)
                        channel_tile(bank[:, j % 4, 0:S], weights(ph["at"][j // 4], CH), (j % 4) * P, h)
                        if j >= 8 and j < 14:
                            t = j - 8
                            pe.wait_ge(gemm_freed, ph["t0"] + t + 1)
                            if t >= 2:
                                pe.wait_ge(rope_done, 7 * l + t - 1)
                            nc.tensor.matmul(bank[:, 4 + t % 2, 0:S], const("rot"), raw[:, t, :], start=True, stop=True)\
                                .then_inc(rot_ready, 1)
                    else:
                        if j == 20:
                            chunk_in(ph["at"][5])
                        tile_free(f"in{l}", j)
                        token_tile(bank[:, j % 4, :], weights(ph["at"][5], CH), 0, CH, h, j - 20)
                modulations(m + 4, m + 5)
                chunk_in(phases[f"tok{l}"]["n0"])
                for qt in range(QT):
                    pe.wait_ge(gemm_freed, phases[f"tok{l}"]["t0"] + qt - 3)
                    token_tile(bank[:, (22 + qt) % 4, 0:TOKW], weights(phases[f"tok{l}"]["n0"], TOKW), 0, TOKW, h, qt)
                modulations(m + 5, m + 6)
                pe.wait_ge(xpe_ready, 2 * (l + 1))
                for kv in range(2):
                    nn = phases[f"cmp{l}"]["n0"] + kv
                    chunk_in(nn)
                    w = ring[:, nn % SLOTS, :].rearrange("p (k n) -> p k n", k=CMP_PAIRS)
                    for ht in range(2):
                        at = (2 * kv + ht) * 16
                        for k in range(CMP_PAIRS):
                            last = nc.tensor.matmul(bank[:, 7, at:at + N_CMP], w[:, k, ht * P:ht * P + P],
                                                    xpe[:, kv, k, :], start=(k == 0), stop=(k == CMP_PAIRS - 1))
                    last.then_inc(gemm_ready, 1)
                pe.wait_ge(hid_ready, l + 1)
                w2k = vec(l, "w2k").rearrange("p (a n) -> p a n", a=2)
                w2v = vec(l, "w2v").rearrange("p (a n) -> p a n", a=2)
                for ht in range(2):
                    nc.tensor.matmul(bank[:, 6, 0:N_CMP], w2k[:, ht, :], hid[:, 0, ht, :], start=(ht == 0), stop=(ht == 1))
                for ht in range(2):
                    last = nc.tensor.matmul(bank[0:N_CMP, 6, 64:64 + HD], hid[:, 1, ht, :], w2v[:, ht, :],
                                            start=(ht == 0), stop=(ht == 1))
                last.then_inc(kc_ps_ready, 1)
                pe.wait_ge(rope_done, 7 * (l + 1))
                pe.wait_ge(kc_ready, l + 1)
                pe.wait_ge(gemm_freed, phases[f"out{l}"]["t0"])
                attention(f"hybrid{l}", m + 6)
                delta_net(l)
                pe.wait_ge(gt_copied, 15 * (l + 1))
                projection(f"out{l}", mix, 0)
                norm_sums(n + 1)
                pe.wait_ge(h_ready, norm_end[n + 1])
                up(f"gu{l}")
                pe.wait_ge(gemm_freed, phases[f"dn{l}"]["t0"])
                down(f"dn{l}")
                n += 2
            norm_sums(n)
            n += 1
            for l, name in enumerate(("even", "odd")):
                norm_sums(n)
                pe.wait_ge(h_ready, norm_end[n])
                ph = phases[name]
                j = 0
                for nn in range(ph["chunks"]):
                    chunk_in(ph["n0"] + nn)
                    w = weights(ph["n0"] + nn, CH)
                    if nn in ((2, 5) if l == 0 else (4, 5)):
                        for qt in range(QT):
                            tile_free(name, j)
                            token_tile(bank[:, j % 4, :], w, 0, CH, h, qt)
                            j += 1
                    else:
                        for m in range(4):
                            tile_free(name, j)
                            channel_tile(bank[:, j % 4, 0:S], w, m * P, h)
                            j += 1
                if l == 0:
                    chunk_in(phases["tail"]["n0"])
                    w = weights(phases["tail"]["n0"], 144)
                    tile_free("tail", 0)
                    channel_tile(bank[:, 0, 0:S], w, 0, h)
                    for qt in range(QT):
                        token_tile(bank[:, 1 + qt, 0:16], w, P, P + 16, h, qt)
                    pe.wait_ge(ki_sq, 1)
                    nc.tensor.matmul(bank[:, 7, 0:S], const("halves"), tmp[:, 0, :], start=True, stop=True)\
                        .then_inc(ki_ssq, 1)
                    pe.wait_ge(ki_ready, 1)
                    pe.wait_ge(gemm_freed, phases["o0"]["t0"])
                    for i in range(QT * 4):
                        qt, g = i // 4, i % 4
                        if i >= 2:
                            pe.wait_ge(ix_relu, i - 1)
                        for s in range(NG):
                            r = LO if s < 2 else HI
                            last = nc.tensor.matmul(
                                bank[:, 2 * (i % 2) + s // 2, (s % 2) * S:(s % 2) * S + P * (qt + 1)],
                                qk2[r, 16 + 2 * g + s % 2, qt * P:qt * P + P], qk2[r, 24, 0:P * (qt + 1)],
                                start=True, stop=True)
                        last.then_inc(ix_ready, 1)
                    pe.wait_ge(ix_relu, QT * 4)
                else:
                    pe.wait_ge(gemm_freed, phases["o1"]["t0"])
                attention(name)
                pe.wait_ge(o_evac, evacs_before(stages[name][1]))
                projection(f"o{l}", mix, 0)
                norm_sums(n + 1)
                pe.wait_ge(h_ready, norm_end[n + 1])
                up(f"up{l}")
                pe.wait_ge(act_ready, FT * (l + 1) + 1)
                down(f"down{l}")
                n += 2
            norm_sums(n)

        @block.scalar
        def _(act):
            ch = Chain(act, act_chain)

            def norm_squares(n):
                for j in range(4):
                    if norm_input[n]:
                        act.wait_ge(gemm_freed, phases[norm_input[n]]["t0"] + 2 * j + 2)
                    elif n:
                        act.wait_ge(x_ready, 2 * j + 2)
                    nc.scalar.activation(h[:, 2 * j:2 * j + 2, :], x[:, 2 * j:2 * j + 2, :], ACT.Square)\
                        .then_inc(sq_ready, 1)
                act.wait_ge(ssq_ready, n + 1)
                nc.scalar.activation(std[:, :], bank[:, 7, 0:S], ACT.Sqrt, bias=const("eps"), scale=1.0 / D)\
                    .then_inc(std_ready, 1)

            def norm_shift(n, l, part):
                for k in range(KT):
                    act.wait_ge(hn_ready, KT * n + k + 1)
                    col = 24 * part + k
                    nc.scalar.activation(h[:, k, :], h[:, k, :], ACT.Identity, bias=mod[:, l, col:col + 1])\
                        .then_inc(h_ready, 1)

            def take(e, dst, src, func=ACT.Copy):
                act.wait_ge(gemm_ready, e + 1)
                nc.scalar.activation(dst, src, func).then_inc(gemm_freed, 1)

            def attention(name):
                u0, u1 = stages[name]

                def exps(u):
                    U, b = units[u], u % DEPTH
                    act.wait_ge(logits_done, u + 1)
                    for s in range(NG):
                        last = nc.scalar.activation(lg[:, b, s, 0:U["w"]], lg[:, b, s, 0:U["w"]], ACT.Exp,
                                                    bias=negm[:, b, s:s + 1], accum_out=sums[:, b, s:s + 1])
                    if U["sink"] is not None:
                        last = nc.scalar.activation(esink[:, b, :], esink[:, b, :], ACT.Exp)
                    last.then_inc(exps_done, 1)

                def copy_pt(u):
                    act.wait_ge(trans_ready, u + 1)
                    if u >= 2:
                        act.wait_ge(pv_done, u - 1)
                    for kt, m in key_tiles(u):
                        last = nc.scalar.activation(pT[0:m, u % 2, kt, :], bank[0:m, 4 + kt, :], ACT.Copy)
                    last.then_inc(pt_ready, 1)

                exps(u0)
                exps(u0 + 1)
                for u in range(u0, u1):
                    if u + 2 < u1:
                        exps(u + 2)
                    copy_pt(u)

            def delta_net(l):
                g0 = 15 * l

                def group(j, dst):
                    act.wait_ge(gt_ready, g0 + j + 1)
                    nc.scalar.activation(dst, bank[:, j % 4, :].rearrange("p (a n) -> p a n", a=4), ACT.Copy)\
                        .then_inc(gt_copied, 1)

                for j in range(6):
                    group(j, tok[:, j // 2, GH * (j % 2):GH * (j % 2) + GH, :])
                act.wait_ge(g_arg, 5 * l + 1)
                nc.scalar.activation(small[:, 64:64 + NCH], small[:, 64:64 + NCH], ACT.Exp)
                nc.scalar.activation(small[:, 88:92], vec(l, "a_log"), ACT.Exp).then_inc(g_fun, 1)
                act.wait_ge(g_arg, 5 * l + 2)
                nc.scalar.activation(small[:, 64:64 + NCH], small[:, 64:64 + NCH], ACT.Ln).then_inc(g_fun, 1)
                act.wait_ge(g_arg, 5 * l + 3)
                nc.scalar.activation(small[:, 128:144], small[:, 128:144], ACT.Sqrt, bias=const("eps")).then_inc(g_fun, 1)
                act.wait_ge(g_arg, 5 * l + 4)
                nc.scalar.activation(Dm, Dm, ACT.Exp)
                nc.scalar.activation(small[:, 112:112 + NCH], small[:, 104:104 + NCH], ACT.Exp)
                nc.scalar.activation(small[:, 120:120 + NCH], small[:, 120:120 + NCH], ACT.Exp).then_inc(g_fun, 1)
                for cc in range(2):
                    group(6 + cc, kbqT[:, GH * cc:GH * cc + GH, 0, :])
                for cc in range(2):
                    group(8 + cc, knT[:, GH * cc:GH * cc + GH, :])
                for cc in range(2):
                    group(10 + cc, kbqT[:, GH * cc:GH * cc + GH, 1, :])
                group(12, qdT)
                for lv in range(1, LEVELS):
                    for half in range(2):
                        act.wait_ge(t1_ready, l * 2 * LEVELS + 2 * lv + half + 1)
                        nc.scalar.activation(T1[:, 4 * half:4 * half + 4, :],
                                             bank[:, half, :].rearrange("p (a n) -> p a n", a=4), ACT.Copy)\
                            .then_inc(t1_copied, 1)
                act.wait_ge(u_ready, l + 1)
                for half in range(2):
                    nc.scalar.activation(U[:, 4 * half:4 * half + 4, :],
                                         bank[:, half, :].rearrange("p (a n) -> p a n", a=4), ACT.Copy)
                nc.scalar.activation(wT, bank[:, 2, :].rearrange("p (a n) -> p a n", a=4), ACT.Copy).then_inc(u_copied, 1)
                act.wait_ge(state_ready, l + 1)
                nc.scalar.activation(st, bank[:, 3, :].rearrange("p (a n) -> p a n", a=4), ACT.Copy)\
                    .then_inc(state_copied, 1)
                for cc in range(2):
                    act.wait_ge(o_ready, 2 * l + cc + 1)
                    nc.scalar.activation(sq_tok[:, GH * cc:GH * cc + GH, :],
                                         bank[:, 4 + 2 * cc, :].rearrange("p (a n) -> p a n", a=4), ACT.Square)\
                        .then_inc(osq_ready, 1)
                act.wait_ge(g_arg, 5 * l + 5)
                nc.scalar.activation(small[:, 152:160], small[:, 144:152], ACT.Sqrt, bias=const("eps"), scale=1.0 / GD)\
                    .then_inc(g_fun, 1)
                for cc in range(2):
                    group(13 + cc, mix[:, 4:8, cc * P:cc * P + P])

            act.wait_ge(c_loaded, 16)
            nc.scalar.activation(c_silu[:, :], c_in[:, :], ACT.Silu).then_inc(c_ready, 1)
            act.wait_ge(consts_in, 16 * 6)
            act.wait_ge(tab_ready, 1)
            for a in range(2):
                nc.scalar.activation(tab_rows[:, a, :], bank[0:16, a, 0:BIAS_W], ACT.Copy).then_inc(tab_copied, 1)
            act.wait_ge(tab_copied, 2)
            act.dma_start(bias_dram.rearrange("a h d -> h a d"), tab_rows[:, :, :]).then_inc(tab_out, 16)
            n = 0
            for l in range(L1):
                norm_squares(n)
                if l == 0:
                    act.wait_ge(tab_out, 16)
                norm_shift(n, l, 0)
                e0 = phases[f"in{l}"]["e0"]
                for j in range(8):
                    take(e0 + j, raw[:, j, :], bank[:, j % 4, 0:S])
                for part in range(4):
                    if part < 3:
                        for j in range(4 * part, 4 * part + 4):
                            take(e0 + 8 + j, conv_in[:, j, 3:3 + S], bank[:, j % 4, 0:S])
                    if part >= 1:
                        act.wait_ge(conv_ready, 3 * l + part)
                        nc.scalar.activation(conv[:, 4 * part - 4:4 * part, :], conv[:, 4 * part - 4:4 * part, :], ACT.Silu)\
                            .then_inc(silu_ready, 1)
                for qt in range(QT):
                    take(e0 + 20 + qt, z[:, qt, :], bank[:, qt, :], ACT.Silu)
                for qt in range(QT):
                    take(phases[f"tok{l}"]["e0"] + qt, tokp[:, qt, :], bank[:, 2 + qt, 0:TOKW])
                act.wait_ge(gemm_freed, phases[f"out{l}"]["t0"])
                for qt in range(QT):
                    nc.scalar.activation(small[:, 16 * qt:16 * qt + 12], tokp[:, qt, GATES:GATES + 12], ACT.Exp, scale=-1.0)
                    last = nc.scalar.activation(small[:, 16 * qt + 12:16 * qt + 16], tokp[:, qt, B_COL:B_COL + 4],
                                                ACT.Exp, scale=-1.0)
                last.then_inc(gate_exp, 1)
                act.wait_ge(gemm_ready, phases[f"cmp{l}"]["e0"] + 2)
                nc.scalar.activation(hid[:, :, :, :].rearrange("p a b n -> p (a b) n"),
                                     bank[:, 7, 0:64].rearrange("p (a n) -> p a n", a=4)[:, :, 0:N_CMP], ACT.Silu)\
                    .then_inc(hid_ready, 1)
                act.wait_ge(kc_ps_ready, l + 1)
                nc.scalar.activation(kcT[:, :], bank[:, 6, 0:N_CMP], ACT.Copy)
                nc.scalar.activation(vc[:, :], bank[0:N_CMP, 6, 64:64 + HD], ACT.Copy).then_inc(kc_ready, 1)
                attention(f"hybrid{l}")
                delta_net(l)
                norm_squares(n + 1)
                norm_shift(n + 1, l, 1)
                ph = phases[f"gu{l}"]
                with act.Fori(0, 11) as i:
                    for b in range(2):
                        act.wait_ge(gemm_ready, i * 4 + ph["e0"] + 2 * b + 1)
                        act.wait_ge(gemm_freed, i * 4 + ph["t0"] + 2 * b - 2)
                        nc.scalar.activation(sg[:, b, :], bank[:, 2 * b, 0:S], ACT.Silu).then_inc(sg_ready, 1)
                n += 2
            norm_squares(n)
            n += 1
            for l, name in enumerate(("even", "odd")):
                norm_squares(n)
                e = phases[name]["e0"]
                t = 0
                j = 0
                for nn in range(phases[name]["chunks"]):
                    if nn in ((2, 5) if l == 0 else (4, 5)):
                        half = 0 if nn in (2, 4) else 1
                        for qt in range(QT):
                            take(e + j, vv2[:, qt, CH * half:CH * half + CH], bank[:, j % 4, :])
                            j += 1
                    else:
                        for m in range(4):
                            take(e + j, qk2[:, t, :], bank[:, j % 4, 0:S])
                            t += 1
                            j += 1
                if l == 0:
                    e = phases["tail"]["e0"]
                    take(e, qk2[:, 24, :], bank[:, 0, 0:S])
                    for qt in range(QT):
                        take(e + 1 + qt, wi[:, qt, :], bank[:, 1 + qt, 0:16])
                    act.wait_ge(gemm_freed, phases["o0"]["t0"])
                    nc.scalar.activation(tmp[:, 0, :], qk2[:, 24, :], ACT.Square).then_inc(ki_sq, 1)
                    act.wait_ge(ki_ssq, 1)
                    nc.scalar.activation(std[:, :], bank[:, 7, 0:S], ACT.Sqrt, bias=const("eps"), scale=1.0 / HD)\
                        .then_inc(ki_std, 1)
                    for i in range(QT * 4):
                        w = P * (i // 4 + 1)
                        act.wait_ge(ix_ready, i + 1)
                        if i >= 2:
                            act.wait_ge(ix_acc, i - 1)
                        nc.scalar.activation(
                            rel[:, i % 2, :, 0:w],
                            bank[:, 2 * (i % 2):2 * (i % 2) + 2, :].rearrange("p b (s n) -> p (b s) n", s=2)[:, :, 0:w],
                            ACT.Relu, scale=HD ** -0.5).then_inc(ix_relu, 1)
                attention(name)
                norm_squares(n + 1)
                ph = phases[f"up{l}"]
                cw = vec_b(l, "conv_w").rearrange("p (j t) -> p j t", j=3)
                cb = vec_b(l, "conv_b")
                with act.Fori(0, 11) as i:
                    for b in range(2):
                        act.wait_ge(gemm_ready, i * 4 + ph["e0"] + 2 * b + 2)
                        act.wait_ge(act_ready, i * 2 + FT * l + 1)
                        for half in range(2):
                            last = nc.scalar.activation(cv[:, b, half, :], bank[:, 2 * b + half, 0:S], ACT.Identity,
                                                        bias=cb[:, bass.ds(i * 4 + 2 * b + half, 1)],
                                                        scale=cw[:, 2, bass.ds(i * 4 + 2 * b + half, 1)])
                        last.then_inc(cv_ready, 1)
                    for b in range(2):
                        act.wait_ge(gemm_freed, i * 4 + ph["t0"] + 2 * b + 2)
                        nc.scalar.activation(sg[:, b, :], cv[:, b, 1, :], ACT.Silu).then_inc(sg_ready, 1)
                n += 2
            norm_squares(n)

        @block.vector
        def _(dve):
            V = nc.vector
            ch = Chain(dve, dve_chain)

            def normalise(n, scale, out, sig):
                dve.wait_ge(std_ready, n + 1)
                ch(V.reciprocal(rstd[:, :], std[:, :]))
                for k in range(KT):
                    V.scalar_tensor_tensor(out=out[:, k, :], in0=x[:, k, :], scalar=scale[:, k:k + 1], in1=rstd[:, :],
                                           op0=ALU.mult, op1=ALU.mult).then_inc(sig, 1)

            def attention(name):
                u0, u1 = stages[name]

                def logits(u):
                    U, b, w = units[u], u % DEPTH, units[u]["w"]
                    dve.wait_ge(scores_ready, u + 1)
                    if u >= DEPTH:
                        dve.wait_ge(trans_ready, u - DEPTH + 1)
                    s_ps = bank[:, 2 * (u % 2):2 * (u % 2) + 2, :].rearrange("p b (s n) -> p (b s) n", s=2)[:, :, 0:w]
                    out = lg[:, b, :, 0:w]
                    ch(V.scalar_tensor_tensor(out=out, in0=s_ps, scalar=SCALE, in1=U["bias"], op0=ALU.mult, op1=ALU.add))
                    if U.get("sel") is not None:
                        ch(V.tensor_tensor(out, out, U["sel"], ALU.add))
                    red = V.tensor_reduce(out=negm[:, b, :], in_=out, op=ALU.max, axis=AX.X, negate=True)
                    if U["sink"] is not None:
                        ch(red)
                        ch(V.scalar_tensor_tensor(out=negm[:, b, :], in0=U["sink"], scalar=-1.0, in1=negm[:, b, :],
                                                  op0=ALU.mult, op1=ALU.min))
                        red = V.tensor_tensor(esink[:, b, :], U["sink"], negm[:, b, :], ALU.add)
                    red.then_inc(logits_done, 1)

                def recip(u):
                    U, b = units[u], u % DEPTH
                    dve.wait_ge(exps_done, u + 1)
                    if U["sink"] is not None:
                        ch(V.tensor_tensor(sums[:, b, :], sums[:, b, :], esink[:, b, :], ALU.add))
                    r = V.reciprocal(rec[:, b, :], sums[:, b, :])
                    if U["gate"] is not None:
                        ch(r)
                        r = V.tensor_tensor(rec[:, b, :], rec[:, b, :], U["gate"], ALU.mult)
                    r.then_inc(rec_ready, 1)

                def evac(u):
                    U = units[u]
                    if not U["end"]:
                        return
                    dve.wait_ge(pv_done, u + 1)
                    for s, rows, tile in U["evac"]:
                        last = V.tensor_copy(mix[rows, tile, U["qs"]], bank[0:HD, 6, s * P:s * P + P])
                    last.then_inc(o_evac, 1)

                logits(u0)
                logits(u0 + 1)
                for u in range(u0, u1 + 1):
                    if u + 2 < u1:
                        logits(u + 2)
                    if u < u1:
                        recip(u)
                    if u > u0:
                        evac(u - 1)

            def delta_net(l):
                a = small[:, 64:64 + NCH]
                relu = small[:, 72:72 + NCH]
                ea, g, gc = small[:, 88:92], small[:, 96:96 + NCH], small[:, 104:104 + NCH]
                eg, ekd = small[:, 112:112 + NCH], small[:, 120:120 + NCH]
                rqk = small[:, 128:144]
                beta = small[:, 160:160 + NCH]
                a3 = a.rearrange("p (c h) -> p c h", c=QT)
                ch(V.tensor_tensor(a3, tokp[:, :, A_COL:A_COL + 4], over(vec(l, "dt"), QT), ALU.add))
                ch(V.tensor_scalar(relu, a, 0.0, None, ALU.max))
                ch(V.scalar_tensor_tensor(out=small[:, 80:88], in0=a, scalar=-1.0, in1=a, op0=ALU.mult, op1=ALU.min))
                V.tensor_copy(a, small[:, 80:88]).then_inc(g_arg, 1)
                ch(V.tensor_copy(beta.rearrange("p (c h) -> p c h", c=QT),
                                 small[:, 0:32].rearrange("p (c n) -> p c n", c=QT)[:, :, 12:16]))
                dve.wait_ge(g_fun, 5 * l + 1)
                V.tensor_scalar(a, a, 1.0, None, ALU.add).then_inc(g_arg, 1)
                dve.wait_ge(g_fun, 5 * l + 2)
                ch(V.tensor_tensor(relu, relu, a, ALU.add))
                ch(V.scalar_tensor_tensor(out=g.rearrange("p (c h) -> p c h", c=QT),
                                          in0=relu.rearrange("p (c h) -> p c h", c=QT), scalar=-1.0, in1=over(ea, QT),
                                          op0=ALU.mult, op1=ALU.mult))
                V.tensor_copy(gB, along(g, P)).then_inc(g_ready, 1)
                dve.wait_ge(gt_copied, 15 * l + 4)
                for qk in range(2):
                    ch(V.tensor_tensor(sq_tok, tok[:, qk], tok[:, qk], ALU.mult))
                    last = V.tensor_reduce(out=rqk[:, NCH * qk:NCH * qk + NCH], in_=sq_tok, op=ALU.add, axis=AX.X)
                    ch(last)
                V.tensor_copy(rqk, rqk).then_inc(g_arg, 1)
                dve.wait_ge(gc_ready, l + 1)
                ch(V.tensor_copy(gc, bank[:, 6, 0:NCH]))
                for i in range(NCH):
                    ch.mark(V.tensor_scalar(Dm[:, i, :], bank[:, 4 + i // 4, (i % 4) * P:(i % 4) * P + P],
                                            gc[:, i:i + 1], 0.0, ALU.subtract, ALU.min))
                for cc in range(2):
                    last = V.tensor_tensor(
                        ekd[:, 4 * cc:4 * cc + 4],
                        bank[:, 4 + cc, :].rearrange("p (a n) -> p a n", a=4)[:, :, P - 1], gc[:, 4 * cc:4 * cc + 4],
                        ALU.subtract)
                    ch.mark(last)
                ch.wait()
                V.tensor_copy(ekd, ekd).then_inc(g_arg, 1)
                dve.wait_ge(g_fun, 5 * l + 3)
                ch(V.reciprocal(rqk, rqk))
                ch(V.tensor_scalar(rqk[:, 0:NCH], rqk[:, 0:NCH], GD ** -0.5, None, ALU.mult))
                dve.wait_ge(gt_copied, 15 * l + 6)
                ch.mark(V.tensor_tensor(qn, tok[:, 0], along(rqk[:, 0:NCH], GD), ALU.mult))
                ch.mark(V.tensor_tensor(kn, tok[:, 1], along(rqk[:, NCH:2 * NCH], GD), ALU.mult))
                ch(V.tensor_tensor(vb, tok[:, 2], along(beta, GD), ALU.mult))
                ch(V.tensor_tensor(kb, kn, along(beta, GD), ALU.mult))
                dve.wait_ge(g_fun, 5 * l + 4)
                ch.mark(V.tensor_tensor(Dm, Dm, over(upper, NCH), ALU.mult))
                ch.mark(V.tensor_tensor(kbg, kb[:, GH:NCH], along(eg[:, GH:NCH], GD), ALU.mult))
                ch.mark(V.tensor_tensor(kd, kn[:, 0:GH], along(ekd[:, 0:GH], GD), ALU.mult))
                V.tensor_tensor(qd, qn[:, GH:NCH], along(eg[:, GH:NCH], GD), ALU.mult).then_inc(scaled, 1)
                ch.wait()
                for b in range(4):
                    dve.wait_ge(kq_ready, 4 * l + b + 1)
                    ps = bank[:, KQ_BANKS[b], :].rearrange("p (i a n) -> p i a n", i=2, a=2)
                    ch.mark(V.tensor_tensor(MT[:, 2 * b:2 * b + 2], ps[:, :, 0, :], Dm[:, 2 * b:2 * b + 2], ALU.mult))
                    ch.mark(V.tensor_tensor(QKT[:, 2 * b:2 * b + 2], ps[:, :, 1, :], Dm[:, 2 * b:2 * b + 2], ALU.mult))
                ch.wait()
                V.tensor_tensor(MT, MT, over(const("strict"), NCH), ALU.mult).then_inc(mt_ready, 1)
                for lv in range(LEVELS):
                    for half in range(2):
                        hs = slice(4 * half, 4 * half + 4)
                        if lv == 0:
                            dve.wait_ge(mb_ready, l * LEVELS + 1)
                            dve.wait_ge(t1_ready, l * 2 * LEVELS + half + 1)
                            ps = bank[:, half, :].rearrange("p (a n) -> p a n", a=4)
                            V.tensor_tensor(X[:, hs], over(ident, 4), ps, ALU.subtract)
                            V.tensor_tensor(XT[:, hs], over(ident, 4), MbT[:, 0, hs], ALU.subtract).then_inc(x_upd, 1)
                        else:
                            dve.wait_ge(dx_ready, l * 2 * (LEVELS - 1) + 2 * (lv - 1) + half + 1)
                            if lv < LEVELS - 1:
                                ps = bank[:, 2 + half, :].rearrange("p (a n) -> p a n", a=4)
                                V.tensor_tensor(X[:, hs], X[:, hs], ps, ALU.subtract)
                            ps = bank[:, 4 + half, :].rearrange("p (a n) -> p a n", a=4)
                            V.tensor_tensor(XT[:, hs], XT[:, hs], ps, ALU.subtract).then_inc(x_upd, 1)
                dve.wait_ge(u_copied, l + 1)
                dve.wait_ge(ws_ready, l + 1)
                V.tensor_tensor(U[:, GH:NCH], U[:, GH:NCH], bank[:, 5, :].rearrange("p (a n) -> p a n", a=4), ALU.subtract)\
                    .then_inc(vnew_ready, 1)
                dve.wait_ge(osq_ready, 2 * (l + 1))
                V.tensor_reduce(out=small[:, 144:152], in_=sq_tok, op=ALU.add, axis=AX.X).then_inc(g_arg, 1)
                dve.wait_ge(g_fun, 5 * l + 5)
                ch(V.reciprocal(small[:, 152:160], small[:, 152:160]))
                for cc in range(2):
                    cs = slice(GH * cc, GH * cc + GH)
                    ps = bank[:, 4 + 2 * cc, :].rearrange("p (a n) -> p a n", a=4)
                    ch.mark(V.tensor_tensor(o_n[:, cs], ps, along(small[:, 152 + GH * cc:156 + GH * cc], GD), ALU.mult))
                ch.wait()
                ch(V.tensor_tensor(o_n, o_n, over(vec(l, "gnorm"), NCH), ALU.mult))
                V.tensor_tensor(o_n, o_n, z.rearrange("p c (h n) -> p (c h) n", h=GH), ALU.mult).then_inc(on_ready, 1)

            def residual(name, gate):
                ph = phases[name]
                for k in range(KT):
                    if name == "dn0" and k < ADA_FIRST:
                        weigh(ADA_L + k)
                    if name == "dn0" and k == ADA_FIRST + 1:
                        dve.wait_ge(mod_ready, ADA_L + ADA_FIRST)
                        modulation(1, 0, ADA_FIRST)
                        norm_gain(1, 0).then_inc(mod_read, 1)
                        dve.wait_ge(mod_read, 2)
                    dve.wait_ge(gemm_ready, ph["e0"] + k + 1)
                    ps = bank[:, k % 4, 0:S]
                    if gate is None:
                        ins = V.tensor_tensor(x[:, k, :], x[:, k, :], ps, ALU.add)
                    else:
                        ins = V.scalar_tensor_tensor(out=x[:, k, :], in0=ps, scalar=gate[:, k:k + 1], in1=x[:, k, :],
                                                     op0=ALU.mult, op1=ALU.add)
                    ins.then_inc(gemm_freed, 1)

            def weigh(m):
                at = ada_at[m]
                dve.wait_ge(slot_in[at % SLOTS], 16 * (at // SLOTS + 1))
                if m >= 2:
                    dve.wait_ge(mod_ready, m - 1)
                w = ring[:, at % SLOTS, :].rearrange("p (k n) -> p k n", k=KT)
                out = acc[:, m % 2, :]
                ch(V.tensor_scalar(out, w[:, 0, :], c_silu[:, 0:1], None, ALU.mult))
                for k in range(1, KT):
                    ins = V.scalar_tensor_tensor(out=out, in0=w[:, k, :], scalar=c_silu[:, k:k + 1], in1=out,
                                                 op0=ALU.mult, op1=ALU.add)
                    if k < KT - 1:
                        ch(ins)
                ins.then_inc(acc_ready, 1)

            def modulation(l, m0, m1):
                at = MOD_COL + 4 * ADA_L * l
                ch(V.tensor_tensor(mod[:, l, 4 * m0:4 * m1], bank[:, 7, at + 4 * m0:at + 4 * m1],
                                   vec(l, "ada_b")[:, 4 * m0:4 * m1], ALU.add))

            def norm_gain(l, part):
                return V.scalar_tensor_tensor(out=gain[:, l, part, :], in0=mod[:, l, 24 * part + 8:24 * part + 16],
                                              scalar=1.0, in1=vec(l, ("norm_mix", "norm_ffn")[part]),
                                              op0=ALU.add, op1=ALU.mult)

            V.memset(conv_in[:, :, 0:3], 0.0).then_inc(act_ready, 1)
            dve.wait_ge(act_ready, 1)
            dve.wait_ge(c_ready, 1)
            for m in range(ADA_FIRST):
                weigh(m)
            n = 0
            for l in range(L1):
                if l:
                    ch(V.memset(conv_in[:, :, 0:3], 0.0))
                if l == 0:
                    dve.wait_ge(consts_in, 16 * 6)
                    dve.wait_ge(mod_ready, ADA_FIRST)
                    modulation(0, 0, ADA_FIRST)
                    norm_gain(0, 0).then_inc(mod_read, 1)
                    dve.wait_ge(mod_read, 1)
                normalise(n, gain[:, l, 0, :], h, hn_ready)
                m = ADA_L * l + ADA_FIRST
                weigh(m)
                t0 = phases[f"in{l}"]["t0"]
                for t in range(6):
                    if t in (0, 3):
                        weigh(m + 1 + t // 3)
                    dve.wait_ge(gemm_freed, t0 + t + 1)
                    dve.wait_ge(rot_ready, 6 * l + t + 1)
                    ch.mark(V.tensor_tensor(tmp[:, 0, :], raw[:, t, :], const("cos"), ALU.mult))
                    ch(V.tensor_tensor(tmp[:, 1, :], bank[:, 4 + t % 2, 0:S], const("sin"), ALU.mult))
                    V.tensor_tensor(rot[:, t, :], tmp[:, 0, :], tmp[:, 1, :], ALU.add).then_inc(rope_done, 1)
                    dve.wait_ge(rope_done, 7 * l + t + 1)
                V.tensor_copy(rot[LO, 6, :], rot[HI, 5, :])
                V.tensor_copy(rot[HI, 6, :], rot[LO, 5, :]).then_inc(rope_done, 1)
                dve.wait_ge(gemm_freed, t0 + 8)
                for kv, pe_name in enumerate(("pe_k", "pe_v")):
                    for two, rows in enumerate((LO, HI)):
                        base = raw[rows, 6 + kv, :].rearrange("p (n q a) -> p a q n", q=8, a=2)[:, two]
                        for hf in range(2):
                            last = V.tensor_tensor(
                                xpe[rows, kv, 8 * hf:8 * hf + 8, :], base[:, :, hf:hf + N_CMP],
                                along(vec(l, pe_name)[rows, 8 * hf:8 * hf + 8], N_CMP), ALU.add)
                    last.then_inc(xpe_ready, 1)
                cw = vec(l, "conv").rearrange("p (j t) -> p j t", j=4)
                for part in range(3):
                    weigh(m + 3 + part)
                    dve.wait_ge(gemm_freed, t0 + 8 + 4 * part + 4)
                    for tap in range(4):
                        if tap:
                            ch.wait()
                        for t in range(4 * part, 4 * part + 4):
                            src, wt = conv_in[:, t, tap:tap + S], cw[:, tap, t:t + 1]
                            if tap == 0:
                                ins = V.tensor_scalar(conv[:, t, :], src, wt, None, ALU.mult)
                            else:
                                ins = V.scalar_tensor_tensor(out=conv[:, t, :], in0=src, scalar=wt, in1=conv[:, t, :],
                                                             op0=ALU.mult, op1=ALU.add)
                            if tap == 3 and t % 4 == 3:
                                ins.then_inc(conv_ready, 1)
                            else:
                                ch.mark(ins)
                weigh(m + 6)
                dve.wait_ge(gate_exp, l + 1)
                ch(V.tensor_scalar(small[:, 0:32], small[:, 0:32], 1.0, None, ALU.add))
                ch(V.reciprocal(small[:, 0:32], small[:, 0:32]))
                weigh(m + 7)
                attention(f"hybrid{l}")
                delta_net(l)
                dve.wait_ge(mod_ready, ADA_L * (l + 1))
                modulation(l, ADA_FIRST, ADA_L)
                ch(norm_gain(l, 1))
                residual(f"out{l}", mod[:, l, 16:24])
                normalise(n + 1, gain[:, l, 1, :], h, hn_ready)
                ph = phases[f"gu{l}"]
                with dve.Fori(0, 11) as i:
                    for b in range(2):
                        dve.wait_ge(sg_ready, i * 2 + FT * l + b + 1)
                        dve.wait_ge(gemm_ready, i * 4 + ph["e0"] + 2 * b + 2)
                        V.tensor_tensor(act_T[:, bass.ds(i * 2 + b, 1), :],
                                        sg[:, b, :].rearrange("p (a n) -> p a n", a=1),
                                        bank[:, 2 * b + 1, 0:S].rearrange("p (a n) -> p a n", a=1), ALU.mult)\
                            .then_inc(gemm_freed, 2)
                residual(f"dn{l}", mod[:, l, 40:48])
                n += 2
            normalise(n, const("final1"), x, x_ready)
            n += 1
            for l, name in enumerate(("even", "odd")):
                normalise(n, vec_b(l, "norm_attn"), h, h_ready)
                if l == 0:
                    dve.wait_ge(ki_std, 1)
                    ch(V.reciprocal(rstd[:, :], std[:, :]))
                    V.scalar_tensor_tensor(out=qk2[:, 24, :], in0=qk2[:, 24, :], scalar=const("knorm"), in1=rstd[:, :],
                                           op0=ALU.mult, op1=ALU.mult).then_inc(ki_ready, 1)
                    ch(V.tensor_scalar(wi, wi, 16 ** -0.5, None, ALU.mult))
                    for i in range(QT * 4):
                        qt, g, w = i // 4, i % 4, P * (i // 4 + 1)
                        dve.wait_ge(ix_relu, i + 1)
                        for s in range(NG):
                            col = wi[:, qt, NG * g + s:NG * g + s + 1]
                            src = rel[:, i % 2, s, 0:w]
                            if g == 0 and s == 0:
                                ins = V.tensor_scalar(score[:, qt, 0:w], src, col, None, ALU.mult)
                            else:
                                ins = V.scalar_tensor_tensor(out=score[:, qt, 0:w], in0=src, scalar=col,
                                                             in1=score[:, qt, 0:w], op0=ALU.mult, op1=ALU.add)
                            if s == NG - 1:
                                ins.then_inc(ix_acc, 1)
                                dve.wait_ge(ix_acc, i + 1)
                            else:
                                ch(ins)
                        if g == 3:
                            mask = const("causal0") if qt == 0 else const("causal1")
                            ch(V.tensor_tensor(work[:, 0, 0:w], score[:, qt, 0:w], mask, ALU.add))
                            for r in range(8):
                                ch(V.max(max8, work[:, r % 2, 0:w]))
                                ch(V.match_replace(work[:, (r + 1) % 2, 0:w], max8, work[:, r % 2, 0:w], -3e38))
                            ch(V.tensor_scalar(selm[:, qt, 0:w], work[:, 0, 0:w], -2e38, NEG, ALU.is_gt, ALU.mult))
                    dve.wait_ge(bias_in, 32)
                attention(name)
                residual(f"o{l}", None)
                normalise(n + 1, vec_b(l, "norm_ffn"), h, h_ready)
                ph = phases[f"up{l}"]
                cw = vec_b(l, "conv_w").rearrange("p (j t) -> p j t", j=3)
                with dve.Fori(0, 11) as i:
                    for b in range(2):
                        dve.wait_ge(cv_ready, i * 2 + FT * l + b + 1)
                        for half in range(2):
                            V.scalar_tensor_tensor(out=cv[:, b, half, 1:S], in0=bank[:, 2 * b + half, 0:S - 1],
                                                   scalar=cw[:, 1, bass.ds(i * 4 + 2 * b + half, 1)],
                                                   in1=cv[:, b, half, 1:S], op0=ALU.mult, op1=ALU.add)\
                                .then_inc(tap_done, 1)
                        for half in range(2):
                            dve.wait_ge(tap_done, i * 4 + 2 * FT * l + 2 * b + half + 1)
                            V.scalar_tensor_tensor(out=cv[:, b, half, 2:S], in0=bank[:, 2 * b + half, 0:S - 2],
                                                   scalar=cw[:, 0, bass.ds(i * 4 + 2 * b + half, 1)],
                                                   in1=cv[:, b, half, 2:S], op0=ALU.mult, op1=ALU.add)\
                                .then_inc(gemm_freed, 1)
                    for b in range(2):
                        dve.wait_ge(sg_ready, i * 2 + FT * (L1 + l) + b + 1)
                        dve.wait_ge(gemm_freed, i * 4 + ph["t0"] + 2 * b + 2)
                        V.tensor_tensor(act_T[:, bass.ds(i * 2 + b, 1), :],
                                        sg[:, b, :].rearrange("p (a n) -> p a n", a=1),
                                        cv[:, b, 0, :].rearrange("p (a n) -> p a n", a=1), ALU.mult)\
                            .then_inc(act_ready, 1)
                residual(f"down{l}", None)
                n += 2
            normalise(n, const("final2"), h, h_ready)

        @block.gpsimd
        def _(pool):
            ch = Chain(pool, pool_chain)
            G = nc.gpsimd

            def attention(name):
                u0, u1 = stages[name]
                for u in range(u0, u1):
                    U, b, w = units[u], u % DEPTH, units[u]["w"]
                    pool.wait_ge(rec_ready, u + 1)
                    out = lg[:, b, :, 0:w]
                    ins = G.tensor_tensor(out, out, along(rec[:, b, :], w), ALU.mult)
                    if U.get("valid") is not None:
                        ch(ins)
                        ins = G.tensor_tensor(out, out, U["valid"], ALU.mult)
                    ins.then_inc(probs_ready, 1)

            for l in range(L1):
                attention(f"hybrid{l}")
                pool.wait_ge(mt_ready, l + 1)
                for lv in range(LEVELS):
                    if lv >= 2:
                        pool.wait_ge(x_upd, l * 2 * LEVELS + 2 * (lv - 1))
                    lm = const("levels")[:, lv * P:lv * P + P]
                    G.tensor_tensor(MbT[:, lv % 2], MT, over(lm, NCH), ALU.mult).then_inc(mb_ready, 1)
            for name in ("even", "odd"):
                attention(name)


def shape_constants():
    import numpy as np

    f = np.float32
    i, j = np.arange(P)[:, None], np.arange(P)[None, :]
    parts = {}
    inv = (f(1) / (f(10000.0) ** (np.arange(0, HD, 2, dtype=f) / f(HD)))).astype(f)
    ang = (np.arange(S, dtype=f)[:, None] * inv[None, :]).astype(f)
    parts["cos"] = np.tile(np.cos(ang).T, (4, 1))
    parts["sin"] = np.tile(np.sin(ang).T, (4, 1))
    parts["ident"] = i == j
    parts["rot"] = (j % HD >= HD // 2) * (i == j - HD // 2) * 1.0 - (j % HD < HD // 2) * (i == j + HD // 2) * 1.0
    parts["ones"] = np.ones((P, P))
    parts["halves"] = i // HD == j // HD
    parts["upper"] = i <= j
    parts["strict"] = i < j
    parts["levels"] = np.concatenate([(i // (2 * b) == j // (2 * b)) & (i // b % 2 == 0) & (j // b % 2 == 1)
                                      for b in (1 << n for n in range(LEVELS))], axis=1)
    k = np.arange(S)[None, :]
    parts["causal0"] = np.where(j <= i, 0.0, NEG)
    parts["band1"] = np.where((k <= i + P) & (k > i), 0.0, NEG)
    parts["causal1"] = np.where(k <= i + P, 0.0, NEG)
    end = np.arange(N_CMP)[None, :] * 16 + 31
    ok = np.concatenate([end <= i + P * qt for qt in range(QT)], axis=1)
    parts["cmp_mask"] = np.where(ok, 0.0, NEG)
    parts["cmp_valid"] = ok
    parts["eps"] = np.full((P, 1), EPS)
    d = S - 1 - np.arange(BIAS_W)
    n = np.maximum(d, 0)
    nf = np.maximum(n, 16).astype(f)
    large = 16 + (np.log(nf / f(16)) / f(np.log(8.0)) * f(16)).astype(np.int32)
    bucket = np.where(n < 16, n, np.minimum(large, 31))
    dist = np.zeros((33, 2, BIAS_W), f)
    seen = d >= 0
    for a in range(2):
        dist[bucket[seen], a, np.nonzero(seen)[0]] = 1.0
    dist[32, 0] = np.where(seen, 0.0, NEG)
    times = ((d <= 128) * 1 + (d % 4 == 0) + (d % 16 == 0)) * seen
    dist[32, 1] = np.where(times > 0, np.log(np.maximum(times, 1)), NEG)
    return parts, dist


def kernel(**inputs):
    import numpy as np
    import concourse.bacc as bacc
    from concourse.bass_utils import run_bass_kernel_spmd as run

    a = {n: np.asarray(v) for n, v in inputs.items()}
    slots = [0, 2, 1, 3]

    def cols(v):
        return v.reshape(-1, P).T

    def pack(w):
        return w.reshape(w.shape[0] // P, P, w.shape[1]).transpose(1, 0, 2).reshape(P, -1)

    def chunks(w, width):
        return np.stack([pack(w[:, c:c + width]) for c in range(0, w.shape[1], width)])

    def pairs(w):
        lo, hi = w[:, :DFF].reshape(-1, FT, P), w[:, DFF:].reshape(-1, FT, P)
        return np.stack([lo, hi], axis=2).reshape(w.shape[0], 2 * DFF)

    def wide(v):
        return np.broadcast_to(v[None, :], (P, v.size))

    w_mix, w_tok, vec1 = [], [], []
    for l in range(L1):
        w = a["w_in"][l]
        aq, bq = w[:, 0:256].reshape(D, 4, HD), w[:, 512:768]
        first = np.concatenate([aq[:, 0], aq[:, 2], aq[:, 1], aq[:, 3], w[:, 256:384], bq, w[:, 896:960], w[:, 1024:1088],
                                w[:, 768:832], w[:, 768:832], w[:, 832:896], w[:, 832:896], w[:, 1164:3212]], axis=1)
        w_mix.append(chunks(first, CH))
        gates = w[:, 1152:1164].reshape(D, 3, 4)[:, :, slots].reshape(D, 12)
        w_tok.append(pack(np.concatenate([w[:, 384:512], w[:, 960:1024], w[:, 1088:1152], gates, w[:, 3212:3220]], axis=1)))
        w2k = a["cmp_k_w2"][l]
        vec1.append(np.concatenate([
            cols(a["norm_mix"][l]), cols(a["norm_ffn"][l]), cols(a["ada_b"][l]),
            a["gdn_conv_w"][l].reshape(4, 12, P).transpose(2, 0, 1).reshape(P, 48), wide(a["gdn_norm"][l]),
            wide(a["attn_sinks"][l]), wide(a["gdn_A_log"][l]), wide(a["gdn_dt_bias"][l]),
            a["cmp_pe_k"][l].reshape(CMP_PAIRS, P).T, a["cmp_pe_v"][l].reshape(CMP_PAIRS, P).T,
            pack(np.concatenate([w2k, w2k], axis=1)), pack(a["cmp_v_w2"][l])], axis=1))
    vec2 = []
    for l in range(2):
        cw, cb = pairs(a["conv_w_2"][l]), pairs(a["conv_b_2"][l][None])
        vec2.append(np.concatenate([
            cols(a["attn_norm_2"][l]), cols(a["ffn_norm_2"][l]),
            cw.reshape(3, 2 * FT, P).transpose(2, 0, 1).reshape(P, -1), cols(cb)], axis=1))
    parts, dist = shape_constants()
    knorm = a["idx_k_norm_2"][0]
    parts.update(final1=cols(a["final_norm"]), final2=cols(a["final_norm_2"]),
                 knorm=np.concatenate([knorm, knorm])[:, None])
    consts = np.concatenate([np.asarray(parts[n], np.float32) for n in CN], axis=1)
    table = np.concatenate([a["rel_bias_2"].reshape(32, 4, 4)[:, :, slots].reshape(32, 16), np.ones((1, 16), np.float32)])
    even = a["w_in_even_2"][0]
    wi = even[:, 4160:4176].reshape(D, 4, 4)[:, :, slots].reshape(D, 16)
    ki = even[:, 4096:4160]
    arrays = dict(
        xT=a["x"][0].T.reshape(KT, P, S).transpose(1, 0, 2), c=cols(a["c"][0]),
        vec1=np.stack(vec1, axis=1), vec2=np.stack(vec2, axis=1), consts=consts, dist=dist, table=table,
        ada=np.concatenate([chunks(a["ada_w"][l], CH) for l in range(L1)]), w_mix=np.stack(w_mix), w_tok=np.stack(w_tok),
        w_cmp=np.stack([np.stack([pack(a[n][l]) for n in ("cmp_k_w1", "cmp_v_w1")]) for l in range(L1)]),
        w_out=np.stack([chunks(a["w_out"][l], CH) for l in range(L1)]),
        w_gu=np.stack([chunks(pairs(a["w_gate_up"][l]), CH) for l in range(L1)]),
        w_dn=np.stack([chunks(a["w_down"][l], P) for l in range(L1)]),
        even_in=chunks(even[:, 0:4096], CH), even_tail=pack(np.concatenate([ki, ki, wi], axis=1)),
        odd_in=chunks(a["w_in_odd_2"][0], CH), w_o2=np.stack([chunks(a["w_o_2"][l], CH) for l in range(2)]),
        w_up2=np.stack([chunks(pairs(a["w_up_2"][l]), CH) for l in range(2)]),
        w_dn2=np.stack([chunks(a["w_down_2"][l], P) for l in range(2)]))
    arrays = {n: np.ascontiguousarray(v, dtype=np.float32) for n, v in arrays.items()}
    nc = bacc.Bacc("TRN2", target_bir_lowering=False, num_devices=1)
    args = [nc.dram_tensor(n, v.shape, F32, kind="ExternalInput").ap() for n, v in arrays.items()]
    y = nc.dram_tensor("y", (P, KT, S), F32, kind="ExternalOutput").ap()
    bias_dram = nc.dram_tensor("bias_dram", (2, 16, BIAS_W), F32, kind="Internal").ap()
    bias_wide = nc.dram_tensor("bias_wide", (32, P, BIAS_W), F32, kind="Internal").ap()
    hybrid_then_mixture(nc, *args, y, bias_dram, bias_wide)
    r = run(nc, [arrays], core_ids=[0])
    out = r.results[0]["y"]
    return np.ascontiguousarray(out.transpose(2, 1, 0).reshape(1, S, D))
```

```python
import concourse.bass as bass
from concourse import mybir
from contextlib import ExitStack

F32 = mybir.dt.float32
F32R = mybir.dt.float32r
ALU = mybir.AluOpType
ACT = mybir.ActivationFunctionType
AX = mybir.AxisListType

P = 128
S = 256
QT = S // P
D = 1024
KT = D // P
HD = 64
NG = 4
L1 = 2
DFF = 2816
FT = DFF // P
CH = 512
HALF = KT * CH // 2
AHEAD = 3
ADA_L = 6 * D // CH
ADA = L1 * ADA_L
ADA_FIRST = 2 * D // CH
SLOTS = 3
EPS = 1e-6
SCALE = HD ** -0.5
NEG = -1e30
N_CMP = S // 16 - 1
CMP_PAIRS = 16
GH = 4
GD = 128
NCH = QT * GH
DEPTH = 3
LEVELS = 7
TAILW = 144
TOKW = 276
GATES, A_COL, B_COL = 256, 268, 272
KQ_BANKS = (4, 5, 6, 3)
MOD_COL = 256
BIAS_W = 384

V1 = dict(norm_mix=(0, 8), norm_ffn=(8, 8), ada_b=(16, 48), conv=(64, 48), gnorm=(112, 128), sink=(240, 4),
          a_log=(244, 4), dt=(248, 4), pe_k=(252, 16), pe_v=(268, 16), w2k=(284, 256), w2v=(540, 128))
V1W = 668
V2 = dict(norm_attn=(0, 8), norm_ffn=(8, 8), conv_w=(16, 132), conv_b=(148, 44))
V2W = 192
CN = dict(cos=(0, 256), sin=(256, 256), ident=(512, 128), rot=(640, 128), ones=(768, 128), halves=(896, 128),
          upper=(1024, 128), strict=(1152, 128), levels=(1280, 896), causal0=(2176, 128), band1=(2304, 256),
          causal1=(2560, 256), cmp_mask=(2816, 30), cmp_valid=(2846, 30), final1=(2876, 8), final2=(2884, 8),
          knorm=(2892, 1), eps=(2893, 1))
CNW = 2894


class Chain:

    def __init__(self, eng, sem):
        self.eng, self.sem, self.n = eng, sem, 0

    def mark(self, ins):
        self.n += 1
        ins.then_inc(self.sem, 1)

    def wait(self):
        self.eng.wait_ge(self.sem, self.n)

    def __call__(self, ins):
        self.mark(ins)
        self.wait()


def hybrid_then_mixture(nc, xT, c, vec1, vec2, consts, dist, table, ada, w_mix, w_tok, w_cmp, w_out, w_gu, w_dn,
                        even_in, even_tail, odd_in, w_o2, w_up2, w_dn2, y, bias_dram,
                        bias_wide):
    phases = {}
    halves = []
    count = dict(chunk=0, event=0, tile=0)
    chunk_end = []
    ada_at = []
    KINDS = dict(columns=((2, 4), (1, 2, 3, 4)), tokens=((1, 3), (2, 3)), rows=((1, 3), (2, 3)),
                 down=((1, 2), (2,)), tail=((1, 4), (2, 3, 4)), compress=((), ()))

    def phase(name, kinds, size=HALF, ada_after=()):
        ph = phases[name] = dict(n0=count["chunk"], e0=count["event"], t0=count["tile"], u0=len(halves), chunks=len(kinds),
                                 at=[], kinds=kinds, tile_event=[])
        for j, kind in enumerate(kinds):
            ends, tiles = KINDS[kind]
            e, n = count["event"], count["chunk"]
            ph["at"].append(n)
            halves.extend((n, part, size, e + end) for part, end in enumerate(ends))
            ph["tile_event"].extend(e + t for t in tiles)
            count["event"] += ends[-1] if ends else 1
            chunk_end.append(("event", count["event"]))
            count["chunk"] += 1
            if j in ada_after:
                ada_chunks(1)
        count["tile"] = ph["t0"] + len(ph["tile_event"])
        ph["u1"] = len(halves)

    def ada_chunks(n):
        for _ in range(n):
            if late_ada(len(ada_at)):
                ada_at.extend([None] * (2 + ADA_FIRST))
            ada_at.append(count["chunk"])
            chunk_end.append(("sums", len(ada_at)))
            count["chunk"] += 1

    def late_ada(m):
        return ADA_L - 2 <= m < ADA_L + ADA_FIRST or m >= ADA - 2

    NEXT_ADA = (1, 3, 5, 7)
    IN_ADA = (1, 3, 4)
    UP, DOWN, OUT = ["columns"] * 11, ["down"] * 8, ["columns"] * 2
    ada_chunks(ADA_FIRST)
    for l in range(L1):
        phase(f"in{l}", ["columns"] * 5 + ["tokens"], ada_after=IN_ADA)
        phase(f"tok{l}", ["rows"], KT * TOKW // 2)
        phase(f"cmp{l}", ["compress"] * 2)
        ada_chunks(3)
        phase(f"out{l}", OUT)
        phase(f"gu{l}", UP)
        phase(f"dn{l}", DOWN, FT * P // 2)
    phase("even", ["columns", "columns", "tokens"] * 2 + ["columns"] * 2)
    phase("tail", ["tail"], KT * TAILW // 2)
    phase("o0", OUT)
    phase("up0", UP)
    phase("down0", DOWN, FT * P // 2)
    phase("odd", ["columns"] * 4 + ["tokens"] * 2)
    phase("o1", OUT)
    phase("up1", UP)
    phase("down1", DOWN, FT * P // 2)
    ada_at.extend([None] * 2)
    ada_alone = [m for m in range(ADA) if ada_at[m] is None]
    late = [u for l in range(L1) for u in range(phases[f"out{l}"]["u0"], phases[f"out{l}"]["u0"] + AHEAD)]

    norm_input = [None, "out0", "dn0", "out1", "dn1", None, "o0", "down0", "o1", "down1"]
    in_place = 4
    split_norms = [n for n in range(len(norm_input) - 1) if n != in_place]
    norm_end = [KT * (n + 1 - (n >= in_place)) for n in range(len(norm_input))]

    ctx = ExitStack()
    with ctx:
        def sb(name, shape):
            return ctx.enter_context(nc.sbuf_tensor(name, shape, F32))

        def sem(name):
            return ctx.enter_context(nc.semaphore(name))

        first_byte = (nc.sbuf_base + 31) // 32 * 32

        ring = sb("ring", [P, SLOTS, KT * CH])
        h = sb("h", [P, KT, S])
        mix = sb("mix", [P, KT, S])
        lg = sb("lg", [P, DEPTH, NG, S])
        arena = sb("arena", [P, 23104])
        sizes = dict(ring=4 * SLOTS * KT * CH, h=4 * KT * S, mix=4 * KT * S, lg=4 * DEPTH * NG * S)
        x = sb("x", [P, KT, S])
        v1 = sb("v1", [P, L1, V1W])
        v2 = sb("v2", [P, 2, V2W])
        cn = sb("cn", [P, CNW])
        c_in = sb("c_in", [P, KT])
        c_silu = sb("c_silu", [P, KT])
        table_sb = sb("table_sb", [33, 16])
        mod = sb("mod", [P, L1, 48])
        gain = sb("gain", [P, L1, 2, KT])
        std = sb("std", [P, S])
        rstd = sb("rstd", [P, S])
        sg = sb("sg", [P, 2, S])
        small = sb("small", [P, 176])
        pT = sb("pT", [P, 2, QT, NG * P])
        negm = sb("negm", [P, DEPTH, NG])
        sums = sb("sums", [P, DEPTH, NG])
        esink = sb("esink", [P, DEPTH, NG])
        rec = sb("rec", [P, DEPTH, NG])
        kcT = sb("kcT", [P, N_CMP])
        vc = sb("vc", [N_CMP, HD])
        hid = sb("hid", [P, 2, 2, N_CMP])

        def split_part(name, place, skip, *shape):
            at = first_byte
            for n, size in sizes.items():
                if n == place:
                    break
                at += size
            return nc.alloc_sbuf_tensor_at(name, [P, *shape], F32R, offset=at + 4 * skip)

        w_lo = split_part("w_lo", "ring", 0, SLOTS, KT * CH)
        h_lo = split_part("h_lo", "h", 0, KT, S)
        mix_lo = split_part("mix_lo", "mix", 0, KT, S)
        hi_T = split_part("hi_T", "lg", 0, KT, S)
        w_hi = split_part("w_hi", "arena", 6656, AHEAD, HALF)
        act_lo = split_part("act_lo", "arena", 0, FT, S)
        act_hi = split_part("act_hi", "arena", 12800, FT, S)

        def view(at, *shape):
            size = 1
            for n in shape:
                size *= n
            flat = arena[:, at:at + size]
            if len(shape) == 1:
                return flat
            if len(shape) == 2:
                return flat.rearrange("p (a b) -> p a b", a=shape[0])
            return flat.rearrange("p (a b c) -> p a b c", a=shape[0], b=shape[1])

        conv_in = view(0, 12, S + 3)
        conv = view(3108, 12, S)
        kn = view(0, NCH, GD)
        kb = view(1024, NCH, GD)
        vb = view(2048, NCH, GD)
        qn = view(3072, NCH, GD)
        kbg = view(4096, GH, GD)
        qd = view(4608, GH, GD)
        kd = view(5120, GH, GD)
        act_T = view(0, FT, S)
        cv = view(FT * S, 2, 2, S)
        tok = view(6656, 3, NCH, GD)
        kbqT = view(6656, NCH, 2, GD)
        knT = view(8704, NCH, GD)
        qdT = view(9728, GH, GD)
        Dm = view(10240, NCH, P)
        MT = view(11264, NCH, P)
        QKT = view(12288, NCH, P)
        MbT = view(13312, 2, NCH, P)
        X = view(15360, NCH, P)
        XT = view(16384, NCH, P)
        T1 = view(17408, NCH, P)
        U = view(10240, NCH, GD)
        wT = view(18432, GH, P)
        st = view(18944, GH, GD)
        z = view(19456, QT, GH * GD)
        tokp = view(20480, QT, TOKW)
        gB = view(13312, NCH, P)
        sq_tok = view(14336, NCH, GD)
        o_n = view(15360, NCH, GD)
        raw = view(21056, 8, S)
        dist_sb = view(21056, 2, BIAS_W)[0:33]
        tab_rows = view(21824, 2, BIAS_W)[0:16]
        rot = view(13312, 7, S)
        xpe = view(16384, 2, CMP_PAIRS * N_CMP).rearrange("p a (k n) -> p a k n", k=CMP_PAIRS)
        tmp = sg
        acc = view(18432, 2, CH)
        late_sums = view(18432, CH)
        ada_late = view(19008, KT, CH)
        qk2 = view(0, 25, S)
        vv2 = view(12800, QT, 1024)
        bias2 = view(14912, 2, 16, S)
        wi = view(6400, QT, 16)
        max8 = view(6432, 8)
        rel = mix[:, :, :].rearrange("p (a s) n -> p a s n", a=2)
        score, work, selm = h[:, 0:2, :], h[:, 2:4, :], h[:, 4:6, :]

        bank = ctx.enter_context(nc.psum_tensor("bank", [P, 8, 512], F32))

        def vec(l, name):
            at, n = V1[name]
            return v1[:, l, at:at + n]

        def vec_b(l, name):
            at, n = V2[name]
            return v2[:, l, at:at + n]

        def const(name):
            at, n = CN[name]
            return cn[:, at:at + n]

        ident = const("ident")
        upper = const("upper")

        def over(ap, n):
            return ap.rearrange("p (a m) -> p a m", a=1).to_broadcast([ap.shape[0], n, ap.shape[1]])

        def along(ap, n):
            return ap.rearrange("p (m a) -> p m a", a=1).to_broadcast([ap.shape[0], ap.shape[1], n])

        consts_in = sem("consts_in")
        tables_in = sem("tables_in")
        vec2_in = sem("vec2_in")
        c_loaded = sem("c_loaded")
        slot_in = [sem(f"slot_in{s}") for s in range(SLOTS)]
        gemm_ready = sem("gemm_ready")
        gemm_freed = sem("gemm_freed")
        c_ready = sem("c_ready")
        x_ready = sem("x_ready")
        acc_ready = sem("acc_ready")
        mod_ready = sem("mod_ready")
        late_in = sem("late_in")
        mod_read = sem("mod_read")
        sq_ready = sem("sq_ready")
        ssq_ready = sem("ssq_ready")
        std_ready = sem("std_ready")
        hn_ready = sem("hn_ready")
        h_hi_ready = sem("h_hi_ready")
        w_hi_ready = sem("w_hi_ready")
        w_lo_ready = sem("w_lo_ready")
        mix_hi_ready = sem("mix_hi_ready")
        mix_ready = sem("mix_ready")
        act_hi_ready = sem("act_hi_ready")
        hidden_ready = sem("hidden_ready")
        h_ready = sem("h_ready")
        rot_ready = sem("rot_ready")
        rope_done = sem("rope_done")
        conv_ready = sem("conv_ready")
        silu_ready = sem("silu_ready")
        xpe_ready = sem("xpe_ready")
        hid_ready = sem("hid_ready")
        kc_ps_ready = sem("kc_ps_ready")
        kc_ready = sem("kc_ready")
        gate_exp = sem("gate_exp")
        gate_arg = sem("gate_arg")
        scores_ready = sem("scores_ready")
        logits_done = sem("logits_done")
        exps_done = sem("exps_done")
        rec_ready = sem("rec_ready")
        probs_ready = sem("probs_ready")
        trans_ready = sem("trans_ready")
        pt_ready = sem("pt_ready")
        pv_done = sem("pv_done")
        o_evac = sem("o_evac")
        gt_ready = sem("gt_ready")
        gt_copied = sem("gt_copied")
        g_arg = sem("g_arg")
        g_fun = sem("g_fun")
        g_ready = sem("g_ready")
        gc_ready = sem("gc_ready")
        scaled = sem("scaled")
        kq_ready = sem("kq_ready")
        mt_ready = sem("mt_ready")
        mb_ready = sem("mb_ready")
        t1_ready = sem("t1_ready")
        t1_copied = sem("t1_copied")
        dx_ready = sem("dx_ready")
        x_upd = sem("x_upd")
        u_ready = sem("u_ready")
        u_copied = sem("u_copied")
        state_ready = sem("state_ready")
        state_copied = sem("state_copied")
        ws_ready = sem("ws_ready")
        vnew_ready = sem("vnew_ready")
        o_ready = sem("o_ready")
        osq_ready = sem("osq_ready")
        on_ready = sem("on_ready")
        cv_ready = sem("cv_ready")
        tap_done = sem("tap_done")
        sg_ready = sem("sg_ready")
        act_ready = sem("act_ready")
        tab_ready = sem("tab_ready")
        tab_copied = sem("tab_copied")
        tab_out = sem("tab_out")
        wide_out = sem("wide_out")
        bias_in = sem("bias_in")
        ki_sq = sem("ki_sq")
        ki_ssq = sem("ki_ssq")
        ki_std = sem("ki_std")
        ki_ready = sem("ki_ready")
        ix_ready = sem("ix_ready")
        ix_relu = sem("ix_relu")
        ix_acc = sem("ix_acc")
        y_out = sem("y_out")
        dve_chain = sem("dve_chain")
        act_chain = sem("act_chain")
        pool_chain = sem("pool_chain")

        units = []
        stages = {}

        def stage(name, us):
            stages[name] = (len(units), len(units) + len(us))
            units.extend(us)

        LO, HI = slice(0, HD), slice(HD, P)

        def hybrid_units(l):
            us = []
            for qt in range(QT):
                qs, w = slice(qt * P, qt * P + P), P * (qt + 1)
                rows = [(0, LO), (1, LO), (0, HI), (1, HI)]
                us.append(dict(
                    q=[rot[r, t, qs] for t, r in rows], k=[rot[r, 2, 0:w] for _, r in rows], w=w,
                    bias=over(const("causal0") if qt == 0 else const("band1"), NG), sink=vec(l, "sink"),
                    pv=[(0, 2, lambda kt: tokp[:, kt, 0:HD]), (2, 4, lambda kt: tokp[:, kt, HD:2 * HD])],
                    start=True, end=True, qs=qs, evac=[(0, LO, 0), (1, HI, 0), (2, LO, 1), (3, HI, 1)], gate=None))
            heads = [(0, LO), (1, LO), (0, HI), (1, HI)]
            evac = [(0, LO, 2), (1, LO, 3), (2, HI, 2), (3, HI, 3)]
            for qt in range(QT):
                qs, w = slice(qt * P, qt * P + P), P * (qt + 1)
                causal = over(const("causal0") if qt == 0 else const("causal1"), NG)
                cm = const("cmp_mask")[:, qt * N_CMP:(qt + 1) * N_CMP]
                cval = const("cmp_valid")[:, qt * N_CMP:(qt + 1) * N_CMP]
                gates = [small[:, 16 * qt + NG * b:16 * qt + NG * b + NG] for b in range(3)]
                us.append(dict(
                    q=[raw[r, 3 + t, qs] for t, r in heads], k=[kcT[r, :] for _, r in heads], w=N_CMP,
                    bias=over(cm, NG), valid=over(cval, NG), sink=None, gate=gates[0],
                    pv=[(0, 4, lambda kt: vc[:, :])], start=True, end=False, qs=qs, evac=evac))
                us.append(dict(
                    q=[rot[r, 3 + t, qs] for t, r in heads],
                    k=[rot[r, 5 if r is LO else 6, 0:w] for _, r in heads], w=w,
                    bias=causal, sink=None, gate=gates[1],
                    pv=[(0, 4, lambda kt: tokp[:, kt, 2 * HD:3 * HD])], start=False, end=False, qs=qs, evac=evac))
                us.append(dict(
                    q=[rot[r, 3 + t, qs] for t, r in heads],
                    k=[rot[r, 6 if r is LO else 5, 0:w] for _, r in heads], w=w,
                    bias=causal, sink=None, gate=gates[2],
                    pv=[(0, 4, lambda kt: tokp[:, kt, 3 * HD:4 * HD])], start=False, end=True, qs=qs, evac=evac))
            return us

        def biased_units(q0, k0, v0, groups, bset, g0, sel):
            us = []
            for g in range(groups):
                for qt in range(QT):
                    qs, w = slice(qt * P, qt * P + P), P * (qt + 1)
                    rows = [(0, LO), (1, LO), (0, HI), (1, HI)]
                    head = [0, 2, 1, 3]
                    us.append(dict(
                        q=[qk2[r, q0 + 2 * g + t, qs] for t, r in rows],
                        k=[qk2[r, k0 + 2 * g + t, 0:w] for t, r in rows], w=w,
                        bias=bias2[:, bset, NG * (g0 + g):NG * (g0 + g) + NG, S - w:S], sink=None, gate=None,
                        sel=over(selm[:, qt, 0:w], NG) if sel else None,
                        pv=[(s, s + 1, (lambda at: lambda kt: vv2[:, kt, at:at + HD])(v0 + HD * (NG * g + head[s])))
                            for s in range(NG)],
                        start=True, end=True, qs=qs,
                        evac=[(0, LO, 2 * (g0 + g)), (1, LO, 2 * (g0 + g) + 1),
                              (2, HI, 2 * (g0 + g)), (3, HI, 2 * (g0 + g) + 1)]))
            return us

        for l in range(L1):
            stage(f"hybrid{l}", hybrid_units(l))
        stage("even", biased_units(0, 4, 0, 2, 0, 0, False) + biased_units(8, 12, 512, 2, 0, 2, True))
        stage("odd", biased_units(0, 8, 0, 4, 1, 0, False))

        def evacs_before(u):
            return sum(units[i]["end"] for i in range(u))

        def key_tiles(u):
            w = units[u]["w"]
            return [(kt, min(P, w - kt * P)) for kt in range((w + P - 1) // P)]

        block = ctx.enter_context(nc.Block())

        @block.sync
        def _(sp):
            sp.dma_start(c_in[:, :], c).then_inc(c_loaded, 16)

            def load(n, src, size):
                if n >= SLOTS:
                    kind, value = chunk_end[n - SLOTS]
                    sp.wait_ge(gemm_ready if kind == "event" else acc_ready, value)
                sp.dma_start(ring[:, n % SLOTS, 0:size], src).then_inc(slot_in[n % SLOTS], 16)

            def load_phase(name, src, per_chunk, size):
                ph = phases[name]
                n0, e0, chunks = ph["n0"], ph["e0"], ph["chunks"]
                turns = (chunks - SLOTS) // SLOTS if per_chunk else 0
                for j in range(min(SLOTS, chunks)):
                    load(n0 + j, src[j], size)
                if turns > 1:
                    with sp.Fori(0, turns) as i:
                        for j in range(SLOTS):
                            sp.wait_ge(gemm_ready, i * (SLOTS * per_chunk) + e0 + per_chunk * (j + 1))
                            sp.dma_start(ring[:, (n0 + j) % SLOTS, 0:size].rearrange("p (a n) -> p a n", a=1),
                                         src[bass.ds(i * SLOTS + SLOTS + j, 1)].rearrange("a p n -> p a n"))\
                                .then_inc(slot_in[(n0 + j) % SLOTS], 16)
                    done = SLOTS * (turns + 1)
                else:
                    done = min(SLOTS, chunks)
                for j in range(done, chunks):
                    load(n0 + j, src[j], size)

            full = KT * CH

            def load_ada(m):
                load(ada_at[m], ada[m], full)

            for l in range(L1):
                if l == 0:
                    for dst, src in ((dist_sb[:, :, :], dist), (table_sb[:, :], table)):
                        sp.dma_start(dst, src).then_inc(tables_in, 16)
                    for dst, src in ((x[:, :, :], xT), (cn[:, :], consts), (v1[:, :, :], vec1)):
                        sp.dma_start(dst, src).then_inc(consts_in, 16)
                    for m in range(ADA_FIRST):
                        load_ada(m)
                m = ADA_L * l + ADA_FIRST
                for j, at in enumerate(phases[f"in{l}"]["at"]):
                    load(at, w_mix[l][j], full)
                    if j in IN_ADA:
                        load_ada(m + IN_ADA.index(j))
                load(phases[f"tok{l}"]["n0"], w_tok[l], KT * TOKW)
                load_phase(f"cmp{l}", w_cmp[l], 0, full)
                for j in range(3, 6):
                    load_ada(m + j)
                if l == 0:
                    sp.dma_start(v2[:, :, :], vec2).then_inc(vec2_in, 16)
                    sp.wait_ge(tab_out, 16)
                    sp.dma_start(bias_wide, bass.AP(tensor=bias_dram.tensor, offset=0,
                                                    ap=[[BIAS_W, 32], [0, P], [1, BIAS_W]])).then_inc(wide_out, 16)
                load_phase(f"out{l}", w_out[l], 0, full)
                load_phase(f"gu{l}", w_gu[l], 4, full)
                load_phase(f"dn{l}", w_dn[l], 2, FT * P)
            for j in range(SLOTS):
                load(phases["even"]["n0"] + j, even_in[j], full)
            sp.wait_ge(wide_out, 16)
            sp.wait_ge(gemm_freed, phases["even"]["t0"])
            for a in range(2):
                skewed = bass.AP(tensor=bias_wide.tensor, offset=a * 16 * P * BIAS_W + P - 1,
                                 ap=[[BIAS_W - 1, P], [P * BIAS_W, 16], [1, S]])
                sp.dma_start(bias2[:, a, :, :], skewed).then_inc(bias_in, 16)
            for j in range(SLOTS, phases["even"]["chunks"]):
                load(phases["even"]["n0"] + j, even_in[j], full)
            load(phases["tail"]["n0"], even_tail, KT * TAILW)
            load_phase("o0", w_o2[0], 0, full)
            load_phase("up0", w_up2[0], 4, full)
            load_phase("down0", w_dn2[0], 2, FT * P)
            load_phase("odd", odd_in, 0, full)
            load_phase("o1", w_o2[1], 0, full)
            load_phase("up1", w_up2[1], 4, full)
            load_phase("down1", w_dn2[1], 2, FT * P)
            sp.wait_ge(h_ready, norm_end[-1])
            sp.dma_start(y, h[:, :, :]).then_inc(y_out, 16)
            sp.wait_ge(y_out, 16)

        @block.tensor
        def _(pe):
            def chunk_in(n):
                pe.wait_ge(slot_in[n % SLOTS], 16 * (n // SLOTS + 1))

            def tile_free(name, j):
                t0 = phases[name]["t0"]
                if name.startswith("tok"):
                    pe.wait_ge(gemm_freed, t0 + j - 3)
                elif j >= 4:
                    pe.wait_ge(gemm_freed, t0 + j - 3)
                elif j == 0 and t0:
                    pe.wait_ge(gemm_freed, t0)

            def split_half(u, cols):
                n, part, size, _ = halves[u]
                hi = w_hi[:, u % AHEAD, 0:size].rearrange("p (k n) -> p k n", n=cols)
                lo = w_lo[:, n % SLOTS, part * size:(part + 1) * size].rearrange("p (k n) -> p k n", n=cols)
                return hi, lo

            def half_in(u):
                pe.wait_ge(w_lo_ready, u + 1)

            def three(out, w_parts, x_parts, start, stop):
                (wh, wl), (xh, xl) = w_parts, x_parts
                nc.tensor.matmul(out, wh, xh, start=start, stop=False)
                nc.tensor.matmul(out, wh, xl, start=False, stop=False)
                return nc.tensor.matmul(out, wl, xh, start=False, stop=stop)

            def channel_tile(out, w, col, src, k0=0, ks=KT, first=None):
                (wh, wl), (xh, xl) = w, src
                for k in range(ks):
                    if first is not None:
                        pe.wait_ge(h_ready, first + k + 1)
                    last = three(out, (wh[:, k, col:col + P], wl[:, k, col:col + P]), (xh[:, k0 + k, :], xl[:, k0 + k, :]),
                                 k0 + k == 0, k0 + k == KT - 1)
                return last

            def token_tile(out, w, lo, hi, src, qt, k0=0, ks=KT):
                (wh, wl), (xh, xl) = w, src
                qs = slice(qt * P, qt * P + P)
                for k in range(ks):
                    last = three(out, (xh[:, k0 + k, qs], xl[:, k0 + k, qs]), (wh[:, k, lo:hi], wl[:, k, lo:hi]),
                                 k0 + k == 0, k0 + k == KT - 1)
                return last

            def columns_chunk(name, nn, j, src, first=None, after=None):
                for part in range(2):
                    u = phases[name]["u0"] + 2 * nn + part
                    half_in(u)
                    w = split_half(u, CH // 2)
                    for m in range(2):
                        t = j + 2 * part + m
                        tile_free(name, t)
                        channel_tile(bank[:, t % 4, 0:S], w, m * P, src, first=first if t == 0 else None)\
                            .then_inc(gemm_ready, 1)
                        if after:
                            after(t)

            def tokens_chunk(name, nn, j):
                for part in range(2):
                    u = phases[name]["u0"] + 2 * nn + part
                    half_in(u)
                    w = split_half(u, CH // 2)
                    for qt in range(QT):
                        if part == 0:
                            tile_free(name, j + qt)
                        last = token_tile(bank[:, (j + qt) % 4, CH // 2 * part:CH // 2 * (part + 1)], w, 0, CH // 2,
                                          (hi_T, h_lo), qt)
                        if part == 1 or qt == QT - 1:
                            last.then_inc(gemm_ready, 1)

            def norm_sums(n):
                for k in range(KT):
                    if k % 2 == 0:
                        pe.wait_ge(sq_ready, 4 * n + k // 2 + 1)
                    last = nc.tensor.matmul(bank[:, 7, 0:S], const("ones"), h[:, k, :],
                                            start=(k == 0), stop=(k == KT - 1))
                last.then_inc(ssq_ready, 1)

            def modulations(m0, m1):
                for m in range(m0, m1):
                    pe.wait_ge(acc_ready, m + 1)
                    for t in range(4):
                        at = MOD_COL + 4 * m + t
                        sums_m = acc[:, m % 2, :] if ada_at[m] is not None else late_sums
                        last = nc.tensor.matmul(bank[:, 7, at:at + 1], sums_m[:, t * P:t * P + P],
                                                const("ones")[:, 0:1], start=True, stop=True)
                    last.then_inc(mod_ready, 1)

            def attention(name, m_next=None):
                u0, u1 = stages[name]

                def scores(u):
                    U = units[u]
                    if u >= 2:
                        pe.wait_ge(logits_done, u - 1)
                    for s in range(NG):
                        last = nc.tensor.matmul(bank[:, 2 * (u % 2) + s // 2, (s % 2) * S:(s % 2) * S + U["w"]],
                                                U["q"][s], U["k"][s], start=True, stop=True)
                    last.then_inc(scores_ready, 1)

                def transposes(u):
                    pe.wait_ge(probs_ready, u + 1)
                    if u >= 1:
                        pe.wait_ge(pt_ready, u)
                    for kt, n in key_tiles(u):
                        for s in range(NG):
                            last = nc.tensor.transpose(bank[0:n, 4 + kt, s * P:s * P + P],
                                                       lg[:, u % DEPTH, s, kt * P:kt * P + n], ident)
                    last.then_inc(trans_ready, 1)

                def values(u):
                    U = units[u]
                    pe.wait_ge(pt_ready, u + 1)
                    if U["start"] and evacs_before(u):
                        pe.wait_ge(o_evac, evacs_before(u))
                    tiles = key_tiles(u)
                    for lo, hi, v in U["pv"]:
                        for kt, n in tiles:
                            last = nc.tensor.matmul(
                                bank[0:HD, 6, lo * P:hi * P], v(kt), pT[0:n, u % 2, kt, lo * P:hi * P],
                                start=U["start"] and kt == 0, stop=U["end"] and kt == tiles[-1][0])
                    last.then_inc(pv_done, 1)

                for u in range(u0, u0 + DEPTH):
                    scores(u)
                for u in range(u0, u1):
                    if m_next and u in (u0 + 1, u0 + 2):
                        modulations(m_next + u - u0 - 1, m_next + u - u0)
                    transposes(u)
                    if u + DEPTH < u1:
                        scores(u + DEPTH)
                    values(u)

            def delta_net(l, m_next):
                g0 = 15 * l
                u_end = stages[f"hybrid{l}"][1]

                def group(j, srcs, done):
                    if j >= 4:
                        pe.wait_ge(gt_copied, done)
                    for i, src in enumerate(srcs):
                        last = nc.tensor.transpose(bank[:, j % 4, i * P:i * P + P], src, ident)
                    last.then_inc(gt_ready, 1)

                pe.wait_ge(silu_ready, 3 * (l + 1))
                pe.wait_ge(logits_done, u_end)
                for j in range(6):
                    group(j, [conv[:, 4 * (j // 2) + hd, (j % 2) * P:(j % 2) * P + P] for hd in range(GH)], g0 + j - 3)
                pe.wait_ge(g_ready, l + 1)
                pe.wait_ge(pt_ready, u_end)
                pe.wait_ge(o_evac, evacs_before(u_end))
                nc.tensor.matmul(bank[:, 6, 0:NCH], upper, small[:, 96:96 + NCH], start=True, stop=True)
                for ch in range(NCH):
                    last = nc.tensor.matmul(bank[:, 4 + ch // 4, (ch % 4) * P:(ch % 4) * P + P], gB[:, ch, :], upper,
                                            start=True, stop=True)
                last.then_inc(gc_ready, 1)
                modulations(m_next, m_next + 1)
                pe.wait_ge(scaled, l + 1)
                lists = [[kb[:, 4 * cc + i, :] for i in range(4)] for cc in range(2)] \
                    + [[kn[:, 4 * cc + i, :] for i in range(4)] for cc in range(2)] \
                    + [[qn[:, 4 * cc + i, :] for i in range(4)] for cc in range(2)] + [[qd[:, i, :] for i in range(4)]]
                for j, srcs in enumerate(lists):
                    group(6 + j, srcs, g0 + 6 + j - 3)
                pe.wait_ge(gt_copied, g0 + 13)
                for ch in range(NCH):
                    last = nc.tensor.matmul(bank[:, KQ_BANKS[ch // 2], (ch % 2) * S:(ch % 2) * S + S], knT[:, ch, :],
                                            kbqT[:, ch, :, :].rearrange("p a n -> p (a n)"), start=True, stop=True)
                    if ch % 2:
                        last.then_inc(kq_ready, 1)
                for lv in range(LEVELS):
                    pe.wait_ge(mb_ready, l * LEVELS + lv + 1)
                    for half in range(2):
                        if lv:
                            pe.wait_ge(x_upd, l * 2 * LEVELS + 2 * (lv - 1) + half + 1)
                        for i in range(4):
                            ch = 4 * half + i
                            last = nc.tensor.matmul(bank[:, half, i * P:i * P + P], MbT[:, lv % 2, ch, :],
                                                    X[:, ch, :] if lv else ident, start=True, stop=True)
                        last.then_inc(t1_ready, 1)
                    for half in range(2 if lv else 0):
                        pe.wait_ge(t1_copied, l * 2 * (LEVELS - 1) + 2 * (lv - 1) + half + 1)
                        for i in range(4):
                            ch = 4 * half + i
                            if lv < LEVELS - 1:
                                nc.tensor.matmul(bank[:, 2 + half, i * P:i * P + P], XT[:, ch, :], T1[:, ch, :],
                                                 start=True, stop=True)
                            last = nc.tensor.matmul(bank[:, 4 + half, i * P:i * P + P], T1[:, ch, :], XT[:, ch, :],
                                                    start=True, stop=True)
                        last.then_inc(dx_ready, 1)
                pe.wait_ge(x_upd, (l + 1) * 2 * LEVELS)
                for ch in range(NCH):
                    nc.tensor.matmul(bank[:, ch // 4, (ch % 4) * P:(ch % 4) * P + P], XT[:, ch, :], vb[:, ch, :],
                                     start=True, stop=True)
                for i in range(GH):
                    last = nc.tensor.matmul(bank[:, 2, i * P:i * P + P], kbg[:, i, :], XT[:, GH + i, :],
                                            start=True, stop=True)
                last.then_inc(u_ready, 1)
                pe.wait_ge(u_copied, l + 1)
                for i in range(GH):
                    last = nc.tensor.matmul(bank[:, 3, i * P:i * P + P], kd[:, i, :], U[:, i, :], start=True, stop=True)
                last.then_inc(state_ready, 1)
                for i in range(GH):
                    last = nc.tensor.matmul(bank[:, 4, i * P:i * P + P], QKT[:, i, :], U[:, i, :], start=True, stop=True)
                last.then_inc(o_ready, 1)
                pe.wait_ge(state_copied, l + 1)
                for i in range(GH):
                    last = nc.tensor.matmul(bank[:, 5, i * P:i * P + P], wT[:, i, :], st[:, i, :], start=True, stop=True)
                last.then_inc(ws_ready, 1)
                pe.wait_ge(vnew_ready, l + 1)
                for i in range(GH):
                    nc.tensor.matmul(bank[:, 6, i * P:i * P + P], qdT[:, i, :], st[:, i, :], start=True, stop=False)
                    last = nc.tensor.matmul(bank[:, 6, i * P:i * P + P], QKT[:, GH + i, :], U[:, GH + i, :],
                                            start=False, stop=True)
                last.then_inc(o_ready, 1)
                pe.wait_ge(on_ready, l + 1)
                for cc in range(2):
                    group(13 + cc, [o_n[:, GH * cc + i, :] for i in range(GH)], g0 + 13)

            def projection(name, done):
                pe.wait_ge(mix_ready, done)
                for nn in range(2):
                    columns_chunk(name, nn, 4 * nn, (hi_T, mix_lo))

            def up(name, first, m_next=None):
                ph = phases[name]
                u0, t0 = ph["u0"], ph["t0"]

                def one(j, split, free):
                    for part in range(2):
                        pe.wait_ge(w_lo_ready, split + part)
                        w = split_half(u0 + 2 * j + part, CH // 2)
                        for m in range(2):
                            pe.wait_ge(gemm_freed, free + 2 * part + m)
                            channel_tile(bank[:, 2 * part + m, 0:S], w, m * P, (hi_T, h_lo),
                                         first=first if (j, part, m) == (0, 0, 0) else None).then_inc(gemm_ready, 1)

                turns = 11 // SLOTS
                pe.wait_ge(gemm_freed, t0)
                with pe.Fori(0, turns) as i:
                    for j in range(SLOTS):
                        one(j, i * (2 * SLOTS) + u0 + 2 * j + 1, i * (4 * SLOTS) + t0 + 4 * j - 3)
                for j in range(SLOTS * turns, 11):
                    if m_next:
                        modulations(m_next + j - SLOTS * turns, m_next + j - SLOTS * turns + 1)
                    one(j, u0 + 2 * j + 1, t0 + 4 * j - 3)

            def down(name, done):
                ph = phases[name]
                for j in range(KT):
                    if name == "dn0" and j in NEXT_ADA:
                        m = ADA_L + NEXT_ADA.index(j)
                        if m == ADA_L:
                            pe.wait_ge(mod_read, 2)
                        modulations(m, m + 1)
                    tile_free(name, j)
                    for part in range(2):
                        if j == 0:
                            pe.wait_ge(hidden_ready, done - (5 if part == 0 else 0))
                        u = ph["u0"] + 2 * j + part
                        half_in(u)
                        wh, wl = split_half(u, P)
                        for k in range(FT // 2):
                            kk = FT // 2 * part + k
                            last = three(bank[:, j % 4, 0:S], (wh[:, k, :], wl[:, k, :]),
                                         (act_hi[:, kk, :], act_lo[:, kk, :]), kk == 0, kk == FT - 1)
                        last.then_inc(gemm_ready, 1)

            pe.wait_ge(tables_in, 16 * 2)
            for a in range(2):
                last = nc.tensor.matmul(bank[0:16, a, 0:BIAS_W], table_sb[:, :], dist_sb[:, a, :], start=True, stop=True)
            last.then_inc(tab_ready, 1)
            pe.wait_ge(consts_in, 16 * 3)
            norm_sums(0)
            pe.wait_ge(std_ready, 1)
            modulations(0, ADA_FIRST)
            n = 0
            for l in range(L1):
                if l:
                    pe.wait_ge(mod_read, 4)
                    norm_sums(n)
                pe.wait_ge(tab_copied, 2)
                ph = phases[f"in{l}"]
                m = ADA_L * l + ADA_FIRST

                def rotate(j):
                    if 8 <= j < 14:
                        t = j - 8
                        pe.wait_ge(gemm_freed, ph["t0"] + t + 1)
                        if t >= 2:
                            pe.wait_ge(rope_done, 7 * l + t - 1)
                        nc.tensor.matmul(bank[:, 4 + t % 2, 0:S], const("rot"), raw[:, t, :], start=True, stop=True)\
                            .then_inc(rot_ready, 1)

                for nn in range(5):
                    if nn == 4:
                        modulations(m, m + 1)
                    columns_chunk(f"in{l}", nn, 4 * nn, (hi_T, h_lo), norm_end[n] - KT, rotate)
                modulations(m + 1, m + 2)
                tokens_chunk(f"in{l}", 5, 20)
                for qt in range(QT):
                    tile_free(f"tok{l}", qt)
                for part in range(2):
                    u = phases[f"tok{l}"]["u0"] + part
                    half_in(u)
                    for qt in range(QT):
                        last = token_tile(bank[:, (22 + qt) % 4, 0:TOKW], split_half(u, TOKW), 0, TOKW, (hi_T, h_lo), qt,
                                          KT // 2 * part, KT // 2)
                        if part == 1 or qt == QT - 1:
                            last.then_inc(gemm_ready, 1)
                modulations(m + 2, m + 3)
                pe.wait_ge(xpe_ready, 2 * (l + 1))
                for kv in range(2):
                    nn = phases[f"cmp{l}"]["n0"] + kv
                    chunk_in(nn)
                    w = ring[:, nn % SLOTS, :].rearrange("p (k n) -> p k n", k=CMP_PAIRS)
                    for ht in range(2):
                        at = (2 * kv + ht) * 16
                        for k in range(CMP_PAIRS):
                            last = nc.tensor.matmul(bank[:, 7, at:at + N_CMP], w[:, k, ht * P:ht * P + P],
                                                    xpe[:, kv, k, :], start=(k == 0), stop=(k == CMP_PAIRS - 1))
                    last.then_inc(gemm_ready, 1)
                pe.wait_ge(hid_ready, l + 1)
                w2k = vec(l, "w2k").rearrange("p (a n) -> p a n", a=2)
                w2v = vec(l, "w2v").rearrange("p (a n) -> p a n", a=2)
                for ht in range(2):
                    nc.tensor.matmul(bank[:, 6, 0:N_CMP], w2k[:, ht, :], hid[:, 0, ht, :], start=(ht == 0), stop=(ht == 1))
                for ht in range(2):
                    last = nc.tensor.matmul(bank[0:N_CMP, 6, 64:64 + HD], hid[:, 1, ht, :], w2v[:, ht, :],
                                            start=(ht == 0), stop=(ht == 1))
                last.then_inc(kc_ps_ready, 1)
                pe.wait_ge(rope_done, 7 * (l + 1))
                pe.wait_ge(kc_ready, l + 1)
                pe.wait_ge(gemm_freed, phases[f"out{l}"]["t0"])
                attention(f"hybrid{l}", m + 3)
                delta_net(l, m + 5)
                projection(f"out{l}", 3 * (l + 1))
                norm_sums(n + 1)
                up(f"gu{l}", norm_end[n + 1] - KT, m + 6)
                down(f"dn{l}", 11 * (l + 1))
                n += 2
            norm_sums(n)
            n += 1
            for l, name in enumerate(("even", "odd")):
                norm_sums(n)
                j = 0
                for nn, kind in enumerate(phases[name]["kinds"]):
                    if kind == "tokens":
                        tokens_chunk(name, nn, j)
                        j += 2
                    else:
                        columns_chunk(name, nn, j, (hi_T, h_lo), norm_end[n] - KT)
                        j += 4
                if l == 0:
                    tile_free("tail", 0)
                    for part in range(2):
                        u = phases["tail"]["u0"] + part
                        half_in(u)
                        w = split_half(u, TAILW)
                        last = channel_tile(bank[:, 0, 0:S], w, 0, (hi_T, h_lo), KT // 2 * part, KT // 2)
                        if part == 1:
                            last.then_inc(gemm_ready, 1)
                        for qt in range(QT):
                            last = token_tile(bank[:, 1 + qt, 0:16], w, P, P + 16, (hi_T, h_lo), qt, KT // 2 * part, KT // 2)
                            if part == 1 or qt == QT - 1:
                                last.then_inc(gemm_ready, 1)
                    pe.wait_ge(ki_sq, 1)
                    nc.tensor.matmul(bank[:, 7, 0:S], const("halves"), tmp[:, 0, :], start=True, stop=True)\
                        .then_inc(ki_ssq, 1)
                    pe.wait_ge(ki_ready, 1)
                    pe.wait_ge(gemm_freed, phases["o0"]["t0"])
                    for i in range(QT * 4):
                        qt, g = i // 4, i % 4
                        if i >= 2:
                            pe.wait_ge(ix_relu, i - 1)
                        for s in range(NG):
                            r = LO if s < 2 else HI
                            last = nc.tensor.matmul(
                                bank[:, 2 * (i % 2) + s // 2, (s % 2) * S:(s % 2) * S + P * (qt + 1)],
                                qk2[r, 16 + 2 * g + s % 2, qt * P:qt * P + P], qk2[r, 24, 0:P * (qt + 1)],
                                start=True, stop=True)
                        last.then_inc(ix_ready, 1)
                    pe.wait_ge(ix_relu, QT * 4)
                else:
                    pe.wait_ge(gemm_freed, phases["o1"]["t0"])
                attention(name)
                projection(f"o{l}", 3 * L1 + 2 * (l + 1))
                norm_sums(n + 1)
                up(f"up{l}", norm_end[n + 1] - KT)
                down(f"down{l}", 11 * (L1 + l + 1))
                n += 2
            norm_sums(n)

        @block.scalar
        def _(act):
            ch = Chain(act, act_chain)

            def norm_squares(n):
                ph = phases[norm_input[n]] if norm_input[n] else None
                for j in range(4):
                    if ph:
                        each = (ph["u1"] - ph["u0"]) // 4
                        ahead = [ph["u0"] + each * j + i + AHEAD for i in range(each)]
                        for u in ahead if j < 3 else ahead[:-1]:
                            high(u)
                        act.wait_ge(gemm_freed, ph["t0"] + 2 * j + 2)
                    elif n:
                        act.wait_ge(x_ready, 2 * j + 2)
                    nc.scalar.activation(h[:, 2 * j:2 * j + 2, :], x[:, 2 * j:2 * j + 2, :], ACT.Square)\
                        .then_inc(sq_ready, 1)
                act.wait_ge(ssq_ready, n + 1)
                nc.scalar.activation(std[:, :], bank[:, 7, 0:S], ACT.Sqrt, bias=const("eps"), scale=1.0 / D)\
                    .then_inc(std_ready, 1)
                if ph:
                    high(ahead[-1])

            def norm_high(n, shift=None):
                for k in range(KT):
                    act.wait_ge(hn_ready, KT * split_norms.index(n) + k + 1)
                    if shift is None:
                        ins = nc.scalar.activation(hi_T[:, k, :], h[:, k, :], ACT.Copy)
                    else:
                        ins = nc.scalar.activation(hi_T[:, k, :], h[:, k, :], ACT.Identity, bias=shift[:, k:k + 1])
                    ins.then_inc(h_hi_ready, 1)

            def high(u, turn=None, late_now=False):
                if u >= len(halves) or (u in late and not late_now):
                    return
                n, part, size, _ = halves[u]
                slot, arrived = n % SLOTS, 16 * (n // SLOTS + 1)
                if part == 0:
                    act.wait_ge(slot_in[slot], arrived if turn is None else turn * 16 + arrived)
                if u >= AHEAD:
                    used = halves[u - AHEAD][3]
                    act.wait_ge(gemm_ready, used if turn is None else turn * (4 * SLOTS) + used)
                nc.scalar.activation(w_hi[:, u % AHEAD, 0:size], ring[:, slot, part * size:(part + 1) * size], ACT.Copy)\
                    .then_inc(w_hi_ready, 1)

            def late_high(l):
                for u in range(AHEAD):
                    high(phases[f"out{l}"]["u0"] + u, late_now=True)

            def take(name, j, dst, src, func=ACT.Copy):
                act.wait_ge(gemm_ready, phases[name]["tile_event"][j])
                nc.scalar.activation(dst, src, func).then_inc(gemm_freed, 1)

            def attention(name):
                u0, u1 = stages[name]

                def exps(u):
                    U, b = units[u], u % DEPTH
                    act.wait_ge(logits_done, u + 1)
                    for s in range(NG):
                        last = nc.scalar.activation(lg[:, b, s, 0:U["w"]], lg[:, b, s, 0:U["w"]], ACT.Exp,
                                                    bias=negm[:, b, s:s + 1], accum_out=sums[:, b, s:s + 1])
                    if U["sink"] is not None:
                        last = nc.scalar.activation(esink[:, b, :], esink[:, b, :], ACT.Exp)
                    last.then_inc(exps_done, 1)

                def copy_pt(u):
                    act.wait_ge(trans_ready, u + 1)
                    if u >= 2:
                        act.wait_ge(pv_done, u - 1)
                    for kt, m in key_tiles(u):
                        last = nc.scalar.activation(pT[0:m, u % 2, kt, :], bank[0:m, 4 + kt, :], ACT.Copy)
                    last.then_inc(pt_ready, 1)

                exps(u0)
                exps(u0 + 1)
                for u in range(u0, u1):
                    if u + 2 < u1:
                        exps(u + 2)
                    copy_pt(u)

            def delta_net(l):
                g0 = 15 * l

                def group(j, dst):
                    act.wait_ge(gt_ready, g0 + j + 1)
                    nc.scalar.activation(dst, bank[:, j % 4, :].rearrange("p (a n) -> p a n", a=4), ACT.Copy)\
                        .then_inc(gt_copied, 1)

                for j in range(6):
                    group(j, tok[:, j // 2, GH * (j % 2):GH * (j % 2) + GH, :])
                act.wait_ge(o_evac, evacs_before(stages[f"hybrid{l}"][1]))
                nc.scalar.activation(hi_T[:, 0:4, :], mix[:, 0:4, :], ACT.Copy).then_inc(mix_hi_ready, 1)
                act.wait_ge(g_arg, 5 * l + 1)
                nc.scalar.activation(small[:, 64:64 + NCH], small[:, 64:64 + NCH], ACT.Exp)
                nc.scalar.activation(small[:, 88:92], vec(l, "a_log"), ACT.Exp).then_inc(g_fun, 1)
                act.wait_ge(g_arg, 5 * l + 2)
                nc.scalar.activation(small[:, 64:64 + NCH], small[:, 64:64 + NCH], ACT.Ln).then_inc(g_fun, 1)
                act.wait_ge(g_arg, 5 * l + 3)
                nc.scalar.activation(small[:, 128:144], small[:, 128:144], ACT.Sqrt, bias=const("eps")).then_inc(g_fun, 1)
                act.wait_ge(g_arg, 5 * l + 4)
                nc.scalar.activation(Dm, Dm, ACT.Exp)
                nc.scalar.activation(small[:, 112:112 + NCH], small[:, 104:104 + NCH], ACT.Exp)
                nc.scalar.activation(small[:, 120:120 + NCH], small[:, 120:120 + NCH], ACT.Exp).then_inc(g_fun, 1)
                for cc in range(2):
                    group(6 + cc, kbqT[:, GH * cc:GH * cc + GH, 0, :])
                for cc in range(2):
                    group(8 + cc, knT[:, GH * cc:GH * cc + GH, :])
                for cc in range(2):
                    group(10 + cc, kbqT[:, GH * cc:GH * cc + GH, 1, :])
                group(12, qdT)
                for lv in range(1, LEVELS):
                    for half in range(2):
                        act.wait_ge(t1_ready, l * 2 * LEVELS + 2 * lv + half + 1)
                        nc.scalar.activation(T1[:, 4 * half:4 * half + 4, :],
                                             bank[:, half, :].rearrange("p (a n) -> p a n", a=4), ACT.Copy)\
                            .then_inc(t1_copied, 1)
                act.wait_ge(u_ready, l + 1)
                for half in range(2):
                    nc.scalar.activation(U[:, 4 * half:4 * half + 4, :],
                                         bank[:, half, :].rearrange("p (a n) -> p a n", a=4), ACT.Copy)
                nc.scalar.activation(wT, bank[:, 2, :].rearrange("p (a n) -> p a n", a=4), ACT.Copy).then_inc(u_copied, 1)
                act.wait_ge(state_ready, l + 1)
                nc.scalar.activation(st, bank[:, 3, :].rearrange("p (a n) -> p a n", a=4), ACT.Copy)\
                    .then_inc(state_copied, 1)
                for cc in range(2):
                    act.wait_ge(o_ready, 2 * l + cc + 1)
                    nc.scalar.activation(sq_tok[:, GH * cc:GH * cc + GH, :],
                                         bank[:, 4 + 2 * cc, :].rearrange("p (a n) -> p a n", a=4), ACT.Square)\
                        .then_inc(osq_ready, 1)
                act.wait_ge(g_arg, 5 * l + 5)
                nc.scalar.activation(small[:, 152:160], small[:, 144:152], ACT.Sqrt, bias=const("eps"), scale=1.0 / GD)\
                    .then_inc(g_fun, 1)
                for cc in range(2):
                    cs = slice(cc * P, cc * P + P)
                    group(13 + cc, mix[:, 4:8, cs])
                    ps = bank[:, (13 + cc) % 4, :].rearrange("p (a n) -> p a n", a=4)
                    nc.scalar.activation(hi_T[:, 4:8, cs], ps, ACT.Copy).then_inc(mix_hi_ready, 1)

            def conv_silu(l, part):
                act.wait_ge(conv_ready, 3 * l + part + 1)
                nc.scalar.activation(conv[:, 4 * part:4 * part + 4, :], conv[:, 4 * part:4 * part + 4, :], ACT.Silu)\
                    .then_inc(silu_ready, 1)

            def hidden_high(j):
                at = slice(2 * j, 2 * j + 2) if isinstance(j, int) else bass.ds(j * 2, 2)
                nc.scalar.activation(act_hi[:, at, :], act_T[:, at, :], ACT.Copy).then_inc(act_hi_ready, 1)

            act.wait_ge(c_loaded, 16)
            nc.scalar.activation(c_silu[:, :], c_in[:, :], ACT.Silu).then_inc(c_ready, 1)
            act.wait_ge(tab_ready, 1)
            for a in range(2):
                nc.scalar.activation(tab_rows[:, a, :], bank[0:16, a, 0:BIAS_W], ACT.Copy).then_inc(tab_copied, 1)
            act.wait_ge(tab_copied, 2)
            act.dma_start(bias_dram.rearrange("a h d -> h a d"), tab_rows[:, :, :]).then_inc(tab_out, 16)
            act.wait_ge(consts_in, 16 * 3)
            norm_squares(0)
            n = 0
            for l in range(L1):
                if l:
                    norm_squares(n)
                if l == 0:
                    act.wait_ge(tab_out, 16)
                u0, name = phases[f"in{l}"]["u0"], f"in{l}"
                if l == 0:
                    high(0)
                    high(1)
                norm_high(n, mod[:, l, 0:8])
                if l == 0:
                    high(2)
                for i in range(10):
                    for j in (2 * i, 2 * i + 1):
                        take(name, j, raw[:, j, :] if j < 8 else conv_in[:, j - 8, 3:3 + S], bank[:, j % 4, 0:S])
                    high(u0 + i + AHEAD)
                    if i in (7, 9):
                        conv_silu(l, (i - 7) // 2)
                high(u0 + 10 + AHEAD)
                for qt in range(QT):
                    take(name, 20 + qt, z[:, qt, :], bank[:, qt, :], ACT.Silu)
                conv_silu(l, 2)
                for qt in range(QT):
                    take(f"tok{l}", qt, tokp[:, qt, :], bank[:, 2 + qt, 0:TOKW])
                act.wait_ge(gemm_freed, phases[f"out{l}"]["t0"])
                for qt in range(QT):
                    nc.scalar.activation(small[:, 16 * qt:16 * qt + 12], tokp[:, qt, GATES:GATES + 12], ACT.Exp, scale=-1.0)
                    last = nc.scalar.activation(small[:, 16 * qt + 12:16 * qt + 16], tokp[:, qt, B_COL:B_COL + 4],
                                                ACT.Exp, scale=-1.0)
                last.then_inc(gate_exp, 1)
                act.wait_ge(gemm_ready, phases[f"cmp{l}"]["e0"] + 2)
                nc.scalar.activation(hid[:, :, :, :].rearrange("p a b n -> p (a b) n"),
                                     bank[:, 7, 0:64].rearrange("p (a n) -> p a n", a=4)[:, :, 0:N_CMP], ACT.Silu)\
                    .then_inc(hid_ready, 1)
                act.wait_ge(kc_ps_ready, l + 1)
                nc.scalar.activation(kcT[:, :], bank[:, 6, 0:N_CMP], ACT.Copy)
                nc.scalar.activation(vc[:, :], bank[0:N_CMP, 6, 64:64 + HD], ACT.Copy).then_inc(kc_ready, 1)
                attention(f"hybrid{l}")
                delta_net(l)
                late_high(l)
                norm_squares(n + 1)
                norm_high(n + 1, mod[:, l, 24:32])
                ph = phases[f"gu{l}"]

                def gate_chunk(j, turn=None):
                    step = 0 if turn is None else turn * (4 * SLOTS)
                    chunk = j if turn is None else turn * SLOTS + j
                    for b in range(2):
                        act.wait_ge(gemm_ready, step + ph["e0"] + 4 * j + 2 * b + 1)
                        act.wait_ge(gemm_freed, step + ph["t0"] + 4 * j + 2 * b - 2)
                        nc.scalar.activation(sg[:, b, :], bank[:, 2 * b, 0:S], ACT.Silu).then_inc(sg_ready, 1)
                        high(ph["u0"] + 2 * j + b + AHEAD, turn)
                    act.wait_ge(gemm_freed, step + ph["t0"] + 4 * j + 4)
                    hidden_high(chunk)

                turns = 11 // SLOTS
                with act.Fori(0, turns) as i:
                    for j in range(SLOTS):
                        gate_chunk(j, i)
                for j in range(SLOTS * turns, 11):
                    gate_chunk(j)
                n += 2
            norm_squares(n)
            n += 1
            act.wait_ge(vec2_in, 16)
            for l, name in enumerate(("even", "odd")):
                norm_squares(n)
                norm_high(n)
                u0 = phases[name]["u0"]
                t = 0
                j = 0
                for nn, kind in enumerate(phases[name]["kinds"]):
                    if kind == "tokens":
                        half = 0 if nn in (2, 4) else 1
                        high(u0 + 2 * nn + AHEAD)
                        for qt in range(QT):
                            take(name, j, vv2[:, qt, CH * half:CH * half + CH], bank[:, j % 4, :])
                            j += 1
                        high(u0 + 2 * nn + 1 + AHEAD)
                    else:
                        for part in range(2):
                            for m in range(2):
                                take(name, j, qk2[:, t, :], bank[:, j % 4, 0:S])
                                t += 1
                                j += 1
                            high(u0 + 2 * nn + part + AHEAD)
                if l == 0:
                    take("tail", 0, qk2[:, 24, :], bank[:, 0, 0:S])
                    for qt in range(QT):
                        take("tail", 1 + qt, wi[:, qt, :], bank[:, 1 + qt, 0:16])
                    for i in range(2):
                        high(phases["tail"]["u0"] + i + AHEAD)
                    act.wait_ge(gemm_freed, phases["o0"]["t0"])
                    nc.scalar.activation(tmp[:, 0, :], qk2[:, 24, :], ACT.Square).then_inc(ki_sq, 1)
                    act.wait_ge(ki_ssq, 1)
                    nc.scalar.activation(std[:, :], bank[:, 7, 0:S], ACT.Sqrt, bias=const("eps"), scale=1.0 / HD)\
                        .then_inc(ki_std, 1)
                    for i in range(QT * 4):
                        w = P * (i // 4 + 1)
                        act.wait_ge(ix_ready, i + 1)
                        if i >= 2:
                            act.wait_ge(ix_acc, i - 1)
                        nc.scalar.activation(
                            rel[:, i % 2, :, 0:w],
                            bank[:, 2 * (i % 2):2 * (i % 2) + 2, :].rearrange("p b (s n) -> p (b s) n", s=2)[:, :, 0:w],
                            ACT.Relu, scale=HD ** -0.5).then_inc(ix_relu, 1)
                attention(name)
                act.wait_ge(o_evac, evacs_before(stages[name][1]))
                for i in range(2):
                    nc.scalar.activation(hi_T[:, 4 * i:4 * i + 4, :], mix[:, 4 * i:4 * i + 4, :], ACT.Copy)\
                        .then_inc(mix_hi_ready, 1)
                norm_squares(n + 1)
                norm_high(n + 1)
                ph = phases[f"up{l}"]
                cw = vec_b(l, "conv_w").rearrange("p (j t) -> p j t", j=3)
                cb = vec_b(l, "conv_b")

                def value_chunk(j, turn=None):
                    step = 0 if turn is None else turn * (4 * SLOTS)
                    chunk = j if turn is None else turn * SLOTS + j

                    def silu(b):
                        act.wait_ge(gemm_freed, step + ph["t0"] + 4 * j + 2 * b + 2)
                        nc.scalar.activation(sg[:, b, :], cv[:, b, 1, :], ACT.Silu).then_inc(sg_ready, 1)

                    products = (0 if turn is None else turn * (2 * SLOTS)) + FT * l + 2 * j + 1
                    for b in range(2):
                        act.wait_ge(gemm_ready, step + ph["e0"] + 4 * j + 2 * b + 2)
                        act.wait_ge(act_ready, products)
                        for half in range(2):
                            at = 4 * j + 2 * b + half if turn is None else turn * (4 * SLOTS) + 4 * j + 2 * b + half
                            at = slice(at, at + 1) if turn is None else bass.ds(at, 1)
                            last = nc.scalar.activation(cv[:, b, half, :], bank[:, 2 * b + half, 0:S], ACT.Identity,
                                                        bias=cb[:, at], scale=cw[:, 2, at])
                        last.then_inc(cv_ready, 1)
                        high(ph["u0"] + 2 * j + b + AHEAD, turn)
                    for b in range(2):
                        silu(b)
                    act.wait_ge(act_ready, products + 2)
                    hidden_high(chunk)

                with act.Fori(0, turns) as i:
                    for j in range(SLOTS):
                        value_chunk(j, i)
                for j in range(SLOTS * turns, 11):
                    value_chunk(j)
                n += 2
            norm_squares(n)

        @block.vector
        def _(dve):
            V = nc.vector
            ch = Chain(dve, dve_chain)

            def rms(n):
                dve.wait_ge(std_ready, n + 1)
                ch(V.reciprocal(rstd[:, :], std[:, :]))

            def normalise(n, scale, out, sig):
                if n:
                    rms(n)
                for k in range(KT):
                    V.scalar_tensor_tensor(out=out[:, k, :], in0=x[:, k, :], scalar=scale[:, k:k + 1], in1=rstd[:, :],
                                           op0=ALU.mult, op1=ALU.mult).then_inc(sig, 1)

            def norm_low(n, shift=None):
                for k in range(KT):
                    dve.wait_ge(h_hi_ready, KT * split_norms.index(n) + k + 1)
                    if shift is None:
                        ins = V.tensor_tensor(h_lo[:, k, :], h[:, k, :], hi_T[:, k, :].bitcast(F32), ALU.subtract)
                    else:
                        ins = V.scalar_tensor_tensor(out=h_lo[:, k, :], in0=h[:, k, :], scalar=shift[:, k:k + 1],
                                                     in1=hi_T[:, k, :].bitcast(F32), op0=ALU.add, op1=ALU.subtract)
                    ins.then_inc(h_ready, 1)
                if norm_input[n]:
                    low(phases[norm_input[n]]["u1"] - 1 + AHEAD)

            def low(u, turn=None, late_now=False):
                if u >= len(halves) or (u in late and not late_now):
                    return
                n, part, size, _ = halves[u]
                at = slice(part * size, (part + 1) * size)
                dve.wait_ge(w_hi_ready, u + 1 if turn is None else turn * (2 * SLOTS) + u + 1)
                V.tensor_tensor(w_lo[:, n % SLOTS, at], ring[:, n % SLOTS, at], w_hi[:, u % AHEAD, 0:size].bitcast(F32),
                                ALU.subtract).then_inc(w_lo_ready, 1)

            def mix_low(done, tiles, cs):
                dve.wait_ge(mix_hi_ready, done)
                V.tensor_tensor(mix_lo[:, tiles, cs], mix[:, tiles, cs], hi_T[:, tiles, cs].bitcast(F32), ALU.subtract)\
                    .then_inc(mix_ready, 1)

            def hidden_low(j, done):
                dve.wait_ge(act_hi_ready, done)
                at = slice(2 * j, 2 * j + 2) if isinstance(j, int) else bass.ds(j * 2, 2)
                V.tensor_tensor(act_lo[:, at, :], act_T[:, at, :], act_hi[:, at, :].bitcast(F32), ALU.subtract)\
                    .then_inc(hidden_ready, 1)

            def attention(name):
                u0, u1 = stages[name]

                def logits(u):
                    U, b, w = units[u], u % DEPTH, units[u]["w"]
                    dve.wait_ge(scores_ready, u + 1)
                    if u >= DEPTH:
                        dve.wait_ge(trans_ready, u - DEPTH + 1)
                    s_ps = bank[:, 2 * (u % 2):2 * (u % 2) + 2, :].rearrange("p b (s n) -> p (b s) n", s=2)[:, :, 0:w]
                    out = lg[:, b, :, 0:w]
                    ch(V.scalar_tensor_tensor(out=out, in0=s_ps, scalar=SCALE, in1=U["bias"], op0=ALU.mult, op1=ALU.add))
                    if U.get("sel") is not None:
                        ch(V.tensor_tensor(out, out, U["sel"], ALU.add))
                    red = V.tensor_reduce(out=negm[:, b, :], in_=out, op=ALU.max, axis=AX.X, negate=True)
                    if U["sink"] is not None:
                        ch(red)
                        ch(V.scalar_tensor_tensor(out=negm[:, b, :], in0=U["sink"], scalar=-1.0, in1=negm[:, b, :],
                                                  op0=ALU.mult, op1=ALU.min))
                        red = V.tensor_tensor(esink[:, b, :], U["sink"], negm[:, b, :], ALU.add)
                    red.then_inc(logits_done, 1)

                def recip(u):
                    U, b = units[u], u % DEPTH
                    dve.wait_ge(exps_done, u + 1)
                    if U["sink"] is not None:
                        ch(V.tensor_tensor(sums[:, b, :], sums[:, b, :], esink[:, b, :], ALU.add))
                    r = V.reciprocal(rec[:, b, :], sums[:, b, :])
                    if U["gate"] is not None:
                        ch(r)
                        r = V.tensor_tensor(rec[:, b, :], rec[:, b, :], U["gate"], ALU.mult)
                    r.then_inc(rec_ready, 1)

                def evac(u):
                    U = units[u]
                    if not U["end"]:
                        return
                    dve.wait_ge(pv_done, u + 1)
                    for s, rows, tile in U["evac"]:
                        last = V.tensor_copy(mix[rows, tile, U["qs"]], bank[0:HD, 6, s * P:s * P + P])
                    last.then_inc(o_evac, 1)

                logits(u0)
                logits(u0 + 1)
                for u in range(u0, u1 + 1):
                    if u + 2 < u1:
                        logits(u + 2)
                    if u < u1:
                        recip(u)
                    if u > u0:
                        evac(u - 1)

            def delta_net(l):
                a = small[:, 64:64 + NCH]
                relu = small[:, 72:72 + NCH]
                ea, g, gc = small[:, 88:92], small[:, 96:96 + NCH], small[:, 104:104 + NCH]
                eg, ekd = small[:, 112:112 + NCH], small[:, 120:120 + NCH]
                rqk = small[:, 128:144]
                beta = small[:, 160:160 + NCH]
                a3 = a.rearrange("p (c h) -> p c h", c=QT)
                ch(V.tensor_tensor(a3, tokp[:, :, A_COL:A_COL + 4], over(vec(l, "dt"), QT), ALU.add))
                ch(V.tensor_scalar(relu, a, 0.0, None, ALU.max))
                ch(V.scalar_tensor_tensor(out=small[:, 80:88], in0=a, scalar=-1.0, in1=a, op0=ALU.mult, op1=ALU.min))
                V.tensor_copy(a, small[:, 80:88]).then_inc(g_arg, 1)
                ch(V.tensor_copy(beta.rearrange("p (c h) -> p c h", c=QT),
                                 small[:, 0:32].rearrange("p (c n) -> p c n", c=QT)[:, :, 12:16]))
                dve.wait_ge(g_fun, 5 * l + 1)
                V.tensor_scalar(a, a, 1.0, None, ALU.add).then_inc(g_arg, 1)
                dve.wait_ge(g_fun, 5 * l + 2)
                ch(V.tensor_tensor(relu, relu, a, ALU.add))
                ch(V.scalar_tensor_tensor(out=g.rearrange("p (c h) -> p c h", c=QT),
                                          in0=relu.rearrange("p (c h) -> p c h", c=QT), scalar=-1.0, in1=over(ea, QT),
                                          op0=ALU.mult, op1=ALU.mult))
                V.tensor_copy(gB, along(g, P)).then_inc(g_ready, 1)
                dve.wait_ge(gt_copied, 15 * l + 4)
                for qk in range(2):
                    ch(V.tensor_tensor(sq_tok, tok[:, qk], tok[:, qk], ALU.mult))
                    last = V.tensor_reduce(out=rqk[:, NCH * qk:NCH * qk + NCH], in_=sq_tok, op=ALU.add, axis=AX.X)
                    ch(last)
                V.tensor_copy(rqk, rqk).then_inc(g_arg, 1)
                mix_low(3 * l + 1, slice(0, 4), slice(0, S))
                dve.wait_ge(gc_ready, l + 1)
                ch(V.tensor_copy(gc, bank[:, 6, 0:NCH]))
                for i in range(NCH):
                    ch.mark(V.tensor_scalar(Dm[:, i, :], bank[:, 4 + i // 4, (i % 4) * P:(i % 4) * P + P],
                                            gc[:, i:i + 1], 0.0, ALU.subtract, ALU.min))
                for cc in range(2):
                    last = V.tensor_tensor(
                        ekd[:, 4 * cc:4 * cc + 4],
                        bank[:, 4 + cc, :].rearrange("p (a n) -> p a n", a=4)[:, :, P - 1], gc[:, 4 * cc:4 * cc + 4],
                        ALU.subtract)
                    ch.mark(last)
                ch.wait()
                V.tensor_copy(ekd, ekd).then_inc(g_arg, 1)
                dve.wait_ge(g_fun, 5 * l + 3)
                ch(V.reciprocal(rqk, rqk))
                ch(V.tensor_scalar(rqk[:, 0:NCH], rqk[:, 0:NCH], GD ** -0.5, None, ALU.mult))
                dve.wait_ge(gt_copied, 15 * l + 6)
                ch.mark(V.tensor_tensor(qn, tok[:, 0], along(rqk[:, 0:NCH], GD), ALU.mult))
                ch.mark(V.tensor_tensor(kn, tok[:, 1], along(rqk[:, NCH:2 * NCH], GD), ALU.mult))
                ch(V.tensor_tensor(vb, tok[:, 2], along(beta, GD), ALU.mult))
                ch(V.tensor_tensor(kb, kn, along(beta, GD), ALU.mult))
                dve.wait_ge(g_fun, 5 * l + 4)
                ch.mark(V.tensor_tensor(Dm, Dm, over(upper, NCH), ALU.mult))
                ch.mark(V.tensor_tensor(kbg, kb[:, GH:NCH], along(eg[:, GH:NCH], GD), ALU.mult))
                ch.mark(V.tensor_tensor(kd, kn[:, 0:GH], along(ekd[:, 0:GH], GD), ALU.mult))
                V.tensor_tensor(qd, qn[:, GH:NCH], along(eg[:, GH:NCH], GD), ALU.mult).then_inc(scaled, 1)
                ch.wait()
                for b in range(4):
                    dve.wait_ge(kq_ready, 4 * l + b + 1)
                    ps = bank[:, KQ_BANKS[b], :].rearrange("p (i a n) -> p i a n", i=2, a=2)
                    ch.mark(V.tensor_tensor(MT[:, 2 * b:2 * b + 2], ps[:, :, 0, :], Dm[:, 2 * b:2 * b + 2], ALU.mult))
                    ch.mark(V.tensor_tensor(QKT[:, 2 * b:2 * b + 2], ps[:, :, 1, :], Dm[:, 2 * b:2 * b + 2], ALU.mult))
                ch.wait()
                V.tensor_tensor(MT, MT, over(const("strict"), NCH), ALU.mult).then_inc(mt_ready, 1)
                for lv in range(LEVELS):
                    for half in range(2):
                        hs = slice(4 * half, 4 * half + 4)
                        if lv == 0:
                            dve.wait_ge(mb_ready, l * LEVELS + 1)
                            dve.wait_ge(t1_ready, l * 2 * LEVELS + half + 1)
                            ps = bank[:, half, :].rearrange("p (a n) -> p a n", a=4)
                            V.tensor_tensor(X[:, hs], over(ident, 4), ps, ALU.subtract)
                            V.tensor_tensor(XT[:, hs], over(ident, 4), MbT[:, 0, hs], ALU.subtract).then_inc(x_upd, 1)
                        else:
                            dve.wait_ge(dx_ready, l * 2 * (LEVELS - 1) + 2 * (lv - 1) + half + 1)
                            if lv < LEVELS - 1:
                                ps = bank[:, 2 + half, :].rearrange("p (a n) -> p a n", a=4)
                                V.tensor_tensor(X[:, hs], X[:, hs], ps, ALU.subtract)
                            ps = bank[:, 4 + half, :].rearrange("p (a n) -> p a n", a=4)
                            V.tensor_tensor(XT[:, hs], XT[:, hs], ps, ALU.subtract).then_inc(x_upd, 1)
                dve.wait_ge(u_copied, l + 1)
                dve.wait_ge(ws_ready, l + 1)
                V.tensor_tensor(U[:, GH:NCH], U[:, GH:NCH], bank[:, 5, :].rearrange("p (a n) -> p a n", a=4), ALU.subtract)\
                    .then_inc(vnew_ready, 1)
                dve.wait_ge(osq_ready, 2 * (l + 1))
                V.tensor_reduce(out=small[:, 144:152], in_=sq_tok, op=ALU.add, axis=AX.X).then_inc(g_arg, 1)
                dve.wait_ge(g_fun, 5 * l + 5)
                ch(V.reciprocal(small[:, 152:160], small[:, 152:160]))
                for cc in range(2):
                    cs = slice(GH * cc, GH * cc + GH)
                    ps = bank[:, 4 + 2 * cc, :].rearrange("p (a n) -> p a n", a=4)
                    ch.mark(V.tensor_tensor(o_n[:, cs], ps, along(small[:, 152 + GH * cc:156 + GH * cc], GD), ALU.mult))
                ch.wait()
                ch(V.tensor_tensor(o_n, o_n, over(vec(l, "gnorm"), NCH), ALU.mult))
                V.tensor_tensor(o_n, o_n, z.rearrange("p c (h n) -> p (c h) n", h=GH), ALU.mult).then_inc(on_ready, 1)
                for cc in range(2):
                    mix_low(3 * l + cc + 2, slice(4, 8), slice(cc * P, cc * P + P))

            def residual(name, gate):
                ph = phases[name]
                each = 2 if ph["kinds"][0] == "down" else 1
                for k in range(KT):
                    if name == "dn0" and k in NEXT_ADA[:-1]:
                        weigh(ADA_L + 1 + NEXT_ADA.index(k))
                    if name == "dn0" and k == KT - 1:
                        dve.wait_ge(mod_ready, ADA_L + ADA_FIRST)
                        modulation(1, 0, ADA_FIRST)
                        norm_gain(1, 0).then_inc(mod_read, 2)
                        dve.wait_ge(mod_read, 4)
                    dve.wait_ge(gemm_ready, ph["tile_event"][k])
                    ps = bank[:, k % 4, 0:S]
                    if gate is None:
                        ins = V.tensor_tensor(x[:, k, :], x[:, k, :], ps, ALU.add)
                    else:
                        ins = V.scalar_tensor_tensor(out=x[:, k, :], in0=ps, scalar=gate[:, k:k + 1], in1=x[:, k, :],
                                                     op0=ALU.mult, op1=ALU.add)
                    ins.then_inc(gemm_freed, 1)
                    used = range(ph["u0"] + 2 * k, ph["u0"] + 2 * k + 2) if each == 2 else [ph["u0"] + k // 2] * (k % 2)
                    for u in used:
                        if u < ph["u1"] - 1:
                            low(u + AHEAD)

            def weigh(m):
                at = ada_at[m]
                if at is None:
                    dve.wait_ge(late_in, 16 * (ada_alone.index(m) + 1))
                    dve.wait_ge(mod_ready, m)
                    w, out = ada_late, late_sums
                else:
                    dve.wait_ge(slot_in[at % SLOTS], 16 * (at // SLOTS + 1))
                    if m >= 2:
                        dve.wait_ge(mod_ready, m - 1)
                    w, out = ring[:, at % SLOTS, :].rearrange("p (k n) -> p k n", k=KT), acc[:, m % 2, :]
                ch(V.tensor_scalar(out, w[:, 0, :], c_silu[:, 0:1], None, ALU.mult))
                for k in range(1, KT):
                    ins = V.scalar_tensor_tensor(out=out, in0=w[:, k, :], scalar=c_silu[:, k:k + 1], in1=out,
                                                 op0=ALU.mult, op1=ALU.add)
                    if k < KT - 1:
                        ch(ins)
                ins.then_inc(acc_ready, 1)

            def modulation(l, m0, m1, read=None):
                at = MOD_COL + 4 * ADA_L * l
                ins = V.tensor_tensor(mod[:, l, 4 * m0:4 * m1], bank[:, 7, at + 4 * m0:at + 4 * m1],
                                      vec(l, "ada_b")[:, 4 * m0:4 * m1], ALU.add)
                if read:
                    ins.then_inc(read, 1)
                    dve.wait_ge(read, 2 + 3 * l)
                else:
                    ch(ins)

            def norm_gain(l, part):
                return V.scalar_tensor_tensor(out=gain[:, l, part, :], in0=mod[:, l, 24 * part + 8:24 * part + 16],
                                              scalar=1.0, in1=vec(l, ("norm_mix", "norm_ffn")[part]),
                                              op0=ALU.add, op1=ALU.mult)

            V.memset(conv_in[:, :, 0:3], 0.0).then_inc(act_ready, 1)
            dve.wait_ge(act_ready, 1)
            dve.wait_ge(c_ready, 1)
            for m in range(ADA_FIRST):
                if m == 2:
                    rms(0)
                weigh(m)
            n = 0
            for l in range(L1):
                if l:
                    ch(V.memset(conv_in[:, :, 0:3], 0.0))
                if l == 0:
                    dve.wait_ge(consts_in, 16 * 3)
                    dve.wait_ge(mod_ready, ADA_FIRST)
                    modulation(0, 0, ADA_FIRST)
                    norm_gain(0, 0).then_inc(mod_read, 1)
                    dve.wait_ge(mod_read, 1)
                normalise(n, gain[:, l, 0, :], h, hn_ready)
                if l == 0:
                    low(0)
                    low(1)
                norm_low(n, mod[:, l, 0:8])
                m = ADA_L * l + ADA_FIRST
                u0 = phases[f"in{l}"]["u0"]
                if l == 0:
                    low(2)
                for i in range(3):
                    low(u0 + i + AHEAD)
                t0 = phases[f"in{l}"]["t0"]
                for t in range(6):
                    if t % 2 == 0:
                        low(u0 + 3 + t // 2 + AHEAD)
                    if t == 2:
                        weigh(m)
                    dve.wait_ge(gemm_freed, t0 + t + 1)
                    dve.wait_ge(rot_ready, 6 * l + t + 1)
                    ch.mark(V.tensor_tensor(tmp[:, 0, :], raw[:, t, :], const("cos"), ALU.mult))
                    ch(V.tensor_tensor(tmp[:, 1, :], bank[:, 4 + t % 2, 0:S], const("sin"), ALU.mult))
                    V.tensor_tensor(rot[:, t, :], tmp[:, 0, :], tmp[:, 1, :], ALU.add).then_inc(rope_done, 1)
                    dve.wait_ge(rope_done, 7 * l + t + 1)
                V.tensor_copy(rot[LO, 6, :], rot[HI, 5, :])
                V.tensor_copy(rot[HI, 6, :], rot[LO, 5, :]).then_inc(rope_done, 1)
                low(u0 + 6 + AHEAD)
                dve.wait_ge(gemm_freed, t0 + 8)
                for kv, pe_name in enumerate(("pe_k", "pe_v")):
                    for two, rows in enumerate((LO, HI)):
                        base = raw[rows, 6 + kv, :].rearrange("p (n q a) -> p a q n", q=8, a=2)[:, two]
                        for hf in range(2):
                            last = V.tensor_tensor(
                                xpe[rows, kv, 8 * hf:8 * hf + 8, :], base[:, :, hf:hf + N_CMP],
                                along(vec(l, pe_name)[rows, 8 * hf:8 * hf + 8], N_CMP), ALU.add)
                    last.then_inc(xpe_ready, 1)
                cw = vec(l, "conv").rearrange("p (j t) -> p j t", j=4)
                for part in range(3):
                    if part == 0:
                        weigh(m + 1)
                    if part == 2:
                        low(u0 + 9 + AHEAD)
                        weigh(m + 2)
                    dve.wait_ge(gemm_freed, t0 + 8 + 4 * part + 4)
                    for tap in range(4):
                        if tap:
                            ch.wait()
                        for t in range(4 * part, 4 * part + 4):
                            src, wt = conv_in[:, t, tap:tap + S], cw[:, tap, t:t + 1]
                            if tap == 0:
                                ins = V.tensor_scalar(conv[:, t, :], src, wt, None, ALU.mult)
                            else:
                                ins = V.scalar_tensor_tensor(out=conv[:, t, :], in0=src, scalar=wt, in1=conv[:, t, :],
                                                             op0=ALU.mult, op1=ALU.add)
                            if tap == 3 and t % 4 == 3:
                                ins.then_inc(conv_ready, 1)
                            else:
                                ch.mark(ins)
                    if part < 2:
                        low(u0 + 7 + part + AHEAD)
                low(u0 + 10 + AHEAD)
                weigh(m + 3)
                dve.wait_ge(gate_exp, l + 1)
                ch(V.tensor_scalar(small[:, 0:32], small[:, 0:32], 1.0, None, ALU.add))
                ch(V.reciprocal(small[:, 0:32], small[:, 0:32]))
                weigh(m + 4)
                attention(f"hybrid{l}")
                weigh(m + 5)
                delta_net(l)
                dve.wait_ge(mod_ready, m + 6)
                modulation(l, ADA_FIRST, ADA_L - 2)
                ch(norm_gain(l, 1))
                for u in range(AHEAD):
                    low(phases[f"out{l}"]["u0"] + u, late_now=True)
                residual(f"out{l}", mod[:, l, 16:24])
                normalise(n + 1, gain[:, l, 1, :], h, hn_ready)
                norm_low(n + 1, mod[:, l, 24:32])
                ph = phases[f"gu{l}"]

                def gate_chunk(j, turn=None):
                    step = 0 if turn is None else turn * (4 * SLOTS)
                    tiles = 0 if turn is None else turn * (2 * SLOTS)
                    for b in range(2):
                        dve.wait_ge(sg_ready, tiles + FT * l + 2 * j + b + 1)
                        dve.wait_ge(gemm_ready, step + ph["e0"] + 4 * j + 2 * b + 2)
                        at = 2 * j + b if turn is None else turn * (2 * SLOTS) + 2 * j + b
                        at = slice(at, at + 1) if turn is None else bass.ds(at, 1)
                        V.tensor_tensor(act_T[:, at, :], sg[:, b, :].rearrange("p (a n) -> p a n", a=1),
                                        bank[:, 2 * b + 1, 0:S].rearrange("p (a n) -> p a n", a=1), ALU.mult)\
                            .then_inc(gemm_freed, 2)
                        low(ph["u0"] + 2 * j + b + AHEAD, turn)
                    hidden_low(j if turn is None else turn * SLOTS + j,
                               (0 if turn is None else turn * SLOTS) + 11 * l + j + 1)

                turns = 11 // SLOTS
                weigh(m + 6)
                with dve.Fori(0, turns) as i:
                    for j in range(SLOTS):
                        gate_chunk(j, i)
                for j in range(SLOTS * turns, 11):
                    if j == SLOTS * turns or l == 0:
                        weigh(m + 7 + j - SLOTS * turns)
                    gate_chunk(j)
                dve.wait_ge(mod_ready, m + 8)
                modulation(l, ADA_L - 2, ADA_L, mod_read)
                residual(f"dn{l}", mod[:, l, 40:48])
                n += 2
            dve.wait_ge(vec2_in, 16)
            normalise(n, const("final1"), x, x_ready)
            low(phases["dn1"]["u1"] - 1 + AHEAD)
            n += 1
            for l, name in enumerate(("even", "odd")):
                normalise(n, vec_b(l, "norm_attn"), h, hn_ready)
                norm_low(n)
                for u in range(phases[name]["u0"], phases["tail" if l == 0 else name]["u1"]):
                    low(u + AHEAD)
                if l == 0:
                    dve.wait_ge(ki_std, 1)
                    ch(V.reciprocal(rstd[:, :], std[:, :]))
                    V.scalar_tensor_tensor(out=qk2[:, 24, :], in0=qk2[:, 24, :], scalar=const("knorm"), in1=rstd[:, :],
                                           op0=ALU.mult, op1=ALU.mult).then_inc(ki_ready, 1)
                    ch(V.tensor_scalar(wi, wi, 16 ** -0.5, None, ALU.mult))
                    for i in range(QT * 4):
                        qt, g, w = i // 4, i % 4, P * (i // 4 + 1)
                        dve.wait_ge(ix_relu, i + 1)
                        for s in range(NG):
                            col = wi[:, qt, NG * g + s:NG * g + s + 1]
                            src = rel[:, i % 2, s, 0:w]
                            if g == 0 and s == 0:
                                ins = V.tensor_scalar(score[:, qt, 0:w], src, col, None, ALU.mult)
                            else:
                                ins = V.scalar_tensor_tensor(out=score[:, qt, 0:w], in0=src, scalar=col,
                                                             in1=score[:, qt, 0:w], op0=ALU.mult, op1=ALU.add)
                            if s == NG - 1:
                                ins.then_inc(ix_acc, 1)
                                dve.wait_ge(ix_acc, i + 1)
                            else:
                                ch(ins)
                        if g == 3:
                            mask = const("causal0") if qt == 0 else const("causal1")
                            ch(V.tensor_tensor(work[:, 0, 0:w], score[:, qt, 0:w], mask, ALU.add))
                            for r in range(8):
                                ch(V.max(max8, work[:, r % 2, 0:w]))
                                ch(V.match_replace(work[:, (r + 1) % 2, 0:w], max8, work[:, r % 2, 0:w], -3e38))
                            ch(V.tensor_scalar(selm[:, qt, 0:w], work[:, 0, 0:w], -2e38, NEG, ALU.is_gt, ALU.mult))
                    dve.wait_ge(bias_in, 32)
                attention(name)
                for i in range(2):
                    mix_low(3 * L1 + 2 * l + i + 1, slice(4 * i, 4 * i + 4), slice(0, S))
                residual(f"o{l}", None)
                normalise(n + 1, vec_b(l, "norm_ffn"), h, hn_ready)
                norm_low(n + 1)
                ph = phases[f"up{l}"]
                cw = vec_b(l, "conv_w").rearrange("p (j t) -> p j t", j=3)

                def value_chunk(j, turn=None):
                    step = 0 if turn is None else turn * (4 * SLOTS)
                    tiles = 0 if turn is None else turn * (2 * SLOTS)
                    for b in range(2):
                        dve.wait_ge(cv_ready, tiles + FT * l + 2 * j + b + 1)
                        for tap in (1, 0):
                            shift = 2 - tap
                            for half in range(2):
                                at = 4 * j + 2 * b + half
                                at = slice(at, at + 1) if turn is None else bass.ds(turn * (4 * SLOTS) + at, 1)
                                if tap == 0:
                                    dve.wait_ge(tap_done, step + 2 * FT * l + 4 * j + 2 * b + half + 1)
                                V.scalar_tensor_tensor(out=cv[:, b, half, shift:S], in0=bank[:, 2 * b + half, 0:S - shift],
                                                       scalar=cw[:, tap, at], in1=cv[:, b, half, shift:S],
                                                       op0=ALU.mult, op1=ALU.add)\
                                    .then_inc(tap_done if tap else gemm_freed, 1)
                        low(ph["u0"] + 2 * j + b + AHEAD, turn)
                    for b in range(2):
                        dve.wait_ge(sg_ready, tiles + FT * (L1 + l) + 2 * j + b + 1)
                        dve.wait_ge(gemm_freed, step + ph["t0"] + 4 * j + 2 * b + 2)
                        at = 2 * j + b
                        at = slice(at, at + 1) if turn is None else bass.ds(turn * (2 * SLOTS) + at, 1)
                        V.tensor_tensor(act_T[:, at, :], sg[:, b, :].rearrange("p (a n) -> p a n", a=1),
                                        cv[:, b, 0, :].rearrange("p (a n) -> p a n", a=1), ALU.mult).then_inc(act_ready, 1)
                    hidden_low(j if turn is None else turn * SLOTS + j,
                               (0 if turn is None else turn * SLOTS) + 11 * (L1 + l) + j + 1)

                with dve.Fori(0, turns) as i:
                    for j in range(SLOTS):
                        value_chunk(j, i)
                for j in range(SLOTS * turns, 11):
                    value_chunk(j)
                residual(f"down{l}", None)
                n += 2
            normalise(n, const("final2"), h, h_ready)

        @block.gpsimd
        def _(pool):
            ch = Chain(pool, pool_chain)
            G = nc.gpsimd

            def attention(name):
                u0, u1 = stages[name]
                for u in range(u0, u1):
                    U, b, w = units[u], u % DEPTH, units[u]["w"]
                    pool.wait_ge(rec_ready, u + 1)
                    out = lg[:, b, :, 0:w]
                    ins = G.tensor_tensor(out, out, along(rec[:, b, :], w), ALU.mult)
                    if U.get("valid") is not None:
                        ch(ins)
                        ins = G.tensor_tensor(out, out, U["valid"], ALU.mult)
                    ins.then_inc(probs_ready, 1)

            for l in range(L1):
                attention(f"hybrid{l}")
                pool.wait_ge(mt_ready, l + 1)
                for lv in range(LEVELS):
                    if lv >= 2:
                        pool.wait_ge(x_upd, l * 2 * LEVELS + 2 * (lv - 1))
                    lm = const("levels")[:, lv * P:lv * P + P]
                    G.tensor_tensor(MbT[:, lv % 2], MT, over(lm, NCH), ALU.mult).then_inc(mb_ready, 1)
                pool.wait_ge(mix_ready, 3 * (l + 1))
                for m in ada_alone[(2 + ADA_FIRST) * l:(2 + ADA_FIRST) * (l + 1)]:
                    if m > ada_alone[(2 + ADA_FIRST) * l]:
                        pool.wait_ge(acc_ready, m)
                    pool.dma_start(ada_late, ada[m].rearrange("p (k n) -> p k n", k=KT)).then_inc(late_in, 16)
            for name in ("even", "odd"):
                attention(name)


def shape_constants():
    import numpy as np

    f = np.float32
    i, j = np.arange(P)[:, None], np.arange(P)[None, :]
    parts = {}
    inv = (f(1) / (f(10000.0) ** (np.arange(0, HD, 2, dtype=f) / f(HD)))).astype(f)
    ang = (np.arange(S, dtype=f)[:, None] * inv[None, :]).astype(f)
    parts["cos"] = np.tile(np.cos(ang).T, (4, 1))
    parts["sin"] = np.tile(np.sin(ang).T, (4, 1))
    parts["ident"] = i == j
    parts["rot"] = (j % HD >= HD // 2) * (i == j - HD // 2) * 1.0 - (j % HD < HD // 2) * (i == j + HD // 2) * 1.0
    parts["ones"] = np.ones((P, P))
    parts["halves"] = i // HD == j // HD
    parts["upper"] = i <= j
    parts["strict"] = i < j
    parts["levels"] = np.concatenate([(i // (2 * b) == j // (2 * b)) & (i // b % 2 == 0) & (j // b % 2 == 1)
                                      for b in (1 << n for n in range(LEVELS))], axis=1)
    k = np.arange(S)[None, :]
    parts["causal0"] = np.where(j <= i, 0.0, NEG)
    parts["band1"] = np.where((k <= i + P) & (k > i), 0.0, NEG)
    parts["causal1"] = np.where(k <= i + P, 0.0, NEG)
    end = np.arange(N_CMP)[None, :] * 16 + 31
    ok = np.concatenate([end <= i + P * qt for qt in range(QT)], axis=1)
    parts["cmp_mask"] = np.where(ok, 0.0, NEG)
    parts["cmp_valid"] = ok
    parts["eps"] = np.full((P, 1), EPS)
    d = S - 1 - np.arange(BIAS_W)
    n = np.maximum(d, 0)
    nf = np.maximum(n, 16).astype(f)
    large = 16 + (np.log(nf / f(16)) / f(np.log(8.0)) * f(16)).astype(np.int32)
    bucket = np.where(n < 16, n, np.minimum(large, 31))
    dist = np.zeros((33, 2, BIAS_W), f)
    seen = d >= 0
    for a in range(2):
        dist[bucket[seen], a, np.nonzero(seen)[0]] = 1.0
    dist[32, 0] = np.where(seen, 0.0, NEG)
    times = ((d <= 128) * 1 + (d % 4 == 0) + (d % 16 == 0)) * seen
    dist[32, 1] = np.where(times > 0, np.log(np.maximum(times, 1)), NEG)
    return parts, dist


def kernel(**inputs):
    import numpy as np
    import concourse.bacc as bacc
    from concourse.bass_utils import run_bass_kernel_spmd as run

    a = {n: np.asarray(v) for n, v in inputs.items()}
    slots = [0, 2, 1, 3]

    def cols(v):
        return v.reshape(-1, P).T

    def pack(w):
        return w.reshape(w.shape[0] // P, P, w.shape[1]).transpose(1, 0, 2).reshape(P, -1)

    def halved(w):
        return np.stack([np.concatenate([pack(w[:, c:c + CH // 2]), pack(w[:, c + CH // 2:c + CH])], axis=1)
                         for c in range(0, w.shape[1], CH)])

    def chunks(w, width):
        return np.stack([pack(w[:, c:c + width]) for c in range(0, w.shape[1], width)])

    def pairs(w):
        lo, hi = w[:, :DFF].reshape(-1, FT, P), w[:, DFF:].reshape(-1, FT, P)
        return np.stack([lo, hi], axis=2).reshape(w.shape[0], 2 * DFF)

    def wide(v):
        return np.broadcast_to(v[None, :], (P, v.size))

    w_mix, w_tok, vec1 = [], [], []
    for l in range(L1):
        w = a["w_in"][l]
        aq, bq = w[:, 0:256].reshape(D, 4, HD), w[:, 512:768]
        first = np.concatenate([aq[:, 0], aq[:, 2], aq[:, 1], aq[:, 3], w[:, 256:384], bq, w[:, 896:960], w[:, 1024:1088],
                                w[:, 768:832], w[:, 768:832], w[:, 832:896], w[:, 832:896], w[:, 1164:3212]], axis=1)
        w_mix.append(halved(first))
        gates = w[:, 1152:1164].reshape(D, 3, 4)[:, :, slots].reshape(D, 12)
        w_tok.append(pack(np.concatenate([w[:, 384:512], w[:, 960:1024], w[:, 1088:1152], gates, w[:, 3212:3220]], axis=1)))
        w2k = a["cmp_k_w2"][l]
        vec1.append(np.concatenate([
            cols(a["norm_mix"][l]), cols(a["norm_ffn"][l]), cols(a["ada_b"][l]),
            a["gdn_conv_w"][l].reshape(4, 12, P).transpose(2, 0, 1).reshape(P, 48), wide(a["gdn_norm"][l]),
            wide(a["attn_sinks"][l]), wide(a["gdn_A_log"][l]), wide(a["gdn_dt_bias"][l]),
            a["cmp_pe_k"][l].reshape(CMP_PAIRS, P).T, a["cmp_pe_v"][l].reshape(CMP_PAIRS, P).T,
            pack(np.concatenate([w2k, w2k], axis=1)), pack(a["cmp_v_w2"][l])], axis=1))
    vec2 = []
    for l in range(2):
        cw, cb = pairs(a["conv_w_2"][l]), pairs(a["conv_b_2"][l][None])
        vec2.append(np.concatenate([
            cols(a["attn_norm_2"][l]), cols(a["ffn_norm_2"][l]),
            cw.reshape(3, 2 * FT, P).transpose(2, 0, 1).reshape(P, -1), cols(cb)], axis=1))
    parts, dist = shape_constants()
    knorm = a["idx_k_norm_2"][0]
    parts.update(final1=cols(a["final_norm"]), final2=cols(a["final_norm_2"]),
                 knorm=np.concatenate([knorm, knorm])[:, None])
    consts = np.concatenate([np.asarray(parts[n], np.float32) for n in CN], axis=1)
    table = np.concatenate([a["rel_bias_2"].reshape(32, 4, 4)[:, :, slots].reshape(32, 16), np.ones((1, 16), np.float32)])
    even = a["w_in_even_2"][0]
    wi = even[:, 4160:4176].reshape(D, 4, 4)[:, :, slots].reshape(D, 16)
    ki = even[:, 4096:4160]
    arrays = dict(
        xT=a["x"][0].T.reshape(KT, P, S).transpose(1, 0, 2), c=cols(a["c"][0]),
        vec1=np.stack(vec1, axis=1), vec2=np.stack(vec2, axis=1), consts=consts, dist=dist, table=table,
        ada=np.concatenate([chunks(a["ada_w"][l], CH) for l in range(L1)]), w_mix=np.stack(w_mix), w_tok=np.stack(w_tok),
        w_cmp=np.stack([np.stack([pack(a[n][l]) for n in ("cmp_k_w1", "cmp_v_w1")]) for l in range(L1)]),
        w_out=np.stack([halved(a["w_out"][l]) for l in range(L1)]),
        w_gu=np.stack([halved(pairs(a["w_gate_up"][l])) for l in range(L1)]),
        w_dn=np.stack([chunks(a["w_down"][l], P) for l in range(L1)]),
        even_in=halved(even[:, 0:4096]), even_tail=pack(np.concatenate([ki, ki, wi], axis=1)),
        odd_in=halved(a["w_in_odd_2"][0]), w_o2=np.stack([halved(a["w_o_2"][l]) for l in range(2)]),
        w_up2=np.stack([halved(pairs(a["w_up_2"][l])) for l in range(2)]),
        w_dn2=np.stack([chunks(a["w_down_2"][l], P) for l in range(2)]))
    arrays = {n: np.ascontiguousarray(v, dtype=np.float32) for n, v in arrays.items()}
    nc = bacc.Bacc("TRN2", target_bir_lowering=False, num_devices=1)
    args = [nc.dram_tensor(n, v.shape, F32, kind="ExternalInput").ap() for n, v in arrays.items()]
    y = nc.dram_tensor("y", (P, KT, S), F32, kind="ExternalOutput").ap()
    bias_dram = nc.dram_tensor("bias_dram", (2, 16, BIAS_W), F32, kind="Internal").ap()
    bias_wide = nc.dram_tensor("bias_wide", (32, P, BIAS_W), F32, kind="Internal").ap()
    hybrid_then_mixture(nc, *args, y, bias_dram, bias_wide)
    r = run(nc, [arrays], core_ids=[0])
    out = r.results[0]["y"]
    return np.ascontiguousarray(out.transpose(2, 1, 0).reshape(1, S, D))
```

```python
import concourse.bass as bass
from concourse import mybir
from contextlib import ExitStack

F32 = mybir.dt.float32
F32R = mybir.dt.float32r
ALU = mybir.AluOpType
ACT = mybir.ActivationFunctionType
AX = mybir.AxisListType

P = 128
S = 256
QT = S // P
D = 1024
KT = D // P
HD = 64
NG = 4
L1 = 2
DFF = 2816
FT = DFF // P
CH = 512
HALF = KT * CH // 2
AHEAD = 3
ADA_L = 6 * D // CH
ADA = L1 * ADA_L
ADA_FIRST = 2 * D // CH
SLOTS = 3
EPS = 1e-6
SCALE = HD ** -0.5
NEG = -1e30
N_CMP = S // 16 - 1
CMP_PAIRS = 16
GH = 4
GD = 128
NCH = QT * GH
NORM_AHEAD = 3
MIX_EARLY = 6
DEPTH = 3
LEVELS = 7
TAILW = 144
TOKW = 276
GATES, A_COL, B_COL = 256, 268, 272
KQ_BANKS = (4, 5, 6, 3)
MOD_COL = 256
BIAS_W = 384

V1 = dict(norm_mix=(0, 8), norm_ffn=(8, 8), ada_b=(16, 48), conv=(64, 48), gnorm=(112, 128), sink=(240, 4),
          a_log=(244, 4), dt=(248, 4), pe_k=(252, 16), pe_v=(268, 16), w2k=(284, 256), w2v=(540, 128))
V1W = 668
V2 = dict(norm_attn=(0, 8), norm_ffn=(8, 8), conv_w=(16, 132), conv_b=(148, 44))
V2W = 192
CN = dict(ones=(0, 128), final1=(128, 8), final2=(136, 8), knorm=(144, 1), eps=(145, 1), cos=(146, 256), sin=(402, 256),
          ident=(658, 128), rot=(786, 128), halves=(914, 128), upper=(1042, 128), levels=(1170, 896), causal0=(2066, 128),
          band1=(2194, 256), causal1=(2450, 256), cmp_mask=(2706, 30), cmp_valid=(2736, 30))
CNW = 2766
CN_FIRST, V1_FIRST = 146, 64


class Chain:

    def __init__(self, eng, sem):
        self.eng, self.sem, self.n = eng, sem, 0

    def mark(self, ins):
        self.n += 1
        ins.then_inc(self.sem, 1)

    def wait(self):
        self.eng.wait_ge(self.sem, self.n)

    def __call__(self, ins):
        self.mark(ins)
        self.wait()


def hybrid_then_mixture(nc, xT, c, vec1, vec2, consts, dist, table, ada, w_mix, w_tok, w_cmp, w_out, w_gu, w_dn,
                        even_in, even_tail, odd_in, w_o2, w_up2, w_dn2, y, bias_dram,
                        bias_wide):
    phases = {}
    halves = []
    count = dict(chunk=0, event=0, tile=0)
    chunk_end = []
    ada_at = []
    KINDS = dict(columns=((2, 4), (1, 2, 3, 4)), tokens=((1, 3), (2, 3)), rows=((1, 3), (2, 3)),
                 down=((1, 2), (2,)), tail=((1, 4), (2, 3, 4)), compress=((), ()))

    def phase(name, kinds, size=HALF, ada_after=()):
        ph = phases[name] = dict(n0=count["chunk"], e0=count["event"], t0=count["tile"], u0=len(halves), chunks=len(kinds),
                                 at=[], kinds=kinds, tile_event=[])
        for j, kind in enumerate(kinds):
            ends, tiles = KINDS[kind]
            e, n = count["event"], count["chunk"]
            ph["at"].append(n)
            halves.extend((n, part, size, e + end) for part, end in enumerate(ends))
            ph["tile_event"].extend(e + t for t in tiles)
            count["event"] += ends[-1] if ends else 1
            chunk_end.append(("event", count["event"]))
            count["chunk"] += 1
            if j in ada_after:
                ada_chunks(1)
        count["tile"] = ph["t0"] + len(ph["tile_event"])
        ph["u1"] = len(halves)

    def ada_chunks(n):
        for _ in range(n):
            if late_ada(len(ada_at)):
                ada_at.extend([None] * (2 + ADA_FIRST))
            ada_at.append(count["chunk"])
            chunk_end.append(("sums", len(ada_at)))
            count["chunk"] += 1

    def late_ada(m):
        return ADA_L - 2 <= m < ADA_L + ADA_FIRST or m >= ADA - 2

    NEXT_ADA = (1, 3, 5, 7)
    IN_ADA = (2, 4)
    UP, DOWN, OUT = ["columns"] * 11, ["down"] * 8, ["columns"] * 2
    ada_chunks(ADA_FIRST)
    for l in range(L1):
        phase(f"in{l}", ["columns"] * 5 + ["tokens"], ada_after=IN_ADA)
        phase(f"tok{l}", ["rows"], KT * TOKW // 2)
        phase(f"cmp{l}", ["compress"] * 2)
        ada_chunks(4)
        phase(f"out{l}", OUT)
        phase(f"gu{l}", UP)
        phase(f"dn{l}", DOWN, FT * P // 2)
    phase("even", ["columns", "columns", "tokens"] * 2 + ["columns"] * 2)
    phase("tail", ["tail"], KT * TAILW // 2)
    phase("o0", OUT)
    phase("up0", UP)
    phase("down0", DOWN, FT * P // 2)
    phase("odd", ["columns"] * 4 + ["tokens"] * 2)
    phase("o1", OUT)
    phase("up1", UP)
    phase("down1", DOWN, FT * P // 2)
    ada_at.extend([None] * 2)
    ada_alone = [m for m in range(ADA) if ada_at[m] is None]
    late = [u for l in range(L1) for u in range(phases[f"out{l}"]["u0"], phases[f"out{l}"]["u0"] + AHEAD)]

    norm_input = [None, "out0", "dn0", "out1", "dn1", None, "o0", "down0", "o1", "down1"]
    in_place = 4
    split_norms = [n for n in range(len(norm_input) - 1) if n != in_place]
    norm_end = [KT * (n + 1 - (n >= in_place)) for n in range(len(norm_input))]

    ctx = ExitStack()
    with ctx:
        def sb(name, shape):
            return ctx.enter_context(nc.sbuf_tensor(name, shape, F32))

        def sem(name):
            return ctx.enter_context(nc.semaphore(name))

        first_byte = (nc.sbuf_base + 31) // 32 * 32

        ring = sb("ring", [P, SLOTS, KT * CH])
        h = sb("h", [P, KT, S])
        mix = sb("mix", [P, KT, S])
        lg = sb("lg", [P, DEPTH, NG, S])
        arena = sb("arena", [P, 23104])
        sizes = dict(ring=4 * SLOTS * KT * CH, h=4 * KT * S, mix=4 * KT * S, lg=4 * DEPTH * NG * S)
        x = sb("x", [P, KT, S])
        v1 = sb("v1", [P, L1, V1W])
        v2 = sb("v2", [P, 2, V2W])
        cn = sb("cn", [P, CNW])
        c_in = sb("c_in", [P, KT])
        c_silu = sb("c_silu", [P, KT])
        table_sb = sb("table_sb", [33, 16])
        mod = sb("mod", [P, L1, 48])
        gain = sb("gain", [P, L1, 2, KT])
        std = sb("std", [P, S])
        rstd = sb("rstd", [P, S])
        sg = sb("sg", [P, 2, S])
        small = sb("small", [P, 176])
        pT = sb("pT", [P, 2, QT, NG * P])
        negm = sb("negm", [P, DEPTH, NG])
        sums = sb("sums", [P, DEPTH, NG])
        esink = sb("esink", [P, DEPTH, NG])
        rec = sb("rec", [P, DEPTH, NG])
        kcT = sb("kcT", [P, N_CMP])
        vc = sb("vc", [N_CMP, HD])
        hid = sb("hid", [P, 2, 2, N_CMP])

        def split_part(name, place, skip, *shape):
            at = first_byte
            for n, size in sizes.items():
                if n == place:
                    break
                at += size
            return nc.alloc_sbuf_tensor_at(name, [P, *shape], F32R, offset=at + 4 * skip)

        w_lo = split_part("w_lo", "ring", 0, SLOTS, KT * CH)
        h_lo = split_part("h_lo", "h", 0, KT, S)
        mix_lo = split_part("mix_lo", "mix", 0, KT, S)
        hi_T = split_part("hi_T", "lg", 0, KT, S)
        w_hi = split_part("w_hi", "arena", 6656, AHEAD, HALF)
        act_lo = split_part("act_lo", "arena", 0, FT, S)
        act_hi = split_part("act_hi", "arena", 12800, FT, S)

        def view(at, *shape):
            size = 1
            for n in shape:
                size *= n
            flat = arena[:, at:at + size]
            if len(shape) == 1:
                return flat
            if len(shape) == 2:
                return flat.rearrange("p (a b) -> p a b", a=shape[0])
            return flat.rearrange("p (a b c) -> p a b c", a=shape[0], b=shape[1])

        conv_in = view(0, 12, S + 3)
        conv = view(3108, 12, S)
        kn = view(0, NCH, GD)
        kb = view(1024, NCH, GD)
        vb = view(2048, NCH, GD)
        qn = view(3072, NCH, GD)
        kbg = view(4096, GH, GD)
        qd = view(4608, GH, GD)
        kd = view(5120, GH, GD)
        act_T = view(0, FT, S)
        cv = view(FT * S, 2, 2, S)
        tok = view(6656, 3, NCH, GD)
        kbqT = view(6656, NCH, 2, GD)
        knT = view(8704, NCH, GD)
        qdT = view(0, GH, GD)
        Dm = view(10240, NCH, P)
        MT = view(21056, NCH, P)
        QKT = view(1024, NCH, P)
        MbT = view(13312, 2, NCH, P)
        X = view(15360, NCH, P)
        XT = view(16384, NCH, P)
        T1 = view(17408, NCH, P)
        U = view(3072, NCH, GD)
        wT = view(512, GH, P)
        st = view(12800, GH, GD)
        z = view(19456, QT, GH * GD)
        tokp = view(20480, QT, TOKW)
        gB = view(13312, NCH, P)
        sq_tok = view(17408, NCH, GD)
        o_n = view(15360, NCH, GD)
        raw = view(21056, 8, S)
        dist_sb = view(21056, 2, BIAS_W)[0:33]
        tab_rows = view(21824, 2, BIAS_W)[0:16]
        rot = view(14336, 7, S)
        xpe = view(16384, 2, CMP_PAIRS * N_CMP).rearrange("p a (k n) -> p a k n", k=CMP_PAIRS)
        tmp = sg
        acc = view(18432, 2, CH)
        ada_late = view(19008, KT, CH)
        late_sums = pT[:, :, 0, :]
        qk2 = view(0, 25, S)
        vv2 = view(12800, QT, 1024)
        bias2 = view(14912, 2, 16, S)
        wi = view(6400, QT, 16)
        max8 = view(6432, 8)
        rel = mix[:, :, :].rearrange("p (a s) n -> p a s n", a=2)
        score, work, selm = h[:, 0:2, :], h[:, 2:4, :], h[:, 4:6, :]

        bank = ctx.enter_context(nc.psum_tensor("bank", [P, 8, 512], F32))

        def vec(l, name):
            at, n = V1[name]
            return v1[:, l, at:at + n]

        def vec_b(l, name):
            at, n = V2[name]
            return v2[:, l, at:at + n]

        def const(name):
            at, n = CN[name]
            return cn[:, at:at + n]

        ident = const("ident")
        upper = const("upper")

        def over(ap, n):
            return ap.rearrange("p (a m) -> p a m", a=1).to_broadcast([ap.shape[0], n, ap.shape[1]])

        def along(ap, n):
            return ap.rearrange("p (m a) -> p m a", a=1).to_broadcast([ap.shape[0], ap.shape[1], n])

        first_in = sem("first_in")
        consts_in = sem("consts_in")
        tables_in = sem("tables_in")
        vec2_in = sem("vec2_in")
        c_loaded = sem("c_loaded")
        slot_in = [sem(f"slot_in{s}") for s in range(SLOTS)]
        gemm_ready = sem("gemm_ready")
        gemm_freed = sem("gemm_freed")
        c_ready = sem("c_ready")
        x_ready = sem("x_ready")
        acc_ready = sem("acc_ready")
        mod_ready = sem("mod_ready")
        late_in = sem("late_in")
        mod_read = sem("mod_read")
        sq_ready = sem("sq_ready")
        ssq_ready = sem("ssq_ready")
        std_ready = sem("std_ready")
        hn_ready = sem("hn_ready")
        h_hi_ready = sem("h_hi_ready")
        w_hi_ready = sem("w_hi_ready")
        w_lo_ready = sem("w_lo_ready")
        mix_hi_ready = sem("mix_hi_ready")
        mix_ready = sem("mix_ready")
        act_hi_ready = sem("act_hi_ready")
        hidden_ready = sem("hidden_ready")
        h_ready = sem("h_ready")
        rot_ready = sem("rot_ready")
        rope_done = sem("rope_done")
        conv_ready = sem("conv_ready")
        silu_ready = sem("silu_ready")
        xpe_ready = sem("xpe_ready")
        hid_ready = sem("hid_ready")
        kc_ps_ready = sem("kc_ps_ready")
        kc_ready = sem("kc_ready")
        gate_exp = sem("gate_exp")
        gate_arg = sem("gate_arg")
        scores_ready = sem("scores_ready")
        logits_done = sem("logits_done")
        exps_done = sem("exps_done")
        rec_ready = sem("rec_ready")
        probs_ready = sem("probs_ready")
        trans_ready = sem("trans_ready")
        pt_ready = sem("pt_ready")
        pv_done = sem("pv_done")
        o_evac = sem("o_evac")
        gt_ready = sem("gt_ready")
        gt_copied = sem("gt_copied")
        g_arg = sem("g_arg")
        g_fun = sem("g_fun")
        g_ready = sem("g_ready")
        gc_ready = sem("gc_ready")
        scaled = sem("scaled")
        kq_ready = sem("kq_ready")
        mb_ready = sem("mb_ready")
        t1_ready = sem("t1_ready")
        t1_copied = sem("t1_copied")
        dx_ready = sem("dx_ready")
        x_upd = sem("x_upd")
        u_ready = sem("u_ready")
        u_copied = sem("u_copied")
        state_ready = sem("state_ready")
        state_copied = sem("state_copied")
        ws_ready = sem("ws_ready")
        vnew_ready = sem("vnew_ready")
        o_ready = sem("o_ready")
        z_scaled = sem("z_scaled")
        o_std = sem("o_std")
        on_ready = sem("on_ready")
        cv_ready = sem("cv_ready")
        tap_done = sem("tap_done")
        sg_ready = sem("sg_ready")
        act_ready = sem("act_ready")
        tab_ready = sem("tab_ready")
        tab_copied = sem("tab_copied")
        tab_out = sem("tab_out")
        wide_out = sem("wide_out")
        bias_in = sem("bias_in")
        ki_sq = sem("ki_sq")
        ki_ssq = sem("ki_ssq")
        ki_std = sem("ki_std")
        ki_ready = sem("ki_ready")
        ix_ready = sem("ix_ready")
        ix_relu = sem("ix_relu")
        ix_acc = sem("ix_acc")
        y_out = sem("y_out")
        dve_chain = sem("dve_chain")
        act_chain = sem("act_chain")
        pool_chain = sem("pool_chain")

        units = []
        stages = {}

        def stage(name, us):
            stages[name] = (len(units), len(units) + len(us))
            for i, U in enumerate(us):
                U["b"] = (i - len(us)) % DEPTH
            units.extend(us)

        LO, HI = slice(0, HD), slice(HD, P)

        def hybrid_units(l):
            us = []
            for qt in range(QT):
                qs, w = slice(qt * P, qt * P + P), P * (qt + 1)
                rows = [(0, LO), (1, LO), (0, HI), (1, HI)]
                us.append(dict(
                    q=[rot[r, t, qs] for t, r in rows], k=[rot[r, 2, 0:w] for _, r in rows], w=w,
                    bias=over(const("causal0") if qt == 0 else const("band1"), NG), sink=vec(l, "sink"),
                    pv=[(0, 2, lambda kt: tokp[:, kt, 0:HD]), (2, 4, lambda kt: tokp[:, kt, HD:2 * HD])],
                    start=True, end=True, qs=qs, evac=[(0, LO, 0), (1, HI, 0), (2, LO, 1), (3, HI, 1)], gate=None))
            heads = [(0, LO), (1, LO), (0, HI), (1, HI)]
            evac = [(0, LO, 2), (1, LO, 3), (2, HI, 2), (3, HI, 3)]
            for qt in range(QT):
                qs, w = slice(qt * P, qt * P + P), P * (qt + 1)
                causal = over(const("causal0") if qt == 0 else const("causal1"), NG)
                cm = const("cmp_mask")[:, qt * N_CMP:(qt + 1) * N_CMP]
                cval = const("cmp_valid")[:, qt * N_CMP:(qt + 1) * N_CMP]
                gates = [small[:, 16 * qt + NG * b:16 * qt + NG * b + NG] for b in range(3)]
                us.append(dict(
                    q=[raw[r, 3 + t, qs] for t, r in heads], k=[kcT[r, :] for _, r in heads], w=N_CMP,
                    bias=over(cm, NG), valid=over(cval, NG), sink=None, gate=gates[0],
                    pv=[(0, 4, lambda kt: vc[:, :])], start=True, end=False, qs=qs, evac=evac))
                us.append(dict(
                    q=[rot[r, 3 + t, qs] for t, r in heads],
                    k=[rot[r, 5 if r is LO else 6, 0:w] for _, r in heads], w=w,
                    bias=causal, sink=None, gate=gates[1],
                    pv=[(0, 4, lambda kt: tokp[:, kt, 2 * HD:3 * HD])], start=False, end=False, qs=qs, evac=evac))
                us.append(dict(
                    q=[rot[r, 3 + t, qs] for t, r in heads],
                    k=[rot[r, 6 if r is LO else 5, 0:w] for _, r in heads], w=w,
                    bias=causal, sink=None, gate=gates[2],
                    pv=[(0, 4, lambda kt: tokp[:, kt, 3 * HD:4 * HD])], start=False, end=True, qs=qs, evac=evac))
            return us

        def biased_units(q0, k0, v0, groups, bset, g0, sel):
            us = []
            for g in range(groups):
                for qt in range(QT):
                    qs, w = slice(qt * P, qt * P + P), P * (qt + 1)
                    rows = [(0, LO), (1, LO), (0, HI), (1, HI)]
                    head = [0, 2, 1, 3]
                    us.append(dict(
                        q=[qk2[r, q0 + 2 * g + t, qs] for t, r in rows],
                        k=[qk2[r, k0 + 2 * g + t, 0:w] for t, r in rows], w=w,
                        bias=bias2[:, bset, NG * (g0 + g):NG * (g0 + g) + NG, S - w:S], sink=None, gate=None,
                        sel=over(selm[:, qt, 0:w], NG) if sel else None,
                        pv=[(s, s + 1, (lambda at: lambda kt: vv2[:, kt, at:at + HD])(v0 + HD * (NG * g + head[s])))
                            for s in range(NG)],
                        start=True, end=True, qs=qs,
                        evac=[(0, LO, 2 * (g0 + g)), (1, LO, 2 * (g0 + g) + 1),
                              (2, HI, 2 * (g0 + g)), (3, HI, 2 * (g0 + g) + 1)]))
            return us

        for l in range(L1):
            stage(f"hybrid{l}", hybrid_units(l))
        stage("even", biased_units(0, 4, 0, 2, 0, 0, False) + biased_units(8, 12, 512, 2, 0, 2, True))
        stage("odd", biased_units(0, 8, 0, 4, 1, 0, False))

        def evacs_before(u):
            return sum(units[i]["end"] for i in range(u))

        def key_tiles(u):
            w = units[u]["w"]
            return [(kt, min(P, w - kt * P)) for kt in range((w + P - 1) // P)]

        block = ctx.enter_context(nc.Block())

        @block.sync
        def _(sp):
            sp.dma_start(c_in[:, :], c).then_inc(c_loaded, 16)

            def load(n, src, size):
                if n >= SLOTS:
                    kind, value = chunk_end[n - SLOTS]
                    sp.wait_ge(gemm_ready if kind == "event" else acc_ready, value)
                sp.dma_start(ring[:, n % SLOTS, 0:size], src).then_inc(slot_in[n % SLOTS], 16)

            def load_phase(name, src, per_chunk, size):
                ph = phases[name]
                n0, e0, chunks = ph["n0"], ph["e0"], ph["chunks"]
                turns = (chunks - SLOTS) // SLOTS if per_chunk else 0
                for j in range(min(SLOTS, chunks)):
                    load(n0 + j, src[j], size)
                if turns > 1:
                    with sp.Fori(0, turns) as i:
                        for j in range(SLOTS):
                            sp.wait_ge(gemm_ready, i * (SLOTS * per_chunk) + e0 + per_chunk * (j + 1))
                            sp.dma_start(ring[:, (n0 + j) % SLOTS, 0:size].rearrange("p (a n) -> p a n", a=1),
                                         src[bass.ds(i * SLOTS + SLOTS + j, 1)].rearrange("a p n -> p a n"))\
                                .then_inc(slot_in[(n0 + j) % SLOTS], 16)
                    done = SLOTS * (turns + 1)
                else:
                    done = min(SLOTS, chunks)
                for j in range(done, chunks):
                    load(n0 + j, src[j], size)

            full = KT * CH

            def load_ada(m):
                load(ada_at[m], ada[m], full)

            for l in range(L1):
                if l == 0:
                    for dst, src in ((dist_sb[:, :, :], dist), (table_sb[:, :], table)):
                        sp.dma_start(dst, src).then_inc(tables_in, 16)
                    load_ada(0)
                    load_ada(1)
                    for dst, src in ((x[:, :, :], xT), (cn[:, 0:CN_FIRST], consts[:, 0:CN_FIRST]),
                                     (v1[:, :, 0:V1_FIRST], vec1[:, :, 0:V1_FIRST])):
                        sp.dma_start(dst, src).then_inc(first_in, 16)
                    for m in range(2, ADA_FIRST):
                        load_ada(m)
                m = ADA_L * l + ADA_FIRST
                for j, at in enumerate(phases[f"in{l}"]["at"]):
                    load(at, w_mix[l][j], full)
                    if l == j == 0:
                        for dst, src in ((cn[:, CN_FIRST:CNW], consts[:, CN_FIRST:CNW]),
                                         (v1[:, :, V1_FIRST:V1W], vec1[:, :, V1_FIRST:V1W])):
                            sp.dma_start(dst, src).then_inc(consts_in, 16)
                    if j in IN_ADA:
                        load_ada(m + IN_ADA.index(j))
                load(phases[f"tok{l}"]["n0"], w_tok[l], KT * TOKW)
                load_phase(f"cmp{l}", w_cmp[l], 0, full)
                for j in range(2, 6):
                    load_ada(m + j)
                if l == 0:
                    sp.dma_start(v2[:, :, :], vec2).then_inc(vec2_in, 16)
                    sp.wait_ge(tab_out, 16)
                    sp.dma_start(bias_wide, bass.AP(tensor=bias_dram.tensor, offset=0,
                                                    ap=[[BIAS_W, 32], [0, P], [1, BIAS_W]])).then_inc(wide_out, 16)
                load_phase(f"out{l}", w_out[l], 0, full)
                load_phase(f"gu{l}", w_gu[l], 4, full)
                load_phase(f"dn{l}", w_dn[l], 2, FT * P)
            for j in range(SLOTS):
                load(phases["even"]["n0"] + j, even_in[j], full)
            sp.wait_ge(wide_out, 16)
            sp.wait_ge(gemm_freed, phases["even"]["t0"])
            for a in range(2):
                skewed = bass.AP(tensor=bias_wide.tensor, offset=a * 16 * P * BIAS_W + P - 1,
                                 ap=[[BIAS_W - 1, P], [P * BIAS_W, 16], [1, S]])
                sp.dma_start(bias2[:, a, :, :], skewed).then_inc(bias_in, 16)
            for j in range(SLOTS, phases["even"]["chunks"]):
                load(phases["even"]["n0"] + j, even_in[j], full)
            load(phases["tail"]["n0"], even_tail, KT * TAILW)
            load_phase("o0", w_o2[0], 0, full)
            load_phase("up0", w_up2[0], 4, full)
            load_phase("down0", w_dn2[0], 2, FT * P)
            load_phase("odd", odd_in, 0, full)
            load_phase("o1", w_o2[1], 0, full)
            load_phase("up1", w_up2[1], 4, full)
            load_phase("down1", w_dn2[1], 2, FT * P)
            sp.wait_ge(h_ready, norm_end[-1])
            sp.dma_start(y, h[:, :, :]).then_inc(y_out, 16)
            sp.wait_ge(y_out, 16)

        @block.tensor
        def _(pe):
            def chunk_in(n):
                pe.wait_ge(slot_in[n % SLOTS], 16 * (n // SLOTS + 1))

            def tile_free(name, j):
                t0 = phases[name]["t0"]
                if name.startswith("tok"):
                    pe.wait_ge(gemm_freed, t0 + j - 3)
                elif j >= 4:
                    pe.wait_ge(gemm_freed, t0 + j - 3)
                elif j == 0 and t0:
                    pe.wait_ge(gemm_freed, t0)

            def split_half(u, cols):
                n, part, size, _ = halves[u]
                hi = w_hi[:, u % AHEAD, 0:size].rearrange("p (k n) -> p k n", n=cols)
                lo = w_lo[:, n % SLOTS, part * size:(part + 1) * size].rearrange("p (k n) -> p k n", n=cols)
                return hi, lo

            def half_in(u):
                pe.wait_ge(w_lo_ready, u + 1)

            def three(out, w_parts, x_parts, start, stop):
                (wh, wl), (xh, xl) = w_parts, x_parts
                nc.tensor.matmul(out, wh, xh, start=start, stop=False)
                nc.tensor.matmul(out, wh, xl, start=False, stop=False)
                return nc.tensor.matmul(out, wl, xh, start=False, stop=stop)

            def channel_tile(out, w, col, src, k0=0, ks=KT):
                (wh, wl), (xh, xl) = w, src
                for k in range(ks):
                    last = three(out, (wh[:, k, col:col + P], wl[:, k, col:col + P]), (xh[:, k0 + k, :], xl[:, k0 + k, :]),
                                 k0 + k == 0, k0 + k == KT - 1)
                return last

            def normalised(first):
                def wait(k):
                    pe.wait_ge(h_ready, first + k + 1)
                return wait

            def mixed(done):
                def wait(k):
                    if k in (0, MIX_EARLY):
                        pe.wait_ge(mix_ready, done + (k > 0))
                return wait

            def first_tiles(w, src, ready):
                (wh, wl), (xh, xl) = w, src
                for k in range(KT):
                    ready(k)
                    for m in range(2):
                        cs = slice(m * P, m * P + P)
                        last = three(bank[:, m, 0:S], (wh[:, k, cs], wl[:, k, cs]), (xh[:, k, :], xl[:, k, :]),
                                     k == 0, k == KT - 1)
                        if k == KT - 1:
                            last.then_inc(gemm_ready, 1)

            def token_tile(out, w, lo, hi, src, qt, k0=0, ks=KT):
                (wh, wl), (xh, xl) = w, src
                qs = slice(qt * P, qt * P + P)
                for k in range(ks):
                    last = three(out, (xh[:, k0 + k, qs], xl[:, k0 + k, qs]), (wh[:, k, lo:hi], wl[:, k, lo:hi]),
                                 k0 + k == 0, k0 + k == KT - 1)
                return last

            def columns_chunk(name, nn, j, src, ready=None, after=None):
                for part in range(2):
                    u = phases[name]["u0"] + 2 * nn + part
                    half_in(u)
                    w = split_half(u, CH // 2)
                    if ready and j + part == 0:
                        tile_free(name, 0)
                        first_tiles(w, src, ready)
                        continue
                    for m in range(2):
                        t = j + 2 * part + m
                        tile_free(name, t)
                        channel_tile(bank[:, t % 4, 0:S], w, m * P, src).then_inc(gemm_ready, 1)
                        if after:
                            after(t)

            def tokens_chunk(name, nn, j):
                for part in range(2):
                    u = phases[name]["u0"] + 2 * nn + part
                    half_in(u)
                    w = split_half(u, CH // 2)
                    for qt in range(QT):
                        if part == 0:
                            tile_free(name, j + qt)
                        last = token_tile(bank[:, (j + qt) % 4, CH // 2 * part:CH // 2 * (part + 1)], w, 0, CH // 2,
                                          (hi_T, h_lo), qt)
                        if part == 1 or qt == QT - 1:
                            last.then_inc(gemm_ready, 1)

            def norm_sums(n):
                for k in range(KT):
                    if k % 2 == 0:
                        pe.wait_ge(sq_ready, 4 * n + k // 2 + 1)
                    last = nc.tensor.matmul(bank[:, 7, 0:S], const("ones"), h[:, k, :],
                                            start=(k == 0), stop=(k == KT - 1))
                last.then_inc(ssq_ready, 1)

            def modulations(m0, m1):
                for m in range(m0, m1):
                    pe.wait_ge(acc_ready, m + 1)
                    for t in range(4):
                        at = MOD_COL + 4 * m + t
                        sums_m = acc[:, m % 2, :] if ada_at[m] is not None else late_sums[:, m % 2, :]
                        last = nc.tensor.matmul(bank[:, 7, at:at + 1], sums_m[:, t * P:t * P + P],
                                                const("ones")[:, 0:1], start=True, stop=True)
                    last.then_inc(mod_ready, 1)

            def attention(name, m_next=None):
                u0, u1 = stages[name]

                def scores(u):
                    U = units[u]
                    if u >= 2:
                        pe.wait_ge(logits_done, u - 1)
                    for s in range(NG):
                        last = nc.tensor.matmul(bank[:, 2 * (u % 2) + s // 2, (s % 2) * S:(s % 2) * S + U["w"]],
                                                U["q"][s], U["k"][s], start=True, stop=True)
                    last.then_inc(scores_ready, 1)

                def transposes(u):
                    pe.wait_ge(probs_ready, u + 1)
                    if u >= 1:
                        pe.wait_ge(pt_ready, u)
                    for kt, n in key_tiles(u):
                        for s in range(NG):
                            last = nc.tensor.transpose(bank[0:n, 4 + kt, s * P:s * P + P],
                                                       lg[:, units[u]["b"], s, kt * P:kt * P + n], ident)
                    last.then_inc(trans_ready, 1)

                def values(u):
                    U = units[u]
                    pe.wait_ge(pt_ready, u + 1)
                    if U["start"] and evacs_before(u):
                        pe.wait_ge(o_evac, evacs_before(u))
                    tiles = key_tiles(u)
                    for lo, hi, v in U["pv"]:
                        for kt, n in tiles:
                            last = nc.tensor.matmul(
                                bank[0:HD, 6, lo * P:hi * P], v(kt), pT[0:n, u % 2, kt, lo * P:hi * P],
                                start=U["start"] and kt == 0, stop=U["end"] and kt == tiles[-1][0])
                    last.then_inc(pv_done, 1)

                for u in range(u0, u0 + DEPTH):
                    scores(u)
                for u in range(u0, u1):
                    if m_next and u == u0 + 2:
                        modulations(m_next, m_next + 1)
                    transposes(u)
                    if u + DEPTH < u1:
                        scores(u + DEPTH)
                    values(u)

            def group(l, j, srcs):
                if j >= 4:
                    pe.wait_ge(gt_copied, 13 * l + min(j - 3, 13))
                for i, src in enumerate(srcs):
                    last = nc.tensor.transpose(bank[:, j % 4, i * P:i * P + P], src, ident)
                last.then_inc(gt_ready, 1)

            def token_major(l, j0, j1):
                pe.wait_ge(silu_ready, 3 * (l + 1))
                for j in range(j0, j1):
                    group(l, j, [conv[:, 4 * (j // 2) + hd, (j % 2) * P:(j % 2) * P + P] for hd in range(GH)])

            def log_decays(l):
                pe.wait_ge(g_ready, l + 1)
                pe.wait_ge(gt_copied, 13 * l + 4)
                pe.wait_ge(rope_done, 7 * (l + 1))
                nc.tensor.matmul(bank[:, 3, 0:NCH], upper, small[:, 96:96 + NCH], start=True, stop=True)
                for ch in range(NCH):
                    last = nc.tensor.matmul(bank[:, 4 + ch // 4, (ch % 4) * P:(ch % 4) * P + P], gB[:, ch, :], upper,
                                            start=True, stop=True)
                last.then_inc(gc_ready, 1)

            def delta_net(l, m_next):
                u_end = stages[f"hybrid{l}"][1]
                pe.wait_ge(logits_done, u_end)
                pe.wait_ge(pt_ready, u_end)
                pe.wait_ge(o_evac, evacs_before(u_end))
                pe.wait_ge(scaled, l + 1)
                lists = [[kb[:, 4 * cc + i, :] for i in range(4)] for cc in range(2)] \
                    + [[kn[:, 4 * cc + i, :] for i in range(4)] for cc in range(2)] \
                    + [[qn[:, 4 * cc + i, :] for i in range(4)] for cc in range(2)] + [[qd[:, i, :] for i in range(4)]]
                for j, srcs in enumerate(lists):
                    group(l, 6 + j, srcs)
                pe.wait_ge(gt_copied, 13 * (l + 1))
                for ch in range(NCH):
                    last = nc.tensor.matmul(bank[:, KQ_BANKS[ch // 2], (ch % 2) * S:(ch % 2) * S + S], knT[:, ch, :],
                                            kbqT[:, ch, :, :].rearrange("p a n -> p (a n)"), start=True, stop=True)
                    if ch % 2:
                        last.then_inc(kq_ready, 1)
                for lv in range(LEVELS):
                    if lv == 3:
                        modulations(m_next, m_next + 1)
                    pe.wait_ge(mb_ready, l * LEVELS + lv + 1)
                    for half in range(2):
                        if lv:
                            pe.wait_ge(x_upd, l * 2 * LEVELS + 2 * (lv - 1) + half + 1)
                        for i in range(4):
                            ch = 4 * half + i
                            last = nc.tensor.matmul(bank[:, half, i * P:i * P + P], MbT[:, lv % 2, ch, :],
                                                    X[:, ch, :] if lv else ident, start=True, stop=True)
                        last.then_inc(t1_ready, 1)
                    for half in range(2 if lv else 0):
                        pe.wait_ge(t1_copied, l * 2 * (LEVELS - 1) + 2 * (lv - 1) + half + 1)
                        for i in range(4):
                            ch = 4 * half + i
                            if lv < LEVELS - 1:
                                nc.tensor.matmul(bank[:, 2 + half, i * P:i * P + P], XT[:, ch, :], T1[:, ch, :],
                                                 start=True, stop=True)
                            last = nc.tensor.matmul(bank[:, 4 + half, i * P:i * P + P], T1[:, ch, :], XT[:, ch, :],
                                                    start=True, stop=True)
                        last.then_inc(dx_ready, 1)
                pe.wait_ge(x_upd, (l + 1) * 2 * LEVELS)
                for ch in range(NCH):
                    nc.tensor.matmul(bank[:, ch // 4, (ch % 4) * P:(ch % 4) * P + P], XT[:, ch, :], vb[:, ch, :],
                                     start=True, stop=True)
                for i in range(GH):
                    last = nc.tensor.matmul(bank[:, 2, i * P:i * P + P], kbg[:, i, :], XT[:, GH + i, :],
                                            start=True, stop=True)
                last.then_inc(u_ready, 1)
                pe.wait_ge(u_copied, l + 1)
                for i in range(GH):
                    last = nc.tensor.matmul(bank[:, 3, i * P:i * P + P], kd[:, i, :], U[:, i, :], start=True, stop=True)
                last.then_inc(state_ready, 1)
                for i in range(GH):
                    last = nc.tensor.matmul(bank[:, 4, i * P:i * P + P], QKT[:, i, :], U[:, i, :], start=True, stop=True)
                last.then_inc(o_ready, 1)
                pe.wait_ge(state_copied, l + 1)
                for i in range(GH):
                    last = nc.tensor.matmul(bank[:, 5, i * P:i * P + P], wT[:, i, :], st[:, i, :], start=True, stop=True)
                last.then_inc(ws_ready, 1)
                pe.wait_ge(vnew_ready, l + 1)
                for i in range(GH):
                    nc.tensor.matmul(bank[:, 6, i * P:i * P + P], qdT[:, i, :], st[:, i, :], start=True, stop=False)
                    last = nc.tensor.matmul(bank[:, 6, i * P:i * P + P], QKT[:, GH + i, :], U[:, GH + i, :],
                                            start=False, stop=True)
                last.then_inc(o_ready, 1)
                modulations(m_next + 1, m_next + 2)
                for cc in range(2):
                    pe.wait_ge(on_ready, 2 * l + cc + 1)
                    group(l, 13 + cc, [o_n[:, GH * cc + i, :] for i in range(GH)])

            def projection(name, done, ready=None):
                if ready is None:
                    pe.wait_ge(mix_ready, done)
                for nn in range(2):
                    columns_chunk(name, nn, 4 * nn, (hi_T, mix_lo), ready)

            def up(name, first, m_next=None):
                ph = phases[name]
                u0, t0 = ph["u0"], ph["t0"]

                def one(j, split, free):
                    for part in range(2):
                        pe.wait_ge(w_lo_ready, split + part)
                        w = split_half(u0 + 2 * j + part, CH // 2)
                        if j + part == 0:
                            pe.wait_ge(gemm_freed, free + 1)
                            first_tiles(w, (hi_T, h_lo), normalised(first))
                            continue
                        for m in range(2):
                            pe.wait_ge(gemm_freed, free + 2 * part + m)
                            channel_tile(bank[:, 2 * part + m, 0:S], w, m * P, (hi_T, h_lo)).then_inc(gemm_ready, 1)

                turns = 11 // SLOTS
                pe.wait_ge(gemm_freed, t0)
                with pe.Fori(0, turns) as i:
                    for j in range(SLOTS):
                        one(j, i * (2 * SLOTS) + u0 + 2 * j + 1, i * (4 * SLOTS) + t0 + 4 * j - 3)
                for j in range(SLOTS * turns, 11):
                    if m_next and j == SLOTS * turns:
                        modulations(m_next, m_next + 1)
                    one(j, u0 + 2 * j + 1, t0 + 4 * j - 3)

            def down(name, done):
                ph = phases[name]
                for j in range(KT):
                    if name == "dn0" and j in NEXT_ADA:
                        m = ADA_L + NEXT_ADA.index(j)
                        if m == ADA_L:
                            pe.wait_ge(mod_read, 2)
                        modulations(m, m + 1)
                    if j >= 3:
                        pe.wait_ge(gemm_freed, ph["t0"] + j - 2)
                    for part in range(2):
                        if j == 0:
                            pe.wait_ge(hidden_ready, done - (5 if part == 0 else 0))
                        u = ph["u0"] + 2 * j + part
                        half_in(u)
                        wh, wl = split_half(u, P)
                        for k in range(FT // 2):
                            kk = FT // 2 * part + k
                            last = three(bank[:, 4 + j % 3, 0:S], (wh[:, k, :], wl[:, k, :]),
                                         (act_hi[:, kk, :], act_lo[:, kk, :]), kk == 0, kk == FT - 1)
                        last.then_inc(gemm_ready, 1)

            pe.wait_ge(tables_in, 16 * 2)
            for a in range(2):
                last = nc.tensor.matmul(bank[0:16, a, 0:BIAS_W], table_sb[:, :], dist_sb[:, a, :], start=True, stop=True)
            last.then_inc(tab_ready, 1)
            pe.wait_ge(first_in, 16 * 3)
            norm_sums(0)
            pe.wait_ge(std_ready, 1)
            modulations(0, ADA_FIRST)
            n = 0
            for l in range(L1):
                if l:
                    pe.wait_ge(mod_read, 4)
                    norm_sums(n)
                pe.wait_ge(tab_copied, 2)
                ph = phases[f"in{l}"]
                m = ADA_L * l + ADA_FIRST

                def rotate(j):
                    if 8 <= j < 14:
                        t = j - 8
                        pe.wait_ge(gemm_freed, ph["t0"] + t + 1)
                        if t >= 2:
                            pe.wait_ge(rope_done, 7 * l + t - 1)
                        nc.tensor.matmul(bank[:, 4 + t % 2, 0:S], const("rot"), raw[:, t, :], start=True, stop=True)\
                            .then_inc(rot_ready, 1)

                for nn in range(5):
                    if l == 0 and nn == 2:
                        pe.wait_ge(consts_in, 16 * 2)
                    columns_chunk(f"in{l}", nn, 4 * nn, (hi_T, h_lo), normalised(norm_end[n] - KT), rotate)
                modulations(m, m + 1)
                tokens_chunk(f"in{l}", 5, 20)
                for qt in range(QT):
                    tile_free(f"tok{l}", qt)
                for part in range(2):
                    u = phases[f"tok{l}"]["u0"] + part
                    half_in(u)
                    for qt in range(QT):
                        last = token_tile(bank[:, (22 + qt) % 4, 0:TOKW], split_half(u, TOKW), 0, TOKW, (hi_T, h_lo), qt,
                                          KT // 2 * part, KT // 2)
                        if part == 1 or qt == QT - 1:
                            last.then_inc(gemm_ready, 1)
                modulations(m + 1, m + 2)
                pe.wait_ge(gemm_freed, phases[f"out{l}"]["t0"])
                token_major(l, 0, 4)
                pe.wait_ge(xpe_ready, 2 * (l + 1))
                for kv in range(2):
                    nn = phases[f"cmp{l}"]["n0"] + kv
                    chunk_in(nn)
                    w = ring[:, nn % SLOTS, :].rearrange("p (k n) -> p k n", k=CMP_PAIRS)
                    for ht in range(2):
                        at = (2 * kv + ht) * 16
                        for k in range(CMP_PAIRS):
                            last = nc.tensor.matmul(bank[:, 7, at:at + N_CMP], w[:, k, ht * P:ht * P + P],
                                                    xpe[:, kv, k, :], start=(k == 0), stop=(k == CMP_PAIRS - 1))
                    last.then_inc(gemm_ready, 1)
                    if kv == 0:
                        token_major(l, 4, 6)
                        log_decays(l)
                pe.wait_ge(hid_ready, l + 1)
                w2k = vec(l, "w2k").rearrange("p (a n) -> p a n", a=2)
                w2v = vec(l, "w2v").rearrange("p (a n) -> p a n", a=2)
                for ht in range(2):
                    nc.tensor.matmul(bank[:, 6, 0:N_CMP], w2k[:, ht, :], hid[:, 0, ht, :], start=(ht == 0), stop=(ht == 1))
                for ht in range(2):
                    last = nc.tensor.matmul(bank[0:N_CMP, 6, 64:64 + HD], hid[:, 1, ht, :], w2v[:, ht, :],
                                            start=(ht == 0), stop=(ht == 1))
                last.then_inc(kc_ps_ready, 1)
                modulations(m + 2, m + 3)
                pe.wait_ge(kc_ready, l + 1)
                pe.wait_ge(gt_copied, 13 * l + 6)
                pe.wait_ge(g_arg, 4 * l + 4)
                attention(f"hybrid{l}", m + 3)
                delta_net(l, m + 4)
                projection(f"out{l}", 3 * (l + 1))
                norm_sums(n + 1)
                pe.wait_ge(std_ready, n + 2)
                modulations(m + 6, m + 7)
                up(f"gu{l}", norm_end[n + 1] - KT, m + 7)
                down(f"dn{l}", 11 * (l + 1))
                n += 2
            norm_sums(n)
            n += 1
            for l, name in enumerate(("even", "odd")):
                norm_sums(n)
                j = 0
                for nn, kind in enumerate(phases[name]["kinds"]):
                    if kind == "tokens":
                        tokens_chunk(name, nn, j)
                        j += 2
                    else:
                        columns_chunk(name, nn, j, (hi_T, h_lo), normalised(norm_end[n] - KT))
                        j += 4
                if l == 0:
                    tile_free("tail", 0)
                    for part in range(2):
                        u = phases["tail"]["u0"] + part
                        half_in(u)
                        w = split_half(u, TAILW)
                        last = channel_tile(bank[:, 0, 0:S], w, 0, (hi_T, h_lo), KT // 2 * part, KT // 2)
                        if part == 1:
                            last.then_inc(gemm_ready, 1)
                        for qt in range(QT):
                            last = token_tile(bank[:, 1 + qt, 0:16], w, P, P + 16, (hi_T, h_lo), qt, KT // 2 * part, KT // 2)
                            if part == 1 or qt == QT - 1:
                                last.then_inc(gemm_ready, 1)
                    pe.wait_ge(ki_sq, 1)
                    nc.tensor.matmul(bank[:, 7, 0:S], const("halves"), tmp[:, 0, :], start=True, stop=True)\
                        .then_inc(ki_ssq, 1)
                    pe.wait_ge(ki_ready, 1)
                    pe.wait_ge(gemm_freed, phases["o0"]["t0"])
                    for i in range(QT * 4):
                        qt, g = i // 4, i % 4
                        if i >= 2:
                            pe.wait_ge(ix_relu, i - 1)
                        for s in range(NG):
                            r = LO if s < 2 else HI
                            last = nc.tensor.matmul(
                                bank[:, 2 * (i % 2) + s // 2, (s % 2) * S:(s % 2) * S + P * (qt + 1)],
                                qk2[r, 16 + 2 * g + s % 2, qt * P:qt * P + P], qk2[r, 24, 0:P * (qt + 1)],
                                start=True, stop=True)
                        last.then_inc(ix_ready, 1)
                    pe.wait_ge(ix_relu, QT * 4)
                else:
                    pe.wait_ge(gemm_freed, phases["o1"]["t0"])
                attention(name)
                projection(f"o{l}", 3 * L1 + 2 * (l + 1), mixed(3 * L1 + 2 * l + 1))
                norm_sums(n + 1)
                up(f"up{l}", norm_end[n + 1] - KT)
                down(f"down{l}", 11 * (L1 + l + 1))
                n += 2
            norm_sums(n)

        @block.scalar
        def _(act):
            ch = Chain(act, act_chain)

            def norm_squares(n):
                ph = phases[norm_input[n]] if norm_input[n] else None
                for j in range(4):
                    if ph:
                        each = (ph["u1"] - ph["u0"]) // 4
                        ahead = [ph["u0"] + each * j + i + AHEAD for i in range(each)]
                        for u in ahead if j < 3 else ahead[:-1]:
                            high(u)
                        act.wait_ge(gemm_freed, ph["t0"] + 2 * j + 2)
                    elif n:
                        act.wait_ge(x_ready, 2 * j + 2)
                    nc.scalar.activation(h[:, 2 * j:2 * j + 2, :], x[:, 2 * j:2 * j + 2, :], ACT.Square)\
                        .then_inc(sq_ready, 1)
                act.wait_ge(ssq_ready, n + 1)
                nc.scalar.activation(std[:, :], bank[:, 7, 0:S], ACT.Sqrt, bias=const("eps"), scale=1.0 / D)\
                    .then_inc(std_ready, 1)
                if ph:
                    high(ahead[-1])

            def norm_high(n, shift=None):
                for k in range(KT):
                    act.wait_ge(hn_ready, KT * split_norms.index(n) + k + 1)
                    if shift is None:
                        ins = nc.scalar.activation(hi_T[:, k, :], h[:, k, :], ACT.Copy)
                    else:
                        ins = nc.scalar.activation(hi_T[:, k, :], h[:, k, :], ACT.Identity, bias=shift[:, k:k + 1])
                    ins.then_inc(h_hi_ready, 1)

            def high(u, turn=None, late_now=False):
                if u >= len(halves) or (u in late and not late_now):
                    return
                n, part, size, _ = halves[u]
                slot, arrived = n % SLOTS, 16 * (n // SLOTS + 1)
                if part == 0:
                    act.wait_ge(slot_in[slot], arrived if turn is None else turn * 16 + arrived)
                if u >= AHEAD:
                    used = halves[u - AHEAD][3]
                    act.wait_ge(gemm_ready, used if turn is None else turn * (4 * SLOTS) + used)
                nc.scalar.activation(w_hi[:, u % AHEAD, 0:size], ring[:, slot, part * size:(part + 1) * size], ACT.Copy)\
                    .then_inc(w_hi_ready, 1)

            def late_high(l, u0, u1):
                for u in range(u0, u1):
                    high(phases[f"out{l}"]["u0"] + u, late_now=True)

            def take(name, j, dst, src, func=ACT.Copy):
                act.wait_ge(gemm_ready, phases[name]["tile_event"][j])
                nc.scalar.activation(dst, src, func).then_inc(gemm_freed, 1)

            def attention(name, before_last=None):
                u0, u1 = stages[name]

                def exps(u):
                    U, b = units[u], units[u]["b"]
                    act.wait_ge(logits_done, u + 1)
                    for s in range(NG):
                        last = nc.scalar.activation(lg[:, b, s, 0:U["w"]], lg[:, b, s, 0:U["w"]], ACT.Exp,
                                                    bias=negm[:, b, s:s + 1], accum_out=sums[:, b, s:s + 1])
                    if U["sink"] is not None:
                        last = nc.scalar.activation(esink[:, b, :], esink[:, b, :], ACT.Exp)
                    last.then_inc(exps_done, 1)

                def copy_pt(u):
                    act.wait_ge(trans_ready, u + 1)
                    if u >= 2:
                        act.wait_ge(pv_done, u - 1)
                    for kt, m in key_tiles(u):
                        last = nc.scalar.activation(pT[0:m, u % 2, kt, :], bank[0:m, 4 + kt, :], ACT.Copy)
                    last.then_inc(pt_ready, 1)

                exps(u0)
                exps(u0 + 1)
                for u in range(u0, u1):
                    if before_last and u == u1 - 1:
                        before_last()
                    copy_pt(u)
                    if u + 2 < u1:
                        exps(u + 2)

            def group(l, j, dst):
                act.wait_ge(gt_ready, 15 * l + j + 1)
                nc.scalar.activation(dst, bank[:, j % 4, :].rearrange("p (a n) -> p a n", a=4), ACT.Copy)\
                    .then_inc(gt_copied, 1)

            def token_major(l, j0, j1):
                for j in range(j0, j1):
                    group(l, j, tok[:, j // 2, GH * (j % 2):GH * (j % 2) + GH, :])

            def softplus(l):
                token_major(l, 0, 2)
                act.wait_ge(g_arg, 4 * l + 1)
                nc.scalar.activation(small[:, 64:64 + NCH], small[:, 64:64 + NCH], ACT.Exp)
                nc.scalar.activation(small[:, 88:92], vec(l, "a_log"), ACT.Exp).then_inc(g_fun, 1)
                token_major(l, 2, 4)
                act.wait_ge(g_arg, 4 * l + 2)
                nc.scalar.activation(small[:, 64:64 + NCH], small[:, 64:64 + NCH], ACT.Ln).then_inc(g_fun, 1)
                token_major(l, 4, 6)

            def decays(l):
                act.wait_ge(g_arg, 4 * l + 3)
                nc.scalar.activation(small[:, 128:144], small[:, 128:144], ACT.Sqrt, bias=const("eps")).then_inc(g_fun, 1)
                act.wait_ge(g_arg, 4 * l + 4)
                nc.scalar.activation(Dm, Dm, ACT.Exp)
                nc.scalar.activation(small[:, 112:112 + NCH], small[:, 104:104 + NCH], ACT.Exp)
                nc.scalar.activation(small[:, 120:120 + NCH], small[:, 120:120 + NCH], ACT.Exp).then_inc(g_fun, 1)

            def delta_net(l):
                act.wait_ge(o_evac, evacs_before(stages[f"hybrid{l}"][1]))
                nc.scalar.activation(hi_T[:, 0:4, :], mix[:, 0:4, :], ACT.Copy).then_inc(mix_hi_ready, 1)
                for cc in range(2):
                    group(l, 6 + cc, kbqT[:, GH * cc:GH * cc + GH, 0, :])
                for cc in range(2):
                    group(l, 8 + cc, knT[:, GH * cc:GH * cc + GH, :])
                for cc in range(2):
                    group(l, 10 + cc, kbqT[:, GH * cc:GH * cc + GH, 1, :])
                group(l, 12, qdT)
                act.wait_ge(mb_ready, l * LEVELS + 1)
                late_high(l, 0, 2)
                for lv in range(1, LEVELS):
                    for half in range(2):
                        act.wait_ge(t1_ready, l * 2 * LEVELS + 2 * lv + half + 1)
                        nc.scalar.activation(T1[:, 4 * half:4 * half + 4, :],
                                             bank[:, half, :].rearrange("p (a n) -> p a n", a=4), ACT.Copy)\
                            .then_inc(t1_copied, 1)
                late_high(l, 2, AHEAD)
                act.wait_ge(u_ready, l + 1)
                for half in range(2):
                    nc.scalar.activation(U[:, 4 * half:4 * half + 4, :],
                                         bank[:, half, :].rearrange("p (a n) -> p a n", a=4), ACT.Copy)
                nc.scalar.activation(wT, bank[:, 2, :].rearrange("p (a n) -> p a n", a=4), ACT.Copy).then_inc(u_copied, 1)
                act.wait_ge(state_ready, l + 1)
                nc.scalar.activation(st, bank[:, 3, :].rearrange("p (a n) -> p a n", a=4), ACT.Copy)\
                    .then_inc(state_copied, 1)
                for cc in range(2):
                    act.wait_ge(o_ready, 2 * l + cc + 1)
                    for i in range(GH):
                        at = GH * cc + i
                        ch.mark(nc.scalar.activation(sq_tok[:, at, :], bank[:, 4 + 2 * cc, i * P:i * P + P], ACT.Square,
                                                     accum_out=small[:, 144 + at:145 + at]))
                    ch.wait()
                    at = slice(152 + GH * cc, 156 + GH * cc)
                    nc.scalar.activation(small[:, at], small[:, 144 + GH * cc:148 + GH * cc], ACT.Sqrt,
                                         bias=const("eps"), scale=1.0 / GD).then_inc(o_std, 1)
                for cc in range(2):
                    act.wait_ge(gt_ready, 15 * l + 14 + cc)
                    nc.scalar.activation(hi_T[:, 4:8, cc * P:cc * P + P],
                                         bank[:, (13 + cc) % 4, :].rearrange("p (a n) -> p a n", a=4), ACT.Copy)\
                        .then_inc(mix_hi_ready, 1)

            def conv_silu(l, part):
                act.wait_ge(conv_ready, 3 * l + part + 1)
                nc.scalar.activation(conv[:, 4 * part:4 * part + 4, :], conv[:, 4 * part:4 * part + 4, :], ACT.Silu)\
                    .then_inc(silu_ready, 1)

            def hidden_high(j):
                at = slice(2 * j, 2 * j + 2) if isinstance(j, int) else bass.ds(j * 2, 2)
                nc.scalar.activation(act_hi[:, at, :], act_T[:, at, :], ACT.Copy).then_inc(act_hi_ready, 1)

            act.wait_ge(c_loaded, 16)
            nc.scalar.activation(c_silu[:, :], c_in[:, :], ACT.Silu).then_inc(c_ready, 1)
            act.wait_ge(tab_ready, 1)
            for a in range(2):
                nc.scalar.activation(tab_rows[:, a, :], bank[0:16, a, 0:BIAS_W], ACT.Copy).then_inc(tab_copied, 1)
            act.wait_ge(tab_copied, 2)
            act.dma_start(bias_dram.rearrange("a h d -> h a d"), tab_rows[:, :, :]).then_inc(tab_out, 16)
            act.wait_ge(first_in, 16 * 3)
            norm_squares(0)
            n = 0
            for l in range(L1):
                if l:
                    norm_squares(n)
                if l == 0:
                    act.wait_ge(tab_out, 16)
                u0, name = phases[f"in{l}"]["u0"], f"in{l}"
                if l == 0:
                    high(0)
                    high(1)
                norm_high(n, mod[:, l, 0:8])
                if l == 0:
                    high(2)
                for i in range(10):
                    for j in (2 * i, 2 * i + 1):
                        take(name, j, raw[:, j, :] if j < 8 else conv_in[:, j - 8, 3:3 + S], bank[:, j % 4, 0:S])
                    high(u0 + i + AHEAD)
                    if l == 0 and i == 7:
                        act.wait_ge(consts_in, 16 * 2)
                    if i in (7, 9):
                        conv_silu(l, (i - 7) // 2)
                high(u0 + 10 + AHEAD)
                for qt in range(QT):
                    take(name, 20 + qt, z[:, qt, :], bank[:, qt, :], ACT.Silu)
                conv_silu(l, 2)
                for qt in range(QT):
                    take(f"tok{l}", qt, tokp[:, qt, :], bank[:, 2 + qt, 0:TOKW])
                act.wait_ge(gemm_freed, phases[f"out{l}"]["t0"])
                for qt in range(QT):
                    nc.scalar.activation(small[:, 16 * qt:16 * qt + 12], tokp[:, qt, GATES:GATES + 12], ACT.Exp, scale=-1.0)
                    last = nc.scalar.activation(small[:, 16 * qt + 12:16 * qt + 16], tokp[:, qt, B_COL:B_COL + 4],
                                                ACT.Exp, scale=-1.0)
                last.then_inc(gate_exp, 1)
                softplus(l)
                act.wait_ge(gemm_ready, phases[f"cmp{l}"]["e0"] + 2)
                nc.scalar.activation(hid[:, :, :, :].rearrange("p a b n -> p (a b) n"),
                                     bank[:, 7, 0:64].rearrange("p (a n) -> p a n", a=4)[:, :, 0:N_CMP], ACT.Silu)\
                    .then_inc(hid_ready, 1)
                act.wait_ge(kc_ps_ready, l + 1)
                nc.scalar.activation(kcT[:, :], bank[:, 6, 0:N_CMP], ACT.Copy)
                nc.scalar.activation(vc[:, :], bank[0:N_CMP, 6, 64:64 + HD], ACT.Copy).then_inc(kc_ready, 1)
                decays(l)
                attention(f"hybrid{l}")
                delta_net(l)
                norm_squares(n + 1)
                norm_high(n + 1, mod[:, l, 24:32])
                ph = phases[f"gu{l}"]

                def gate_chunk(j, turn=None):
                    step = 0 if turn is None else turn * (4 * SLOTS)
                    chunk = j if turn is None else turn * SLOTS + j
                    for b in range(2):
                        act.wait_ge(gemm_ready, step + ph["e0"] + 4 * j + 2 * b + 1)
                        act.wait_ge(gemm_freed, step + ph["t0"] + 4 * j + 2 * b - 2)
                        nc.scalar.activation(sg[:, b, :], bank[:, 2 * b, 0:S], ACT.Silu).then_inc(sg_ready, 1)
                        high(ph["u0"] + 2 * j + b + AHEAD, turn)
                    act.wait_ge(gemm_freed, step + ph["t0"] + 4 * j + 4)
                    hidden_high(chunk)

                turns = 11 // SLOTS
                with act.Fori(0, turns) as i:
                    for j in range(SLOTS):
                        gate_chunk(j, i)
                for j in range(SLOTS * turns, 11):
                    gate_chunk(j)
                n += 2
            norm_squares(n)
            n += 1
            act.wait_ge(vec2_in, 16)
            for l, name in enumerate(("even", "odd")):
                norm_squares(n)
                norm_high(n)
                u0 = phases[name]["u0"]
                t = 0
                j = 0
                for nn, kind in enumerate(phases[name]["kinds"]):
                    if kind == "tokens":
                        half = 0 if nn in (2, 4) else 1
                        high(u0 + 2 * nn + AHEAD)
                        for qt in range(QT):
                            take(name, j, vv2[:, qt, CH * half:CH * half + CH], bank[:, j % 4, :])
                            j += 1
                        high(u0 + 2 * nn + 1 + AHEAD)
                    else:
                        for part in range(2):
                            for m in range(2):
                                take(name, j, qk2[:, t, :], bank[:, j % 4, 0:S])
                                t += 1
                                j += 1
                            high(u0 + 2 * nn + part + AHEAD)
                if l == 0:
                    take("tail", 0, qk2[:, 24, :], bank[:, 0, 0:S])
                    for qt in range(QT):
                        take("tail", 1 + qt, wi[:, qt, :], bank[:, 1 + qt, 0:16])
                    act.wait_ge(gemm_freed, phases["o0"]["t0"])
                    nc.scalar.activation(tmp[:, 0, :], qk2[:, 24, :], ACT.Square).then_inc(ki_sq, 1)
                    act.wait_ge(ki_ssq, 1)
                    nc.scalar.activation(std[:, :], bank[:, 7, 0:S], ACT.Sqrt, bias=const("eps"), scale=1.0 / HD)\
                        .then_inc(ki_std, 1)
                    for i in range(QT * 4):
                        w = P * (i // 4 + 1)
                        act.wait_ge(ix_ready, i + 1)
                        if i >= 2:
                            act.wait_ge(ix_acc, i - 1)
                        nc.scalar.activation(
                            rel[:, i % 2, :, 0:w],
                            bank[:, 2 * (i % 2):2 * (i % 2) + 2, :].rearrange("p b (s n) -> p (b s) n", s=2)[:, :, 0:w],
                            ACT.Relu, scale=HD ** -0.5).then_inc(ix_relu, 1)
                        if i in (1, 3):
                            high(phases["tail"]["u0"] + i // 2 + AHEAD)

                def mix_high(tiles, units_done):
                    act.wait_ge(o_evac, evacs_before(units_done))
                    nc.scalar.activation(hi_T[:, tiles, :], mix[:, tiles, :], ACT.Copy).then_inc(mix_hi_ready, 1)

                attention(name, lambda: mix_high(slice(0, MIX_EARLY), stages[name][1] - 2))
                mix_high(slice(MIX_EARLY, KT), stages[name][1])
                norm_squares(n + 1)
                norm_high(n + 1)
                ph = phases[f"up{l}"]
                cw = vec_b(l, "conv_w").rearrange("p (j t) -> p j t", j=3)
                cb = vec_b(l, "conv_b")

                def value_chunk(j, turn=None):
                    step = 0 if turn is None else turn * (4 * SLOTS)
                    chunk = j if turn is None else turn * SLOTS + j

                    def silu(b):
                        act.wait_ge(gemm_freed, step + ph["t0"] + 4 * j + 2 * b + 2)
                        nc.scalar.activation(sg[:, b, :], cv[:, b, 1, :], ACT.Silu).then_inc(sg_ready, 1)

                    products = (0 if turn is None else turn * (2 * SLOTS)) + FT * l + 2 * j + 1
                    for b in range(2):
                        act.wait_ge(gemm_ready, step + ph["e0"] + 4 * j + 2 * b + 2)
                        act.wait_ge(act_ready, products)
                        for half in range(2):
                            at = 4 * j + 2 * b + half if turn is None else turn * (4 * SLOTS) + 4 * j + 2 * b + half
                            at = slice(at, at + 1) if turn is None else bass.ds(at, 1)
                            last = nc.scalar.activation(cv[:, b, half, :], bank[:, 2 * b + half, 0:S], ACT.Identity,
                                                        bias=cb[:, at], scale=cw[:, 2, at])
                        last.then_inc(cv_ready, 1)
                        high(ph["u0"] + 2 * j + b + AHEAD, turn)
                    for b in range(2):
                        silu(b)
                    act.wait_ge(act_ready, products + 2)
                    hidden_high(chunk)

                with act.Fori(0, turns) as i:
                    for j in range(SLOTS):
                        value_chunk(j, i)
                for j in range(SLOTS * turns, 11):
                    value_chunk(j)
                n += 2
            norm_squares(n)

        @block.vector
        def _(dve):
            V = nc.vector
            ch = Chain(dve, dve_chain)

            def rms(n):
                dve.wait_ge(std_ready, n + 1)
                ch(V.reciprocal(rstd[:, :], std[:, :]))

            def normalise_tile(k, scale, out, sig):
                V.scalar_tensor_tensor(out=out[:, k, :], in0=x[:, k, :], scalar=scale[:, k:k + 1], in1=rstd[:, :],
                                       op0=ALU.mult, op1=ALU.mult).then_inc(sig, 1)

            def normalise_into(n, scale, out, sig):
                rms(n)
                for k in range(KT):
                    normalise_tile(k, scale, out, sig)

            def normalise(n, scale, shift=None):
                if n:
                    rms(n)
                for k in range(NORM_AHEAD):
                    normalise_tile(k, scale, h, hn_ready)
                for k in range(KT):
                    dve.wait_ge(h_hi_ready, KT * split_norms.index(n) + k + 1)
                    if shift is None:
                        ins = V.tensor_tensor(h_lo[:, k, :], h[:, k, :], hi_T[:, k, :].bitcast(F32), ALU.subtract)
                    else:
                        ins = V.scalar_tensor_tensor(out=h_lo[:, k, :], in0=h[:, k, :], scalar=shift[:, k:k + 1],
                                                     in1=hi_T[:, k, :].bitcast(F32), op0=ALU.add, op1=ALU.subtract)
                    ins.then_inc(h_ready, 1)
                    if k + NORM_AHEAD < KT:
                        normalise_tile(k + NORM_AHEAD, scale, h, hn_ready)
                if norm_input[n]:
                    low(phases[norm_input[n]]["u1"] - 1 + AHEAD)

            def low(u, turn=None):
                if u >= len(halves) or u in late:
                    return
                n, part, size, _ = halves[u]
                at = slice(part * size, (part + 1) * size)
                dve.wait_ge(w_hi_ready, u + 1 if turn is None else turn * (2 * SLOTS) + u + 1)
                V.tensor_tensor(w_lo[:, n % SLOTS, at], ring[:, n % SLOTS, at], w_hi[:, u % AHEAD, 0:size].bitcast(F32),
                                ALU.subtract).then_inc(w_lo_ready, 1)

            def mix_low(done, tiles, cs):
                dve.wait_ge(mix_hi_ready, done)
                V.tensor_tensor(mix_lo[:, tiles, cs], mix[:, tiles, cs], hi_T[:, tiles, cs].bitcast(F32), ALU.subtract)\
                    .then_inc(mix_ready, 1)

            def hidden_low(j, done):
                dve.wait_ge(act_hi_ready, done)
                at = slice(2 * j, 2 * j + 2) if isinstance(j, int) else bass.ds(j * 2, 2)
                V.tensor_tensor(act_lo[:, at, :], act_T[:, at, :], act_hi[:, at, :].bitcast(F32), ALU.subtract)\
                    .then_inc(hidden_ready, 1)

            def attention(name, steps=(), before_last=None):
                u0, u1 = stages[name]

                def logits(u):
                    U, b, w = units[u], units[u]["b"], units[u]["w"]
                    dve.wait_ge(scores_ready, u + 1)
                    if u >= DEPTH:
                        dve.wait_ge(trans_ready, u - DEPTH + 1)
                    s_ps = bank[:, 2 * (u % 2):2 * (u % 2) + 2, :].rearrange("p b (s n) -> p (b s) n", s=2)[:, :, 0:w]
                    out = lg[:, b, :, 0:w]
                    ch(V.scalar_tensor_tensor(out=out, in0=s_ps, scalar=SCALE, in1=U["bias"], op0=ALU.mult, op1=ALU.add))
                    if U.get("sel") is not None:
                        ch(V.tensor_tensor(out, out, U["sel"], ALU.add))
                    red = V.tensor_reduce(out=negm[:, b, :], in_=out, op=ALU.max, axis=AX.X, negate=True)
                    if U["sink"] is not None:
                        ch(red)
                        ch(V.scalar_tensor_tensor(out=negm[:, b, :], in0=U["sink"], scalar=-1.0, in1=negm[:, b, :],
                                                  op0=ALU.mult, op1=ALU.min))
                        red = V.tensor_tensor(esink[:, b, :], U["sink"], negm[:, b, :], ALU.add)
                    red.then_inc(logits_done, 1)

                def recip(u):
                    U, b = units[u], units[u]["b"]
                    dve.wait_ge(exps_done, u + 1)
                    if U["sink"] is not None:
                        ch(V.tensor_tensor(sums[:, b, :], sums[:, b, :], esink[:, b, :], ALU.add))
                    r = V.reciprocal(rec[:, b, :], sums[:, b, :])
                    if U["gate"] is not None:
                        ch(r)
                        r = V.tensor_tensor(rec[:, b, :], rec[:, b, :], U["gate"], ALU.mult)
                    r.then_inc(rec_ready, 1)

                def evac(u):
                    U = units[u]
                    if not U["end"]:
                        return
                    dve.wait_ge(pv_done, u + 1)
                    for s, rows, tile in U["evac"]:
                        last = V.tensor_copy(mix[rows, tile, U["qs"]], bank[0:HD, 6, s * P:s * P + P])
                    last.then_inc(o_evac, 1)

                logits(u0)
                logits(u0 + 1)
                for u in range(u0, u1 + 1):
                    if u < u1:
                        recip(u)
                    if u + 2 < u1:
                        logits(u + 2)
                    if u > u0:
                        evac(u - 1)
                    if before_last and u == u1 - 1:
                        before_last()
                    if u - u0 < len(steps):
                        steps[u - u0]()

            ga = small[:, 64:64 + NCH]
            relu = small[:, 72:72 + NCH]
            ea, g, gc = small[:, 88:92], small[:, 96:96 + NCH], small[:, 104:104 + NCH]
            eg, ekd = small[:, 112:112 + NCH], small[:, 120:120 + NCH]
            rqk = small[:, 128:144]
            beta = small[:, 160:160 + NCH]
            ga3 = ga.rearrange("p (c h) -> p c h", c=QT)

            def softplus(l):
                ch(V.tensor_tensor(ga3, tokp[:, :, A_COL:A_COL + 4], over(vec(l, "dt"), QT), ALU.add))
                ch(V.tensor_scalar(relu, ga, 0.0, None, ALU.max))
                ch(V.scalar_tensor_tensor(out=small[:, 80:88], in0=ga, scalar=-1.0, in1=ga, op0=ALU.mult, op1=ALU.min))
                V.tensor_copy(ga, small[:, 80:88]).then_inc(g_arg, 1)
                ch(V.tensor_copy(beta.rearrange("p (c h) -> p c h", c=QT),
                                 small[:, 0:32].rearrange("p (c n) -> p c n", c=QT)[:, :, 12:16]))
                dve.wait_ge(g_fun, 4 * l + 1)
                V.tensor_scalar(ga, ga, 1.0, None, ALU.add).then_inc(g_arg, 1)
                dve.wait_ge(g_fun, 4 * l + 2)
                ch(V.tensor_tensor(relu, relu, ga, ALU.add))
                ch(V.scalar_tensor_tensor(out=g.rearrange("p (c h) -> p c h", c=QT),
                                          in0=relu.rearrange("p (c h) -> p c h", c=QT), scalar=-1.0, in1=over(ea, QT),
                                          op0=ALU.mult, op1=ALU.mult))
                V.tensor_copy(gB, along(g, P)).then_inc(g_ready, 1)
                dve.wait_ge(gt_copied, 13 * l + 4)
                for qk in range(2):
                    ch(V.tensor_tensor(sq_tok, tok[:, qk], tok[:, qk], ALU.mult))
                    last = V.tensor_reduce(out=rqk[:, NCH * qk:NCH * qk + NCH], in_=sq_tok, op=ALU.add, axis=AX.X)
                    ch(last)
                V.tensor_copy(rqk, rqk).then_inc(g_arg, 1)

            def decays(l):
                dve.wait_ge(gc_ready, l + 1)
                ch(V.tensor_copy(gc, bank[:, 3, 0:NCH]))
                for i in range(NCH):
                    ch.mark(V.tensor_scalar(Dm[:, i, :], bank[:, 4 + i // 4, (i % 4) * P:(i % 4) * P + P],
                                            gc[:, i:i + 1], 0.0, ALU.subtract, ALU.min))
                for cc in range(2):
                    last = V.tensor_tensor(
                        ekd[:, 4 * cc:4 * cc + 4],
                        bank[:, 4 + cc, :].rearrange("p (a n) -> p a n", a=4)[:, :, P - 1], gc[:, 4 * cc:4 * cc + 4],
                        ALU.subtract)
                    ch.mark(last)
                ch.wait()
                V.tensor_copy(ekd, ekd).then_inc(g_arg, 1)

            def operands(l):
                def step0():
                    dve.wait_ge(g_fun, 4 * l + 3)
                    ch(V.reciprocal(rqk, rqk))
                    ch(V.tensor_scalar(rqk[:, 0:NCH], rqk[:, 0:NCH], GD ** -0.5, None, ALU.mult))
                    dve.wait_ge(gt_copied, 13 * l + 6)
                    ch(V.tensor_tensor(qn, tok[:, 0], along(rqk[:, 0:NCH], GD), ALU.mult))

                def step1():
                    ch(V.tensor_tensor(kn, tok[:, 1], along(rqk[:, NCH:2 * NCH], GD), ALU.mult))

                def step2():
                    ch(V.tensor_tensor(vb, tok[:, 2], along(beta, GD), ALU.mult))

                def step3():
                    ch(V.tensor_tensor(kb, kn, along(beta, GD), ALU.mult))

                def step4():
                    dve.wait_ge(g_fun, 4 * l + 4)
                    ch(V.tensor_tensor(Dm, Dm, over(upper, NCH), ALU.mult))

                def step5():
                    ch(V.tensor_tensor(kbg, kb[:, GH:NCH], along(eg[:, GH:NCH], GD), ALU.mult))
                    ch(V.tensor_tensor(kd, kn[:, 0:GH], along(ekd[:, 0:GH], GD), ALU.mult))

                def step6():
                    V.tensor_tensor(qd, qn[:, GH:NCH], along(eg[:, GH:NCH], GD), ALU.mult).then_inc(scaled, 1)
                    dve.wait_ge(scaled, l + 1)

                return [step0, step1, step2, step3, step4, step5, step6]

            def delta_net(l, m_next):
                mix_low(3 * l + 1, slice(0, 4), slice(0, S))
                weigh(m_next)
                for b in range(4):
                    dve.wait_ge(kq_ready, 4 * l + b + 1)
                    ps = bank[:, KQ_BANKS[b], :].rearrange("p (i a n) -> p i a n", i=2, a=2)
                    ch.mark(V.tensor_tensor(MT[:, 2 * b:2 * b + 2], ps[:, :, 0, :], Dm[:, 2 * b:2 * b + 2], ALU.mult))
                    ch.mark(V.tensor_tensor(QKT[:, 2 * b:2 * b + 2], ps[:, :, 1, :], Dm[:, 2 * b:2 * b + 2], ALU.mult))
                ch.wait()
                if l:
                    dve.wait_ge(mb_ready, l * LEVELS)
                V.tensor_tensor(MbT[:, 0], MT, over(const("levels")[:, 0:P], NCH), ALU.mult).then_inc(mb_ready, 1)
                for lv in range(LEVELS):
                    for half in range(2):
                        hs = slice(4 * half, 4 * half + 4)
                        if lv == 0:
                            dve.wait_ge(mb_ready, l * LEVELS + 1)
                            dve.wait_ge(t1_ready, l * 2 * LEVELS + half + 1)
                            ps = bank[:, half, :].rearrange("p (a n) -> p a n", a=4)
                            V.tensor_tensor(X[:, hs], over(ident, 4), ps, ALU.subtract)
                            V.tensor_tensor(XT[:, hs], over(ident, 4), MbT[:, 0, hs], ALU.subtract).then_inc(x_upd, 1)
                        else:
                            dve.wait_ge(dx_ready, l * 2 * (LEVELS - 1) + 2 * (lv - 1) + half + 1)
                            if lv < LEVELS - 1:
                                ps = bank[:, 2 + half, :].rearrange("p (a n) -> p a n", a=4)
                                V.tensor_tensor(X[:, hs], X[:, hs], ps, ALU.subtract)
                            ps = bank[:, 4 + half, :].rearrange("p (a n) -> p a n", a=4)
                            V.tensor_tensor(XT[:, hs], XT[:, hs], ps, ALU.subtract).then_inc(x_upd, 1)
                weigh(m_next + 1)
                dve.wait_ge(u_copied, l + 1)
                dve.wait_ge(ws_ready, l + 1)
                V.tensor_tensor(U[:, GH:NCH], U[:, GH:NCH], bank[:, 5, :].rearrange("p (a n) -> p a n", a=4), ALU.subtract)\
                    .then_inc(vnew_ready, 1)
                dve.wait_ge(z_scaled, l + 1)
                for cc in range(2):
                    dve.wait_ge(o_std, 2 * l + cc + 1)
                    at = slice(152 + GH * cc, 156 + GH * cc)
                    ch(V.reciprocal(small[:, at], small[:, at]))
                    for i in range(GH):
                        last = V.scalar_tensor_tensor(
                            out=o_n[:, GH * cc + i, :], in0=bank[:, 4 + 2 * cc, i * P:i * P + P],
                            scalar=small[:, 152 + GH * cc + i:153 + GH * cc + i],
                            in1=z[:, cc, i * GD:i * GD + GD], op0=ALU.mult, op1=ALU.mult)
                    last.then_inc(on_ready, 1)
                for cc in range(2):
                    cs = slice(cc * P, cc * P + P)
                    dve.wait_ge(mix_hi_ready, 3 * l + cc + 2)
                    V.tensor_tensor(mix_lo[:, 4:8, cs], bank[:, (13 + cc) % 4, :].rearrange("p (a n) -> p a n", a=4),
                                    hi_T[:, 4:8, cs].bitcast(F32), ALU.subtract).then_inc(mix_ready, 1)

            def residual(name, gate):
                ph = phases[name]
                each = 2 if ph["kinds"][0] == "down" else 1
                for k in range(KT):
                    if name == "dn0" and k == KT - 1:
                        dve.wait_ge(mod_ready, ADA_L + ADA_FIRST)
                        modulation(1, 0, ADA_FIRST)
                        norm_gain(1, 0).then_inc(mod_read, 2)
                        dve.wait_ge(mod_read, 4)
                    dve.wait_ge(gemm_ready, ph["tile_event"][k])
                    ps = bank[:, 4 + k % 3 if each == 2 else k % 4, 0:S]
                    if gate is None:
                        ins = V.tensor_tensor(x[:, k, :], x[:, k, :], ps, ALU.add)
                    else:
                        ins = V.scalar_tensor_tensor(out=x[:, k, :], in0=ps, scalar=gate[:, k:k + 1], in1=x[:, k, :],
                                                     op0=ALU.mult, op1=ALU.add)
                    ins.then_inc(gemm_freed, 1)
                    used = range(ph["u0"] + 2 * k, ph["u0"] + 2 * k + 2) if each == 2 else [ph["u0"] + k // 2] * (k % 2)
                    for u in used:
                        if u < ph["u1"] - 1:
                            low(u + AHEAD)

            def weigh(m):
                at = ada_at[m]
                dve.wait_ge(slot_in[at % SLOTS], 16 * (at // SLOTS + 1))
                if m >= 2:
                    dve.wait_ge(mod_ready, m - 1)
                w, out = ring[:, at % SLOTS, :].rearrange("p (k n) -> p k n", k=KT), acc[:, m % 2, :]
                ch(V.tensor_scalar(out, w[:, 0, :], c_silu[:, 0:1], None, ALU.mult))
                for k in range(1, KT):
                    ins = V.scalar_tensor_tensor(out=out, in0=w[:, k, :], scalar=c_silu[:, k:k + 1], in1=out,
                                                 op0=ALU.mult, op1=ALU.add)
                    if k < KT - 1:
                        ch(ins)
                ins.then_inc(acc_ready, 1)

            def highest(qt, r0, r1):
                w = P * (qt + 1)
                mask = const("causal0") if qt == 0 else const("causal1")
                if r0 == 0:
                    ch(V.tensor_tensor(work[:, 0, 0:w], score[:, qt, 0:w], mask, ALU.add))
                for r in range(r0, r1):
                    ch(V.max(max8, work[:, r % 2, 0:w]))
                    ch(V.match_replace(work[:, (r + 1) % 2, 0:w], max8, work[:, r % 2, 0:w], -3e38))
                if r1 == 8:
                    ch(V.tensor_scalar(selm[:, qt, 0:w], work[:, 0, 0:w], -2e38, NEG, ALU.is_gt, ALU.mult))

            def modulation(l, m0, m1, read=None):
                at = MOD_COL + 4 * ADA_L * l
                ins = V.tensor_tensor(mod[:, l, 4 * m0:4 * m1], bank[:, 7, at + 4 * m0:at + 4 * m1],
                                      vec(l, "ada_b")[:, 4 * m0:4 * m1], ALU.add)
                if read:
                    ins.then_inc(read, 1)
                    dve.wait_ge(read, 2 + 3 * l)
                else:
                    ch(ins)

            def norm_gain(l, part):
                return V.scalar_tensor_tensor(out=gain[:, l, part, :], in0=mod[:, l, 24 * part + 8:24 * part + 16],
                                              scalar=1.0, in1=vec(l, ("norm_mix", "norm_ffn")[part]),
                                              op0=ALU.add, op1=ALU.mult)

            V.memset(conv_in[:, :, 0:3], 0.0).then_inc(act_ready, 1)
            dve.wait_ge(act_ready, 1)
            dve.wait_ge(c_ready, 1)
            for m in range(ADA_FIRST):
                if m == 2:
                    rms(0)
                weigh(m)
            n = 0
            for l in range(L1):
                if l:
                    ch(V.memset(conv_in[:, :, 0:3], 0.0))
                if l == 0:
                    dve.wait_ge(first_in, 16 * 3)
                    low(0)
                    dve.wait_ge(mod_ready, ADA_FIRST)
                    modulation(0, 0, ADA_FIRST)
                    norm_gain(0, 0).then_inc(mod_read, 1)
                    dve.wait_ge(mod_read, 1)
                normalise(n, gain[:, l, 0, :], mod[:, l, 0:8])
                m = ADA_L * l + ADA_FIRST
                u0 = phases[f"in{l}"]["u0"]
                if l == 0:
                    dve.wait_ge(consts_in, 16 * 2)
                t0 = phases[f"in{l}"]["t0"]
                for t in range(6):
                    if t == 2:
                        weigh(m)
                    dve.wait_ge(gemm_freed, t0 + t + 1)
                    dve.wait_ge(rot_ready, 6 * l + t + 1)
                    ch.mark(V.tensor_tensor(tmp[:, 0, :], raw[:, t, :], const("cos"), ALU.mult))
                    ch(V.tensor_tensor(tmp[:, 1, :], bank[:, 4 + t % 2, 0:S], const("sin"), ALU.mult))
                    V.tensor_tensor(rot[:, t, :], tmp[:, 0, :], tmp[:, 1, :], ALU.add).then_inc(rope_done, 1)
                    dve.wait_ge(rope_done, 7 * l + t + 1)
                V.tensor_copy(rot[LO, 6, :], rot[HI, 5, :])
                V.tensor_copy(rot[HI, 6, :], rot[LO, 5, :]).then_inc(rope_done, 1)
                weigh(m + 1)
                dve.wait_ge(gemm_freed, t0 + 8)
                for kv, pe_name in enumerate(("pe_k", "pe_v")):
                    for two, rows in enumerate((LO, HI)):
                        base = raw[rows, 6 + kv, :].rearrange("p (n q a) -> p a q n", q=8, a=2)[:, two]
                        for hf in range(2):
                            last = V.tensor_tensor(
                                xpe[rows, kv, 8 * hf:8 * hf + 8, :], base[:, :, hf:hf + N_CMP],
                                along(vec(l, pe_name)[rows, 8 * hf:8 * hf + 8], N_CMP), ALU.add)
                    last.then_inc(xpe_ready, 1)
                cw = vec(l, "conv").rearrange("p (j t) -> p j t", j=4)
                for part in range(3):
                    dve.wait_ge(gemm_freed, t0 + 8 + 4 * part + 4)
                    for tap in range(4):
                        if tap:
                            ch.wait()
                        for t in range(4 * part, 4 * part + 4):
                            src, wt = conv_in[:, t, tap:tap + S], cw[:, tap, t:t + 1]
                            if tap == 0:
                                ins = V.tensor_scalar(conv[:, t, :], src, wt, None, ALU.mult)
                            else:
                                ins = V.scalar_tensor_tensor(out=conv[:, t, :], in0=src, scalar=wt, in1=conv[:, t, :],
                                                             op0=ALU.mult, op1=ALU.add)
                            if tap == 3 and t % 4 == 3:
                                ins.then_inc(conv_ready, 1)
                            else:
                                ch.mark(ins)
                dve.wait_ge(gate_exp, l + 1)
                ch(V.tensor_scalar(small[:, 0:32], small[:, 0:32], 1.0, None, ALU.add))
                ch(V.reciprocal(small[:, 0:32], small[:, 0:32]))
                softplus(l)
                weigh(m + 2)
                decays(l)
                weigh(m + 3)
                attention(f"hybrid{l}", operands(l))
                delta_net(l, m + 4)
                dve.wait_ge(mod_ready, m + 6)
                modulation(l, ADA_FIRST, ADA_L - 2)
                ch(norm_gain(l, 1))
                dve.wait_ge(w_lo_ready, phases[f"out{l}"]["u0"] + AHEAD)
                residual(f"out{l}", mod[:, l, 16:24])
                normalise(n + 1, gain[:, l, 1, :], mod[:, l, 24:32])
                ph = phases[f"gu{l}"]

                def gate_chunk(j, turn=None):
                    step = 0 if turn is None else turn * (4 * SLOTS)
                    tiles = 0 if turn is None else turn * (2 * SLOTS)
                    for b in range(2):
                        dve.wait_ge(sg_ready, tiles + FT * l + 2 * j + b + 1)
                        dve.wait_ge(gemm_ready, step + ph["e0"] + 4 * j + 2 * b + 2)
                        at = 2 * j + b if turn is None else turn * (2 * SLOTS) + 2 * j + b
                        at = slice(at, at + 1) if turn is None else bass.ds(at, 1)
                        V.tensor_tensor(act_T[:, at, :], sg[:, b, :].rearrange("p (a n) -> p a n", a=1),
                                        bank[:, 2 * b + 1, 0:S].rearrange("p (a n) -> p a n", a=1), ALU.mult)\
                            .then_inc(gemm_freed, 2)
                        low(ph["u0"] + 2 * j + b + AHEAD, turn)
                    hidden_low(j if turn is None else turn * SLOTS + j,
                               (0 if turn is None else turn * SLOTS) + 11 * l + j + 1)

                turns = 11 // SLOTS
                with dve.Fori(0, turns) as i:
                    for j in range(SLOTS):
                        gate_chunk(j, i)
                for j in range(SLOTS * turns, 11):
                    gate_chunk(j)
                dve.wait_ge(mod_ready, m + 8)
                modulation(l, ADA_L - 2, ADA_L, mod_read)
                residual(f"dn{l}", mod[:, l, 40:48])
                n += 2
            dve.wait_ge(vec2_in, 16)
            normalise_into(n, const("final1"), x, x_ready)
            low(phases["dn1"]["u1"] - 1 + AHEAD)
            n += 1
            for l, name in enumerate(("even", "odd")):
                normalise(n, vec_b(l, "norm_attn"))
                for u in range(phases[name]["u0"], phases[name]["u1"]):
                    low(u + AHEAD)
                if l == 0:
                    dve.wait_ge(ki_std, 1)
                    ch(V.reciprocal(rstd[:, :], std[:, :]))
                    V.scalar_tensor_tensor(out=qk2[:, 24, :], in0=qk2[:, 24, :], scalar=const("knorm"), in1=rstd[:, :],
                                           op0=ALU.mult, op1=ALU.mult).then_inc(ki_ready, 1)
                    ch(V.tensor_scalar(wi, wi, 16 ** -0.5, None, ALU.mult))
                    for i in range(QT * 4):
                        qt, g, w = i // 4, i % 4, P * (i // 4 + 1)
                        dve.wait_ge(ix_relu, i + 1)
                        for s in range(NG):
                            col = wi[:, qt, NG * g + s:NG * g + s + 1]
                            src = rel[:, i % 2, s, 0:w]
                            if g == 0 and s == 0:
                                ins = V.tensor_scalar(score[:, qt, 0:w], src, col, None, ALU.mult)
                            else:
                                ins = V.scalar_tensor_tensor(out=score[:, qt, 0:w], in0=src, scalar=col,
                                                             in1=score[:, qt, 0:w], op0=ALU.mult, op1=ALU.add)
                            if s == NG - 1:
                                ins.then_inc(ix_acc, 1)
                                dve.wait_ge(ix_acc, i + 1)
                            else:
                                ch(ins)
                        if qt == 1:
                            highest(0, 2 * g, 2 * g + 2)
                    dve.wait_ge(bias_in, 32)
                attention(name, [lambda: highest(1, 0, 4), lambda: highest(1, 4, 8)] if l == 0 else (),
                          lambda: mix_low(3 * L1 + 2 * l + 1, slice(0, MIX_EARLY), slice(0, S)))
                mix_low(3 * L1 + 2 * l + 2, slice(MIX_EARLY, KT), slice(0, S))
                if l == 0:
                    dve.wait_ge(w_lo_ready, phases["o0"]["u0"] + AHEAD)
                residual(f"o{l}", None)
                normalise(n + 1, vec_b(l, "norm_ffn"))
                ph = phases[f"up{l}"]
                cw = vec_b(l, "conv_w").rearrange("p (j t) -> p j t", j=3)

                def value_chunk(j, turn=None):
                    step = 0 if turn is None else turn * (4 * SLOTS)
                    tiles = 0 if turn is None else turn * (2 * SLOTS)
                    for b in range(2):
                        dve.wait_ge(cv_ready, tiles + FT * l + 2 * j + b + 1)
                        for tap in (1, 0):
                            shift = 2 - tap
                            for half in range(2):
                                at = 4 * j + 2 * b + half
                                at = slice(at, at + 1) if turn is None else bass.ds(turn * (4 * SLOTS) + at, 1)
                                if tap == 0:
                                    dve.wait_ge(tap_done, step + 2 * FT * l + 4 * j + 2 * b + half + 1)
                                V.scalar_tensor_tensor(out=cv[:, b, half, shift:S], in0=bank[:, 2 * b + half, 0:S - shift],
                                                       scalar=cw[:, tap, at], in1=cv[:, b, half, shift:S],
                                                       op0=ALU.mult, op1=ALU.add)\
                                    .then_inc(tap_done if tap else gemm_freed, 1)
                        low(ph["u0"] + 2 * j + b + AHEAD, turn)
                    for b in range(2):
                        dve.wait_ge(sg_ready, tiles + FT * (L1 + l) + 2 * j + b + 1)
                        dve.wait_ge(gemm_freed, step + ph["t0"] + 4 * j + 2 * b + 2)
                        at = 2 * j + b
                        at = slice(at, at + 1) if turn is None else bass.ds(turn * (2 * SLOTS) + at, 1)
                        V.tensor_tensor(act_T[:, at, :], sg[:, b, :].rearrange("p (a n) -> p a n", a=1),
                                        cv[:, b, 0, :].rearrange("p (a n) -> p a n", a=1), ALU.mult).then_inc(act_ready, 1)
                    hidden_low(j if turn is None else turn * SLOTS + j,
                               (0 if turn is None else turn * SLOTS) + 11 * (L1 + l) + j + 1)

                with dve.Fori(0, turns) as i:
                    for j in range(SLOTS):
                        value_chunk(j, i)
                for j in range(SLOTS * turns, 11):
                    value_chunk(j)
                residual(f"down{l}", None)
                n += 2
            normalise_into(n, const("final2"), h, h_ready)

        @block.gpsimd
        def _(pool):
            ch = Chain(pool, pool_chain)
            G = nc.gpsimd

            def attention(name):
                u0, u1 = stages[name]
                for u in range(u0, u1):
                    U, b, w = units[u], units[u]["b"], units[u]["w"]
                    pool.wait_ge(rec_ready, u + 1)
                    out = lg[:, b, :, 0:w]
                    ins = G.tensor_tensor(out, out, along(rec[:, b, :], w), ALU.mult)
                    if U.get("valid") is not None:
                        ch(ins)
                        ins = G.tensor_tensor(out, out, U["valid"], ALU.mult)
                    ins.then_inc(probs_ready, 1)

            def low(u):
                n, part, size, _ = halves[u]
                at = slice(part * size, (part + 1) * size)
                pool.wait_ge(w_hi_ready, u + 1)
                G.tensor_tensor(w_lo[:, n % SLOTS, at], ring[:, n % SLOTS, at], w_hi[:, u % AHEAD, 0:size].bitcast(F32),
                                ALU.subtract).then_inc(w_lo_ready, 1)

            def weigh(m):
                pool.dma_start(ada_late, ada[m].rearrange("p (k n) -> p k n", k=KT)).then_inc(late_in, 16)
                pool.wait_ge(late_in, 16 * (ada_alone.index(m) + 1))
                ch(G.tensor_tensor(ada_late, ada_late, along(c_silu, CH), ALU.mult))
                for half in (KT // 2, KT // 4):
                    ch(G.tensor_tensor(ada_late[:, 0:half], ada_late[:, 0:half], ada_late[:, half:2 * half], ALU.add))
                pool.wait_ge(mod_ready, m - 1)
                G.tensor_tensor(late_sums[:, m % 2, :], ada_late[:, 0, :], ada_late[:, 1, :], ALU.add).then_inc(acc_ready, 1)
                pool.wait_ge(acc_ready, m + 1)

            pool.wait_ge(c_ready, 1)
            for l in range(L1):
                u0, u1 = phases[f"in{l}"]["u0"] + (AHEAD if l else 1), phases[f"tok{l}"]["u1"]
                pool.wait_ge(w_lo_ready, u0)
                for u in range(u0, u1):
                    low(u)
                attention(f"hybrid{l}")
                if l == 0:
                    pool.wait_ge(consts_in, 16 * 2)
                pool.wait_ge(gemm_freed, phases[f"in{l}"]["t0"] + 22)
                z4 = z.rearrange("p c (h n) -> p (c h) n", h=GH)
                G.tensor_tensor(z4, z4, over(vec(l, "gnorm"), NCH), ALU.mult).then_inc(z_scaled, 1)
                pool.wait_ge(mb_ready, l * LEVELS + 1)
                for lv in range(1, LEVELS):
                    if lv >= 2:
                        pool.wait_ge(x_upd, l * 2 * LEVELS + 2 * (lv - 1))
                    lm = const("levels")[:, lv * P:lv * P + P]
                    G.tensor_tensor(MbT[:, lv % 2], MT, over(lm, NCH), ALU.mult).then_inc(mb_ready, 1)
                for u in range(phases[f"out{l}"]["u0"], phases[f"out{l}"]["u0"] + AHEAD):
                    low(u)
                pool.wait_ge(mix_ready, 3 * (l + 1))
                for m in ada_alone[(2 + ADA_FIRST) * l:(2 + ADA_FIRST) * (l + 1)]:
                    weigh(m)
            pool.wait_ge(w_lo_ready, phases["o0"]["u0"] + 1)
            for u in range(phases["o0"]["u0"] + 1, phases["o0"]["u0"] + AHEAD):
                low(u)
            for name in ("even", "odd"):
                attention(name)


def shape_constants():
    import numpy as np

    f = np.float32
    i, j = np.arange(P)[:, None], np.arange(P)[None, :]
    parts = {}
    inv = (f(1) / (f(10000.0) ** (np.arange(0, HD, 2, dtype=f) / f(HD)))).astype(f)
    ang = (np.arange(S, dtype=f)[:, None] * inv[None, :]).astype(f)
    parts["cos"] = np.tile(np.cos(ang).T, (4, 1))
    parts["sin"] = np.tile(np.sin(ang).T, (4, 1))
    parts["ident"] = i == j
    parts["rot"] = (j % HD >= HD // 2) * (i == j - HD // 2) * 1.0 - (j % HD < HD // 2) * (i == j + HD // 2) * 1.0
    parts["ones"] = np.ones((P, P))
    parts["halves"] = i // HD == j // HD
    parts["upper"] = i <= j
    parts["levels"] = np.concatenate([(i // (2 * b) == j // (2 * b)) & (i // b % 2 == 0) & (j // b % 2 == 1)
                                      for b in (1 << n for n in range(LEVELS))], axis=1)
    k = np.arange(S)[None, :]
    parts["causal0"] = np.where(j <= i, 0.0, NEG)
    parts["band1"] = np.where((k <= i + P) & (k > i), 0.0, NEG)
    parts["causal1"] = np.where(k <= i + P, 0.0, NEG)
    end = np.arange(N_CMP)[None, :] * 16 + 31
    ok = np.concatenate([end <= i + P * qt for qt in range(QT)], axis=1)
    parts["cmp_mask"] = np.where(ok, 0.0, NEG)
    parts["cmp_valid"] = ok
    parts["eps"] = np.full((P, 1), EPS)
    d = S - 1 - np.arange(BIAS_W)
    n = np.maximum(d, 0)
    nf = np.maximum(n, 16).astype(f)
    large = 16 + (np.log(nf / f(16)) / f(np.log(8.0)) * f(16)).astype(np.int32)
    bucket = np.where(n < 16, n, np.minimum(large, 31))
    dist = np.zeros((33, 2, BIAS_W), f)
    seen = d >= 0
    for a in range(2):
        dist[bucket[seen], a, np.nonzero(seen)[0]] = 1.0
    dist[32, 0] = np.where(seen, 0.0, NEG)
    times = ((d <= 128) * 1 + (d % 4 == 0) + (d % 16 == 0)) * seen
    dist[32, 1] = np.where(times > 0, np.log(np.maximum(times, 1)), NEG)
    return parts, dist


def kernel(**inputs):
    import numpy as np
    import concourse.bacc as bacc
    from concourse.bass_utils import run_bass_kernel_spmd as run

    a = {n: np.asarray(v) for n, v in inputs.items()}
    slots = [0, 2, 1, 3]

    def cols(v):
        return v.reshape(-1, P).T

    def pack(w):
        return w.reshape(w.shape[0] // P, P, w.shape[1]).transpose(1, 0, 2).reshape(P, -1)

    def halved(w):
        return np.stack([np.concatenate([pack(w[:, c:c + CH // 2]), pack(w[:, c + CH // 2:c + CH])], axis=1)
                         for c in range(0, w.shape[1], CH)])

    def chunks(w, width):
        return np.stack([pack(w[:, c:c + width]) for c in range(0, w.shape[1], width)])

    def pairs(w):
        lo, hi = w[:, :DFF].reshape(-1, FT, P), w[:, DFF:].reshape(-1, FT, P)
        return np.stack([lo, hi], axis=2).reshape(w.shape[0], 2 * DFF)

    def wide(v):
        return np.broadcast_to(v[None, :], (P, v.size))

    w_mix, w_tok, vec1 = [], [], []
    for l in range(L1):
        w = a["w_in"][l]
        aq, bq = w[:, 0:256].reshape(D, 4, HD), w[:, 512:768]
        first = np.concatenate([aq[:, 0], aq[:, 2], aq[:, 1], aq[:, 3], w[:, 256:384], bq, w[:, 896:960], w[:, 1024:1088],
                                w[:, 768:832], w[:, 768:832], w[:, 832:896], w[:, 832:896], w[:, 1164:3212]], axis=1)
        w_mix.append(halved(first))
        gates = w[:, 1152:1164].reshape(D, 3, 4)[:, :, slots].reshape(D, 12)
        w_tok.append(pack(np.concatenate([w[:, 384:512], w[:, 960:1024], w[:, 1088:1152], gates, w[:, 3212:3220]], axis=1)))
        w2k = a["cmp_k_w2"][l]
        vec1.append(np.concatenate([
            cols(a["norm_mix"][l]), cols(a["norm_ffn"][l]), cols(a["ada_b"][l]),
            a["gdn_conv_w"][l].reshape(4, 12, P).transpose(2, 0, 1).reshape(P, 48), wide(a["gdn_norm"][l]),
            wide(a["attn_sinks"][l]), wide(a["gdn_A_log"][l]), wide(a["gdn_dt_bias"][l]),
            a["cmp_pe_k"][l].reshape(CMP_PAIRS, P).T, a["cmp_pe_v"][l].reshape(CMP_PAIRS, P).T,
            pack(np.concatenate([w2k, w2k], axis=1)), pack(a["cmp_v_w2"][l])], axis=1))
    vec2 = []
    for l in range(2):
        cw, cb = pairs(a["conv_w_2"][l]), pairs(a["conv_b_2"][l][None])
        vec2.append(np.concatenate([
            cols(a["attn_norm_2"][l]), cols(a["ffn_norm_2"][l]),
            cw.reshape(3, 2 * FT, P).transpose(2, 0, 1).reshape(P, -1), cols(cb)], axis=1))
    parts, dist = shape_constants()
    knorm = a["idx_k_norm_2"][0]
    parts.update(final1=cols(a["final_norm"]), final2=cols(a["final_norm_2"]),
                 knorm=np.concatenate([knorm, knorm])[:, None])
    consts = np.concatenate([np.asarray(parts[n], np.float32) for n in CN], axis=1)
    table = np.concatenate([a["rel_bias_2"].reshape(32, 4, 4)[:, :, slots].reshape(32, 16), np.ones((1, 16), np.float32)])
    even = a["w_in_even_2"][0]
    wi = even[:, 4160:4176].reshape(D, 4, 4)[:, :, slots].reshape(D, 16)
    ki = even[:, 4096:4160]
    arrays = dict(
        xT=a["x"][0].T.reshape(KT, P, S).transpose(1, 0, 2), c=cols(a["c"][0]),
        vec1=np.stack(vec1, axis=1), vec2=np.stack(vec2, axis=1), consts=consts, dist=dist, table=table,
        ada=np.concatenate([chunks(a["ada_w"][l], CH) for l in range(L1)]), w_mix=np.stack(w_mix), w_tok=np.stack(w_tok),
        w_cmp=np.stack([np.stack([pack(a[n][l]) for n in ("cmp_k_w1", "cmp_v_w1")]) for l in range(L1)]),
        w_out=np.stack([halved(a["w_out"][l]) for l in range(L1)]),
        w_gu=np.stack([halved(pairs(a["w_gate_up"][l])) for l in range(L1)]),
        w_dn=np.stack([chunks(a["w_down"][l], P) for l in range(L1)]),
        even_in=halved(even[:, 0:4096]), even_tail=pack(np.concatenate([ki, ki, wi], axis=1)),
        odd_in=halved(a["w_in_odd_2"][0]), w_o2=np.stack([halved(a["w_o_2"][l]) for l in range(2)]),
        w_up2=np.stack([halved(pairs(a["w_up_2"][l])) for l in range(2)]),
        w_dn2=np.stack([chunks(a["w_down_2"][l], P) for l in range(2)]))
    arrays = {n: np.ascontiguousarray(v, dtype=np.float32) for n, v in arrays.items()}
    nc = bacc.Bacc("TRN2", target_bir_lowering=False, num_devices=1)
    args = [nc.dram_tensor(n, v.shape, F32, kind="ExternalInput").ap() for n, v in arrays.items()]
    y = nc.dram_tensor("y", (P, KT, S), F32, kind="ExternalOutput").ap()
    bias_dram = nc.dram_tensor("bias_dram", (2, 16, BIAS_W), F32, kind="Internal").ap()
    bias_wide = nc.dram_tensor("bias_wide", (32, P, BIAS_W), F32, kind="Internal").ap()
    hybrid_then_mixture(nc, *args, y, bias_dram, bias_wide)
    r = run(nc, [arrays], core_ids=[0])
    out = r.results[0]["y"]
    return np.ascontiguousarray(out.transpose(2, 1, 0).reshape(1, S, D))
```
